# Optimizing a Trainium2 kernel written in Bass

```python
import jax, jax.numpy as jnp
from jax import lax
import numpy as np

D_MODEL = 2048
BATCH = 1
SEQ = 256
DEPTH = 1

MIX_WIDTH = D_MODEL
LRU_WIDTH = MIX_WIDTH // 2
GMLP_WIDTH = MIX_WIDTH - LRU_WIDTH
IN_WIDTH = 2 * LRU_WIDTH + 2 * GMLP_WIDTH
LRU_HEADS = 8
LRU_HEAD_DIM = LRU_WIDTH // LRU_HEADS
CONV_WIDTH = 4
CONV_LEFT = 2
LRU_C = 8.0
GMLP_HEADS = 8
GMLP_HEAD_DIM = GMLP_WIDTH // GMLP_HEADS
CHUNK = 128
PEER_HEADS = 8
PEER_KEYS = 128
PEER_EXPERTS = PEER_KEYS * PEER_KEYS
PEER_TOPK = 16
PEER_QDIM = 256
PEER_HALF = PEER_QDIM // 2
PEER_BLOCK = 128
EPS = 1e-6


def rms_norm(x, g):
    xf = x.astype(jnp.float32)
    y = xf * lax.rsqrt(jnp.mean(xf * xf, axis=-1, keepdims=True) + EPS)
    return (y * g.astype(jnp.float32)).astype(x.dtype)

def layer_norm(x, g, b):
    xf = x.astype(jnp.float32)
    mu = jnp.mean(xf, axis=-1, keepdims=True)
    xc = xf - mu
    y = xc * lax.rsqrt(jnp.mean(xc * xc, axis=-1, keepdims=True) + EPS)
    return (y * g.astype(jnp.float32) + b.astype(jnp.float32)).astype(x.dtype)

def centred_depthwise_conv(x, w, b):
    S = x.shape[1]
    xp = jnp.pad(x, ((0, 0), (CONV_LEFT, CONV_WIDTH - 1 - CONV_LEFT), (0, 0)))
    y = b + xp[:, 0:S] * w[0]
    for k in range(1, CONV_WIDTH):
        y = y + xp[:, k:k + S] * w[k]
    return y

def _recurrence_combine(left, right):
    a_l, b_l = left
    a_r, b_r = right
    return a_l * a_r, a_r * b_l + b_r

def rglru(x, w_a, b_a, w_x, b_x, lam, reverse):
    B, S, _ = x.shape
    xh = x.reshape(B, S, LRU_HEADS, LRU_HEAD_DIM)
    r = jax.nn.sigmoid(jnp.einsum('bshc,hce->bshe', xh, w_a.astype(jnp.float32)).reshape(B, S, LRU_WIDTH) + b_a.astype(jnp.float32))
    i = jax.nn.sigmoid(jnp.einsum('bshc,hce->bshe', xh, w_x.astype(jnp.float32)).reshape(B, S, LRU_WIDTH) + b_x.astype(jnp.float32))
    log_a = -LRU_C * jax.nn.softplus(-lam.astype(jnp.float32)) * r
    a = jnp.exp(log_a)
    u = jnp.sqrt(-jnp.expm1(2.0 * log_a)) * (i * x)
    _, h = lax.associative_scan(_recurrence_combine, (a, u), reverse=reverse, axis=1)
    return h

def recurrent_group(xr, gr, conv_w, conv_b, w_a, b_a, w_x, b_x, lam):
    xc = centred_depthwise_conv(xr, conv_w, conv_b).astype(jnp.float32)
    h = (rglru(xc, w_a[0], b_a[0], w_x[0], b_x[0], lam[0], reverse=False)
         + rglru(xc, w_a[1], b_a[1], w_x[1], b_x[1], lam[1], reverse=True))
    return (jax.nn.gelu(gr.astype(jnp.float32)) * h).astype(xr.dtype)

def spatial_gating_group(gu, gv, ln_g, ln_b, w_s, b_s):
    B, S, _ = gv.shape
    u = jax.nn.gelu(gu)
    v = layer_norm(jax.nn.gelu(gv), ln_g, ln_b)
    vc = v.reshape(B, S // CHUNK, CHUNK, GMLP_HEADS, GMLP_HEAD_DIM)
    mixed = jnp.einsum('hpq,bnqhc->bnphc', w_s, vc) + b_s.T[None, None, :, :, None]
    return u * mixed.reshape(B, S, GMLP_WIDTH)

def peer(x, w_q, sub_keys, expert_u, expert_v):
    B, S, D = x.shape
    q = (x @ w_q).reshape(B, S, PEER_HEADS, 2, PEER_HALF)
    s = jnp.einsum('bshpk,hpnk->bshpn', q, sub_keys).astype(jnp.float32)
    top_s, top_i = lax.top_k(s, PEER_TOPK)
    cand_s = (top_s[..., 0, :, None] + top_s[..., 1, None, :]).reshape(B, S, PEER_HEADS, PEER_TOPK * PEER_TOPK)
    cand_i = (top_i[..., 0, :, None] * PEER_KEYS + top_i[..., 1, None, :]).reshape(B, S, PEER_HEADS, PEER_TOPK * PEER_TOPK)
    best_s, pos = lax.top_k(cand_s, PEER_TOPK)
    ids = jnp.take_along_axis(cand_i, pos, axis=-1)
    g = jax.nn.softmax(best_s, axis=-1).astype(x.dtype)
    n_blk = (B * S) // PEER_BLOCK
    xb = x.reshape(n_blk, PEER_BLOCK, D)
    ib = ids.reshape(n_blk, PEER_BLOCK, PEER_HEADS * PEER_TOPK)
    gb = g.reshape(n_blk, PEER_BLOCK, PEER_HEADS * PEER_TOPK)

    def block(args):
        xt, it, gt = args
        u = jnp.take(expert_u, it, axis=0)
        act = jax.nn.gelu(jnp.einsum('td,tkd->tk', xt, u)) * gt
        v = jnp.take(expert_v, it, axis=0)
        return jnp.einsum('tk,tkd->td', act, v)

    out = lax.map(block, (xb, ib, gb))
    return out.reshape(B, S, D)

def first_inputs(seed: int = 0) -> dict:
    key = jax.random.key(seed)
    ks = jax.random.split(key, 24)
    f32 = jnp.float32
    nrm = lambda k, shape, scale: jax.random.normal(k, shape, f32) * scale
    lam_u = jax.random.uniform(ks[10], (DEPTH, 2, LRU_WIDTH), f32, minval=0.9, maxval=0.999)
    lam_base = lam_u ** (1.0 / LRU_C)
    return {
        "x": nrm(ks[0], (BATCH, SEQ, D_MODEL), 1.0),
        "mix_norm_g": 1.0 + nrm(ks[1], (DEPTH, D_MODEL), 0.02),
        "w_in": nrm(ks[2], (DEPTH, D_MODEL, IN_WIDTH), D_MODEL ** -0.5),
        "conv_w": nrm(ks[3], (DEPTH, CONV_WIDTH, LRU_WIDTH), CONV_WIDTH ** -0.5),
        "conv_b": nrm(ks[4], (DEPTH, LRU_WIDTH), 0.02),
        "lru_w_a": nrm(ks[5], (DEPTH, 2, LRU_HEADS, LRU_HEAD_DIM, LRU_HEAD_DIM), LRU_HEAD_DIM ** -0.5),
        "lru_b_a": nrm(ks[6], (DEPTH, 2, LRU_WIDTH), 0.02),
        "lru_w_x": nrm(ks[7], (DEPTH, 2, LRU_HEADS, LRU_HEAD_DIM, LRU_HEAD_DIM), LRU_HEAD_DIM ** -0.5),
        "lru_b_x": nrm(ks[8], (DEPTH, 2, LRU_WIDTH), 0.02),
        "lru_lambda": jnp.log(lam_base) - jnp.log1p(-lam_base),
        "gmlp_ln_g": 1.0 + nrm(ks[11], (DEPTH, GMLP_WIDTH), 0.02),
        "gmlp_ln_b": nrm(ks[12], (DEPTH, GMLP_WIDTH), 0.02),
        "gmlp_w_s": nrm(ks[13], (DEPTH, GMLP_HEADS, CHUNK, CHUNK), 0.5 * CHUNK ** -0.5),
        "gmlp_b_s": 1.0 + nrm(ks[14], (DEPTH, GMLP_HEADS, CHUNK), 0.1),
        "w_out": nrm(ks[15], (DEPTH, MIX_WIDTH, D_MODEL), MIX_WIDTH ** -0.5),
        "ffn_norm_g": 1.0 + nrm(ks[16], (DEPTH, D_MODEL), 0.02),
        "peer_w_q": nrm(ks[17], (DEPTH, D_MODEL, PEER_HEADS * PEER_QDIM), D_MODEL ** -0.5),
        "peer_sub_keys": nrm(ks[18], (DEPTH, PEER_HEADS, 2, PEER_KEYS, PEER_HALF), PEER_HALF ** -0.5),
        "peer_u": nrm(ks[19], (DEPTH, PEER_EXPERTS, D_MODEL), D_MODEL ** -0.5),
        "peer_v": nrm(ks[20], (DEPTH, PEER_EXPERTS, D_MODEL), PEER_HEADS ** -0.5),
        "final_norm_g": 1.0 + nrm(ks[21], (D_MODEL,), 0.02),
    }

def first_block(x, mix_norm_g, w_in, conv_w, conv_b, lru_w_a, lru_b_a, lru_w_x, lru_b_x, lru_lambda,
              gmlp_ln_g, gmlp_ln_b, gmlp_w_s, gmlp_b_s, w_out, ffn_norm_g, peer_w_q, peer_sub_keys,
              peer_u, peer_v, final_norm_g):
    h = x
    for l in range(DEPTH):
        n = rms_norm(h, mix_norm_g[l])
        z = n @ w_in[l]
        xr = z[..., :LRU_WIDTH]
        gr = z[..., LRU_WIDTH:2 * LRU_WIDTH]
        gu = z[..., 2 * LRU_WIDTH:2 * LRU_WIDTH + GMLP_WIDTH]
        gv = z[..., 2 * LRU_WIDTH + GMLP_WIDTH:]
        a_out = recurrent_group(xr, gr, conv_w[l], conv_b[l], lru_w_a[l], lru_b_a[l],
                                lru_w_x[l], lru_b_x[l], lru_lambda[l])
        b_out = spatial_gating_group(gu, gv, gmlp_ln_g[l], gmlp_ln_b[l], gmlp_w_s[l], gmlp_b_s[l])
        h = h + jnp.concatenate([a_out, b_out], axis=-1) @ w_out[l]
        h = h + peer(rms_norm(h, ffn_norm_g[l]), peer_w_q[l], peer_sub_keys[l], peer_u[l], peer_v[l])
    return rms_norm(h, final_norm_g)


PLE_DIM = 256
ATT_HEADS = 16
ATT_HD = 64
ATT_W = ATT_HEADS * ATT_HD
ROT_DIM = ATT_HD // 4
ROPE_THETA = 500000.0
DILATION_CFG = ((128, 1), (512, 4), (2048, 16))
HG_HEADS = 8
HG_DK = 128
HG_DV = 128
HG_W = HG_HEADS * HG_DV
HG_F = HG_HEADS * HG_DK
HG_CHUNK = 64
MIX_W = ATT_W + HG_W
SPLITS = (ATT_W, ATT_W, ATT_W, ATT_W,
          HG_F, HG_F, HG_F, HG_W, HG_W)
IN_W = sum(SPLITS)
SPLIT_IDX = [int(i) for i in np.cumsum(SPLITS)[:-1]]
NEG = -1e30


def rmsnorm(x, g):
    xf = x.astype(jnp.float32)
    y = xf * lax.rsqrt(jnp.mean(xf * xf, axis=-1, keepdims=True) + EPS)
    return (y * g.astype(jnp.float32)).astype(x.dtype)

def rope_partial(x, pos):
    inv = jnp.power(ROPE_THETA, -jnp.arange(0, ROT_DIM, 2, dtype=jnp.float32) / ROT_DIM)
    ang = pos.astype(jnp.float32)[..., None] * inv
    c = jnp.cos(ang)[:, :, None, :]
    s = jnp.sin(ang)[:, :, None, :]
    x1 = x[..., :ROT_DIM // 2]
    x2 = x[..., ROT_DIM // 2:ROT_DIM]
    return jnp.concatenate([x1 * c - x2 * s, x2 * c + x1 * s, x[..., ROT_DIM:]], axis=-1)

def dilated_band_attention(q, k, v, window, dilation):
    B, S, H, E = q.shape
    half = (window // 2) // dilation
    blk = half
    L = S // dilation
    nb = -(-L // blk)
    Lp = nb * blk

    def strided(t):
        t = t.reshape(B, L, dilation, H, E).transpose(0, 2, 3, 1, 4)
        return jnp.pad(t, ((0, 0), (0, 0), (0, 0), (0, Lp - L), (0, 0)))

    def neighbours(t):
        tp = jnp.pad(t, ((0, 0), (0, 0), (0, 0), (blk, blk), (0, 0)))
        parts = [tp[:, :, :, j * blk:j * blk + Lp].reshape(B, dilation, H, nb, blk, E) for j in range(3)]
        return jnp.concatenate(parts, axis=4)

    qb = strided(q).reshape(B, dilation, H, nb, blk, E)
    kb = neighbours(strided(k))
    vb = neighbours(strided(v))
    qa = jnp.arange(nb)[:, None] * blk + jnp.arange(blk)[None, :]
    ka = jnp.arange(nb)[:, None] * blk - blk + jnp.arange(3 * blk)[None, :]
    rel = ka[:, None, :] - qa[:, :, None]
    valid = (jnp.abs(rel) <= half) & (ka[:, None, :] >= 0) & (ka[:, None, :] < L)
    s = jnp.einsum('bdhnqe,bdhnke->bdhnqk', qb, kb)
    s = jnp.where(valid, s, NEG)
    m = jnp.max(s, axis=-1, keepdims=True)
    pe = jnp.exp(s - m)
    den = jnp.sum(pe, axis=-1)
    o = jnp.einsum('bdhnqk,bdhnke->bdhnqe', pe, vb) / den[..., None]
    lse = m[..., 0] + jnp.log(den)
    o = o.reshape(B, dilation, H, Lp, E)[:, :, :, :L].transpose(0, 3, 1, 2, 4).reshape(B, S, H, E)
    lse = lse.reshape(B, dilation, H, Lp)[:, :, :, :L].transpose(0, 3, 1, 2).reshape(B, S, H)
    return o, lse

def hgrn2_chunk_scan(q, k, v, g):
    B, S, H, K = q.shape
    V = v.shape[-1]
    C = HG_CHUNK
    N = S // C

    def chunks(t):
        return t.reshape(B, N, C, H, t.shape[-1]).transpose(1, 0, 3, 2, 4)

    tri = jnp.tril(jnp.ones((C, C), dtype=bool))

    def step(state, inp):
        qc, kc, vc, gc = inp
        b = jnp.cumsum(gc, axis=2)
        diff = b[:, :, :, None, :] - b[:, :, None, :, :]
        decay = jnp.exp(jnp.where(tri[:, :, None], diff, -jnp.inf))
        att = jnp.einsum('bhtk,bhsk,bhtsk->bhts', qc, kc, decay)
        o = (jnp.einsum('bhts,bhsv->bhtv', att, vc)
             + jnp.einsum('bhtk,bhkv->bhtv', qc * jnp.exp(b), state))
        b_last = b[:, :, -1:, :]
        state = (jnp.exp(b_last[:, :, 0, :])[..., None] * state
                 + jnp.einsum('bhsk,bhsv->bhkv', kc * jnp.exp(b_last - b), vc))
        return state, o

    s0 = jnp.zeros((B, H, K, V), dtype=q.dtype)
    _, o = lax.scan(step, s0, (chunks(q), chunks(k), chunks(v), chunks(g)))
    return o.transpose(1, 0, 3, 2, 4).reshape(B, S, H, V)

def hgrn2_direction(qh, vh, f_logit, lb):
    f = lb + (1.0 - lb) * jax.nn.sigmoid(f_logit)
    return hgrn2_chunk_scan(qh, 1.0 - f, vh, jnp.log(f))

def hybrid_layer(h, p_l, pos, w_in, w_out, g_pre, g_post, g_hg, lb_f, lb_b, w_pg, w_pp, g_ple):
    B, S, _ = h.shape
    f32 = jnp.float32
    u = rmsnorm(h, g_pre)
    z = u @ w_in
    aq, ak, av, ag, hq, hf_f, hf_b, hv, hg = jnp.split(z, SPLIT_IDX, axis=-1)

    def heads(t, n):
        return t.reshape(B, S, n, -1).astype(f32)

    q = rope_partial(heads(aq, ATT_HEADS), pos) * (ATT_HD ** -0.5)
    k = rope_partial(heads(ak, ATT_HEADS), pos)
    v = heads(av, ATT_HEADS)
    res = [dilated_band_attention(q, k, v, w, d) for (w, d) in DILATION_CFG]
    outs = jnp.stack([r[0] for r in res])
    lses = jnp.stack([r[1] for r in res])
    alpha = jax.nn.softmax(lses, axis=0)
    o_att = jnp.einsum('gbsh,gbshe->bshe', alpha, outs).reshape(B, S, ATT_W)
    y_att = o_att * jax.nn.silu(ag.astype(f32))

    qh = jax.nn.silu(heads(hq, HG_HEADS))
    vh = heads(hv, HG_HEADS)
    o_fw = hgrn2_direction(qh, vh, heads(hf_f, HG_HEADS), lb_f)
    o_bw = jnp.flip(hgrn2_direction(jnp.flip(qh, 1), jnp.flip(vh, 1),
                                    jnp.flip(heads(hf_b, HG_HEADS), 1), lb_b), 1)
    o_hg = rmsnorm(o_fw + o_bw, g_hg).reshape(B, S, HG_W)
    y_hg = o_hg * jax.nn.silu(hg.astype(f32))

    y = jnp.concatenate([y_att, y_hg], axis=-1).astype(h.dtype) @ w_out
    h = h + rmsnorm(y, g_post)

    gate = jax.nn.sigmoid((h @ w_pg).astype(f32))
    e = (p_l @ w_pp).astype(f32)
    h = h + rmsnorm((gate * e).astype(h.dtype), g_ple)
    return h

def second_inputs(seed: int = 0) -> dict:
    key = jax.random.key(seed)
    ks = jax.random.split(key, 16)
    nrm = jax.random.normal
    x = nrm(ks[0], (BATCH, SEQ, D_MODEL), jnp.float32)
    p = nrm(ks[1], (DEPTH, BATCH, SEQ, PLE_DIM), jnp.float32)
    positions = (jnp.arange(SEQ, dtype=jnp.int32)[None, :]
                 + jax.random.randint(ks[2], (BATCH, 1), 0, 1024, dtype=jnp.int32))
    w_in = nrm(ks[3], (DEPTH, D_MODEL, IN_W), jnp.float32) * D_MODEL ** -0.5
    w_out = nrm(ks[4], (DEPTH, MIX_W, D_MODEL), jnp.float32) * MIX_W ** -0.5
    g_pre = 1.0 + 0.05 * nrm(ks[5], (DEPTH, D_MODEL), jnp.float32)
    g_post = 1.0 + 0.05 * nrm(ks[6], (DEPTH, D_MODEL), jnp.float32)
    g_hg = 1.0 + 0.05 * nrm(ks[7], (DEPTH, HG_DV), jnp.float32)
    lb_fwd = 0.1 * nrm(ks[8], (DEPTH + 1, HG_F), jnp.float32)
    lb_bwd = 0.1 * nrm(ks[9], (DEPTH + 1, HG_F), jnp.float32)
    w_pg = nrm(ks[10], (DEPTH, D_MODEL, D_MODEL), jnp.float32) * D_MODEL ** -0.5
    w_pp = nrm(ks[11], (DEPTH, PLE_DIM, D_MODEL), jnp.float32) * PLE_DIM ** -0.5
    g_ple = 1.0 + 0.05 * nrm(ks[12], (DEPTH, D_MODEL), jnp.float32)
    return {'x': x, 'p': p, 'positions': positions, 'w_in': w_in, 'w_out': w_out,
            'g_pre': g_pre, 'g_post': g_post, 'g_hg': g_hg, 'lb_fwd': lb_fwd, 'lb_bwd': lb_bwd,
            'w_pg': w_pg, 'w_pp': w_pp, 'g_ple': g_ple}

def second_block(x, p, positions, w_in, w_out, g_pre, g_post, g_hg, lb_fwd, lb_bwd, w_pg, w_pp, g_ple):
    lb_f_all = jnp.cumsum(jax.nn.softmax(lb_fwd.astype(jnp.float32), axis=0), axis=0)
    lb_b_all = jnp.cumsum(jax.nn.softmax(lb_bwd.astype(jnp.float32), axis=0), axis=0)
    h = x
    for i in range(DEPTH):
        h = hybrid_layer(h, p[i], positions, w_in[i], w_out[i], g_pre[i], g_post[i], g_hg[i],
                         lb_f_all[i].reshape(HG_HEADS, HG_DK), lb_b_all[i].reshape(HG_HEADS, HG_DK),
                         w_pg[i], w_pp[i], g_ple[i])
    return h


def setup_inputs(seed=0):
    out = dict(first_inputs(seed))
    for name, value in second_inputs(seed + 1).items():
        if name != "x":
            out[name + "_2"] = value
    return out


def reference(
    x, mix_norm_g, w_in, conv_w, conv_b, lru_w_a, lru_b_a, lru_w_x, lru_b_x, lru_lambda,
    gmlp_ln_g, gmlp_ln_b, gmlp_w_s, gmlp_b_s, w_out, ffn_norm_g, peer_w_q, peer_sub_keys,
    peer_u, peer_v, final_norm_g, p_2, positions_2, w_in_2, w_out_2, g_pre_2, g_post_2, g_hg_2,
    lb_fwd_2, lb_bwd_2, w_pg_2, w_pp_2, g_ple_2,
):
    x = first_block(
        x, mix_norm_g, w_in, conv_w, conv_b, lru_w_a, lru_b_a, lru_w_x, lru_b_x, lru_lambda,
        gmlp_ln_g, gmlp_ln_b, gmlp_w_s, gmlp_b_s, w_out, ffn_norm_g, peer_w_q, peer_sub_keys,
        peer_u, peer_v, final_norm_g,
    )
    return second_block(
        x, p_2, positions_2, w_in_2, w_out_2, g_pre_2, g_post_2, g_hg_2, lb_fwd_2, lb_bwd_2,
        w_pg_2, w_pp_2, g_ple_2,
    )


_drawn_inputs = setup_inputs


def setup_inputs(seed=0):
    import zlib

    import numpy as np

    out = dict(_drawn_inputs(seed))
    spreads = {}
    factors = {'lru_b_a': 31.37,
     'lru_b_x': 19.708,
     'gmlp_ln_g': 13.705,
     'gmlp_ln_b': 13.761,
     'lb_fwd_2': 8.0,
     'lb_bwd_2': 8.0,
     'ffn_norm_g': 8.926,
     'gmlp_b_s': 2.744}
    for name, (base, spread) in spreads.items():
        noise = np.random.default_rng([zlib.crc32(name.encode()), seed]).standard_normal(out[name].shape)
        drawn = base * np.exp(spread * noise) if base else spread * noise
        out[name] = __import__('jax').numpy.asarray(drawn.astype(out[name].dtype))
    for name, factor in factors.items():
        out[name] = (out[name] * factor).astype(out[name].dtype)
    return out
```

```python
from contextlib import ExitStack

import numpy as np

import concourse.bass as bass
from concourse import mybir

F32 = mybir.dt.float32
I32 = mybir.dt.int32
U32 = mybir.dt.uint32
ALU = mybir.AluOpType
ACT = mybir.ActivationFunctionType
AX_X = mybir.AxisListType.X

P = 128
D = 2048
T = 256
TT = T // P
KC = D // P
NB = 256
EPS = 1e-6
LRU = 1024
HEADS = 8
KEYS = 128
TOPK = 16
SLOTS = HEADS * TOPK
CHUNK = 32
NCH = T // CHUNK
LRU_C = 8.0
LOWEST = -3.0e38
ROT = 8
TWO_PI = 2 * np.pi
TURN_PARTS = (6.28125, 0.001934051513671875, TWO_PI - 6.28125 - 0.001934051513671875)
ROUNDER = 1.5 * 2.0 ** 23

C_IDENT = 0
C_BIAS = C_IDENT + P
C_IOTA = C_BIAS + TT * T
C_FWD = C_IOTA + TOPK
C_BWD = C_FWD + P
C_INV = C_BWD + P
C_ONES = C_INV + ROT
C_END = C_ONES + P


def shape_constants():
    c = np.zeros((P, C_END), np.float32)
    c[:, C_IDENT:C_IDENT + P] = np.eye(P)
    i, j = np.arange(T)[:, None], np.arange(T)[None, :]
    times = np.zeros((T, T))
    for window, dilation in ((128, 1), (512, 4), (2048, 16)):
        times += (np.abs(i - j) <= window // 2) & ((i - j) % dilation == 0)
    bias = np.where(times > 0, np.log(np.maximum(times, 1)), -1e30)
    c[:, C_BIAS:C_BIAS + TT * T] = bias.reshape(TT, P, T).transpose(1, 0, 2).reshape(P, -1)
    c[:, C_IOTA:C_IOTA + TOPK] = np.arange(TOPK)
    s, t = np.arange(P)[:, None], np.arange(P)[None, :]
    same = s // CHUNK == t // CHUNK
    c[:, C_FWD:C_FWD + P] = same & (s <= t)
    c[:, C_BWD:C_BWD + P] = same & (s >= t)
    exponent = -np.arange(0, 2 * ROT, 2, dtype=np.float32) / np.float32(2 * ROT)
    c[:, C_INV:C_INV + ROT] = np.power(np.float32(500000.0), exponent)
    c[:, C_ONES:C_ONES + P] = 1.0
    return c


A_MIX, A_CONVW, A_CONVB, A_BA, A_BX, A_LAM, A_FFN = 0, 16, 48, 56, 72, 88, 104
A_ROWS = 120
B_LBF, B_LBB, B_PRE, B_HG = 0, 16, 32, 48
B_ROWS = 49


def build(nc, x, mix_norm_g, w_in, conv_w, conv_b, lru_w_a, lru_b_a, lru_w_x, lru_b_x, lru_lambda,
          gmlp_ln_g, gmlp_ln_b, gmlp_w_s, gmlp_b_s, w_out, ffn_norm_g, peer_w_q, peer_sub_keys,
          peer_u, peer_v, final_norm_g, p_2, positions_2, w_in_2, w_out_2, g_pre_2, g_post_2,
          g_hg_2, lb_fwd_2, lb_bwd_2, w_pg_2, w_pp_2, g_ple_2, constants, out):
    ctx = ExitStack()
    with ctx:
        def sbuf(name, words, dtype=F32):
            return ctx.enter_context(nc.sbuf_tensor(name, [P, words], dtype))

        sems = {}

        def sem(name):
            if name not in sems:
                sems[name] = ctx.enter_context(nc.semaphore(name))
            return sems[name]

        h_t = sbuf("residual", TT * D)
        h = h_t[:, :].rearrange("p (a d) -> p a d", a=TT)
        actT_t = sbuf("actT", KC * T)
        actT = actT_t[:, :].rearrange("p (k t) -> p k t", k=KC)
        wblk = [ctx.enter_context(nc.sbuf_tensor(f"weights{s}", [P, KC, NB], F32)) for s in range(4)]
        cst = sbuf("constants_sb", C_END)
        colsA = sbuf("colsA", A_ROWS)
        colsB = sbuf("colsB", B_ROWS)
        stat = sbuf("stat", 64)
        area_t = sbuf("area", 26700)
        vec_t = sbuf("vectors", 2 * P + 128)

        def area(at, *dims, dtype=F32):
            n = int(np.prod(dims))
            v = area_t[:, at:at + n]
            if dtype != F32:
                v = v.bitcast(dtype)
            if len(dims) == 2:
                v = v.rearrange("p (a b) -> p a b", a=dims[0])
            if len(dims) == 3:
                v = v.rearrange("p (a b c) -> p a b c", a=dims[0], b=dims[1])
            if len(dims) == 4:
                v = v.rearrange("p (a b c d) -> p a b c d", a=dims[0], b=dims[1], c=dims[2])
            return v

        bank = [ctx.enter_context(nc.psum_tensor(f"bank{s}", [P, 512], F32)) for s in range(4)]
        aux_t = ctx.enter_context(nc.psum_tensor("aux", [P, 4, 512], F32))
        aux = [aux_t[:, s, :] for s in range(4)]
        ident = cst[:, C_IDENT:C_IDENT + P]

        chained = {}

        def link(engine, instruction):
            name = f"{engine.engine.name}_own"
            chained[name] = chained.get(name, 0) + 1
            instruction.then_inc(sem(name), 1)
            engine.wait_ge(sem(name), chained[name])

        tile_done = [sem(f"tile_done{s}") for s in range(4)]
        w_loaded = [sem(f"w_loaded{s}") for s in range(4)]
        bank_free = [sem(f"bank_free{s}") for s in range(4)]

        turns = {}
        for name, blocks in (("in", 16), ("out", 8), ("q", 8), ("in2", 36), ("out2", 8), ("pg", 8)):
            turns[name] = (sum(n for _, n in turns.values()), blocks // 4)

        def starts(use):
            return isinstance(use, int) and use == 0

        def load_turn(sp, w, use, col):
            wv = w[0].rearrange("(k p) n -> p k n", p=P)
            for s in range(4):
                if not starts(use):
                    sp.wait_ge(tile_done[s], use)
                sp.dma_start(wblk[s][:, :, :], wv[:, :, bass.ds(col + s * NB, NB)]).then_inc(w_loaded[s], 16)

        def load_first(sp, w, name):
            load_turn(sp, w, turns[name][0], 0)

        def load_rest(sp, w, name):
            first, n = turns[name]
            with sp.Fori(1, n) as i:
                load_turn(sp, w, i + first, i * (4 * NB))

        def multiply_turn(pe, use, token, src):
            for s in range(4):
                pe.wait_ge(w_loaded[s], use * 16 + 16)
                if not starts(use):
                    pe.wait_ge(bank_free[s], use)
                for half in range(2):
                    to = bank[s][:, half * NB:half * NB + NB]
                    for k in range(KC):
                        if token:
                            lhsT, rhs = src[:, k, half * P:half * P + P], wblk[s][:, k, :]
                        else:
                            lhsT, rhs = wblk[s][:, k, half * P:half * P + P], src[:, k, :]
                        last = nc.tensor.matmul(to, lhsT, rhs, start=k == 0, stop=k == KC - 1)
                last.then_inc(tile_done[s], 1)

        def multiply(pe, first, n, token, src):
            if n == 1 or first == 0:
                multiply_turn(pe, first, token, src)
                first, n = first + 1, n - 1
            if n:
                with pe.Fori(0, n) as i:
                    multiply_turn(pe, i + first, token, src)

        def transpose_tokens(pe, src, ready, done, moved, groups=4):
            for a in range(TT):
                pe.wait_ge(sem(ready), a + 1)
                for q in range(groups):
                    j = a * groups + q
                    if j >= 4:
                        pe.wait_ge(sem(moved), j - 3)
                    for c in range(4):
                        last = nc.tensor.transpose(aux[j % 4][:, c * P:c * P + P],
                                                   src[:, a, (4 * q + c) * P:(4 * q + c) * P + P], ident)
                    last.then_inc(sem(done), 1)

        def squares(act, src, n, ready, step=1):
            for a in range(TT):
                if ready:
                    act.wait_ge(sem(ready), step * (a + 1))
                link(act, nc.scalar.activation(aux_t[:, 0:src.shape[2] // 512, :].rearrange("p s n -> p (s n)"),
                                               src[:, a, :], ACT.Square, accum_out=stat[:, n + a:n + a + 1]))
            act.nop().then_inc(sem("squares_done"), 1)

        def roots(act, n):
            act.wait_ge(sem("mean_done"), n // 2 + 1)
            nc.scalar.activation(stat[:, 16 + n:18 + n], stat[:, n:n + 2], ACT.Sqrt).then_inc(sem("root_done"), 1)

        def reciprocal_rms(dve, n, width):
            dve.wait_ge(sem("squares_done"), n // 2 + 1)
            nc.vector.tensor_scalar(stat[:, n:n + 2], stat[:, n:n + 2], 1.0 / width, EPS, ALU.mult, ALU.add).then_inc(sem("mean_done"), 1)
            dve.wait_ge(sem("root_done"), n // 2 + 1)
            link(dve, nc.vector.reciprocal(stat[:, 32 + n:34 + n], stat[:, 16 + n:18 + n]))

        def rms_col(n, a):
            return stat[:, 32 + n + a:33 + n + a]

        mixT = area(0, KC, T)
        xn = area(0, TT, D)
        decay = area(0, 2, 8, T)
        grT = area(4096, 8, T)
        guT = area(6144, 8, T)
        gv = area(8192, TT, LRU)
        xrp = area(10240, 8, T + 3)
        ws_raw = area(10240, 8, P)
        xcT = area(12320, 8, T)
        gates = area(14368, 2, 2, 8, P)
        ln_g = area(14368, LRU)
        ln_b = area(15392, LRU)
        bs_bc = area(16416, 8, P)
        wsT = area(17440, 8, P)
        rT = area(18464, 2, 8, T)
        iT = area(22560, 2, 8, T)
        vecs = vec_t[:, 0:2 * P].rearrange("p (a c) -> p a c", a=2)
        lam = vec_t[:, 2 * P:2 * P + 128].rearrange("p (a c) -> p a c", a=8)

        with nc.Block() as block:
            @block.sync
            def _(sp):
                sp.dma_start(h, x[0].rearrange("(a p) d -> p a d", p=P)).then_inc(sem("x_loaded"), 16)
                load_first(sp, w_in, "in")
                load_rest(sp, w_in, "in")
                load_first(sp, w_out, "out")

            @block.gpsimd
            def _(pool):
                nc.gpsimd.memset(xrp[:, :, 0:2], 0.0).then_inc(sem("padded"), 1)
                nc.gpsimd.memset(xrp[:, :, T + 2:T + 3], 0.0).then_inc(sem("padded"), 1)

            @block.scalar
            def _(act):
                def load(dst, src, name):
                    act.dma_start(dst, src).then_inc(sem(name), 16)

                load(cst[:, :], constants, "cst_loaded")
                for which, row, src in (
                    (0, A_MIX, mix_norm_g[0].rearrange("(r c) -> r c", c=P)),
                    (0, A_CONVW, conv_w[0].rearrange("k (r c) -> (k r) c", c=P)),
                    (0, A_CONVB, conv_b[0].rearrange("(r c) -> r c", c=P)),
                    (0, A_BA, lru_b_a[0].rearrange("d (r c) -> (d r) c", c=P)),
                    (0, A_BX, lru_b_x[0].rearrange("d (r c) -> (d r) c", c=P)),
                    (0, A_LAM, lru_lambda[0].rearrange("d (r c) -> (d r) c", c=P)),
                    (0, A_FFN, ffn_norm_g[0].rearrange("(r c) -> r c", c=P)),
                    (1, B_LBF, lb_fwd_2.rearrange("l (r c) -> (l r) c", c=P)),
                    (1, B_LBB, lb_bwd_2.rearrange("l (r c) -> (l r) c", c=P)),
                    (1, B_PRE, g_pre_2[0].rearrange("(r c) -> r c", c=P)),
                    (1, B_HG, g_hg_2),
                ):
                    load(vecs[row:row + src.shape[0], which, :], src, "vecs_loaded")
                for g, w in ((0, lru_w_a), (1, lru_w_x)):
                    for d in range(2):
                        load(gates[:, g, d, :, :], w[0, d].rearrange("h c e -> c h e"), "gates_loaded")

                act.wait_ge(sem("x_loaded"), 16)
                squares(act, h, 0, None)
                roots(act, 0)
                act.wait_ge(sem("lam_abs"), 1)
                nc.scalar.activation(lam[:, 1, :], lam[:, 0, :], ACT.Exp).then_inc(sem("lam_exp"), 1)

                def read_product(use, s, dst, func):
                    act.wait_ge(tile_done[s], use + 1)
                    nc.scalar.activation(dst, bank[s][:, :].rearrange("p (a n) -> p a n", a=2), func).then_inc(bank_free[s], 1)

                act.wait_ge(sem("padded"), 2)
                for s in range(4):
                    read_product(0, s, xrp[:, 2 * s:2 * s + 2, 2:2 + T], ACT.Copy)
                for s in range(4):
                    read_product(1, s, grT[:, 2 * s:2 * s + 2, :], ACT.Gelu_apprx_tanh)
                for j in range(16):
                    d, hd = j // 8, j % 8
                    act.wait_ge(sem("gate_product"), j + 1)
                    nc.scalar.activation(rT[:, d, hd, :], aux[j % 4][:, 0:T], ACT.Sigmoid,
                                         bias=colsA[:, A_BA + j:A_BA + j + 1]).then_inc(sem("r_ready"), 1)
                    nc.scalar.activation(iT[:, d, hd, :], aux[j % 4][:, T:2 * T], ACT.Sigmoid,
                                         bias=colsA[:, A_BX + j:A_BX + j + 1]).then_inc(sem("gate_read"), 1)
                act.wait_ge(sem("lam_done"), 1)
                for j in range(16):
                    act.wait_ge(sem("r_ready"), j + 1)
                    nc.scalar.activation(rT[:, j // 8, j % 8, :], rT[:, j // 8, j % 8, :], ACT.Tanh,
                                         scale=lam[:, 7, j:j + 1]).then_inc(sem("tanh_ready"), 1)
                for d in range(2):
                    act.wait_ge(sem("plus_one"), d + 1)
                    act.wait_ge(sem("tanh_ready"), 16)
                    nc.scalar.activation(rT[:, d], rT[:, d], ACT.Sqrt).then_inc(sem("tanh_root"), 1)
                act.wait_ge(sem("gate_product"), 16)
                load(ln_g, gmlp_ln_g.broadcast_to([P, LRU]), "ln_loaded")
                load(ln_b, gmlp_ln_b.broadcast_to([P, LRU]), "ln_loaded")
                load(bs_bc, gmlp_b_s[0:1].broadcast_to([P, 8, P]), "ln_loaded")
                act.wait_ge(sem("conv_done"), 8)
                load(ws_raw, gmlp_w_s[0].rearrange("h p q -> p h q"), "ws_loaded")
                for s in range(4):
                    read_product(2, s, guT[:, 2 * s:2 * s + 2, :], ACT.Gelu_apprx_tanh)
                for s in range(4):
                    read_product(3, s, gv[:, :, s * NB:s * NB + NB], ACT.Gelu_apprx_tanh)
                for j in range(2):
                    act.wait_ge(sem("ws_transposed"), j + 1)
                    nc.scalar.activation(wsT[:, 4 * j:4 * j + 4, :], aux[j].rearrange("p (c t) -> p c t", c=4), ACT.Copy).then_inc(sem("ws_moved"), 1)
                act.wait_ge(sem("ws_moved"), 2)
                squares(act, gv, 2, "v_centred")
                roots(act, 2)

            @block.vector
            def _(dve):
                def step(instruction):
                    link(dve, instruction)

                dve.wait_ge(sem("vecs_transposed"), 1)
                step(nc.vector.tensor_copy(colsA[:, :], aux[0][:, 0:A_ROWS]))
                step(nc.vector.tensor_copy(colsB[:, :], aux[1][:, 0:B_ROWS]))
                dve.nop().then_inc(sem("cols_ready"), 1)
                lam0 = colsA[:, A_LAM:A_LAM + 16]
                step(nc.vector.tensor_scalar(lam[:, 2, :], lam0, -1.0, None, ALU.mult))
                nc.vector.tensor_tensor(lam[:, 0, :], lam0, lam[:, 2, :], ALU.min).then_inc(sem("lam_abs"), 1)
                reciprocal_rms(dve, 0, D)
                for a in range(TT):
                    nc.vector.tensor_scalar(xn[:, a, :], h[:, a, :], rms_col(0, a), None, ALU.mult).then_inc(sem("n1_ready"), 1)
                for j in range(8):
                    a, q = j // 4, j % 4
                    dve.wait_ge(sem("n1_transposed"), j + 1)
                    nc.vector.tensor_tensor(actT[:, 4 * q:4 * q + 4, a * P:a * P + P], aux[j % 4].rearrange("p (c t) -> p c t", c=4),
                                            colsA[:, A_MIX + 4 * q:A_MIX + 4 * q + 4].unsqueeze(2).broadcast_to([P, 4, P]),
                                            ALU.mult).then_inc(sem("n1_moved"), 1)
                dve.wait_ge(sem("lam_exp"), 1)
                step(nc.vector.tensor_scalar(lam[:, 3, :], lam[:, 1, :], 2.0, None, ALU.add))
                step(nc.vector.reciprocal(lam[:, 3, :], lam[:, 3, :]))
                step(nc.vector.tensor_tensor(lam[:, 3, :], lam[:, 3, :], lam[:, 1, :], ALU.mult))
                step(nc.vector.tensor_tensor(lam[:, 4, :], lam[:, 3, :], lam[:, 3, :], ALU.mult))
                step(nc.vector.memset(lam[:, 5, :], 1.0 / 19))
                for n in range(17, 0, -2):
                    step(nc.vector.tensor_tensor(lam[:, 5, :], lam[:, 5, :], lam[:, 4, :], ALU.mult))
                    step(nc.vector.tensor_scalar(lam[:, 5, :], lam[:, 5, :], 1.0 / n, None, ALU.add))
                step(nc.vector.tensor_tensor(lam[:, 5, :], lam[:, 5, :], lam[:, 3, :], ALU.mult))
                step(nc.vector.tensor_scalar(lam[:, 2, :], lam[:, 2, :], 0.0, None, ALU.max))
                step(nc.vector.scalar_tensor_tensor(lam[:, 6, :], lam[:, 5, :], 2.0, lam[:, 2, :], ALU.mult, ALU.add))
                nc.vector.tensor_scalar(lam[:, 7, :], lam[:, 6, :], LRU_C / 2, None, ALU.mult).then_inc(sem("lam_done"), 1)

                for c in range(8):
                    dve.wait_ge(bank_free[c // 2], 1)
                    step(nc.vector.tensor_scalar(xcT[:, c, :], xrp[:, c, 0:T], colsA[:, A_CONVW + c:A_CONVW + c + 1],
                                                 colsA[:, A_CONVB + c:A_CONVB + c + 1], ALU.mult, ALU.add))
                    for k in (1, 2, 3):
                        tap = nc.vector.scalar_tensor_tensor(xcT[:, c, :], xrp[:, c, k:k + T],
                                                             colsA[:, A_CONVW + 8 * k + c:A_CONVW + 8 * k + c + 1],
                                                             xcT[:, c, :], ALU.mult, ALU.add)
                        if k < 3:
                            step(tap)
                    tap.then_inc(sem("conv_done"), 1)

                for d in range(2):
                    dve.wait_ge(sem("tanh_ready"), 8 * d + 8)
                    nc.vector.tensor_scalar(decay[:, d], rT[:, d], 1.0, None, ALU.add).then_inc(sem("plus_one"), 1)
                    dve.wait_ge(sem("plus_one"), d + 1)
                    step(nc.vector.reciprocal(decay[:, d], decay[:, d]))
                for d in range(2):
                    dve.wait_ge(sem("tanh_root"), d + 1)
                    step(nc.vector.scalar_tensor_tensor(rT[:, d], decay[:, d], 2.0, rT[:, d], ALU.mult, ALU.mult))
                    step(nc.vector.tensor_scalar(decay[:, d], decay[:, d], 2.0, -1.0, ALU.mult, ALU.add))
                    dve.wait_ge(sem("gate_read"), 16)
                    step(nc.vector.tensor_tensor(rT[:, d], rT[:, d], iT[:, d], ALU.mult))
                    step(nc.vector.tensor_tensor(rT[:, d], rT[:, d], xcT, ALU.mult))
                    for hd in range(8):
                        way = slice(None, None, -1) if d else slice(None)
                        step(nc.vector.tensor_tensor_scan(iT[:, d, hd, way], decay[:, d, hd, way], rT[:, d, hd, way],
                                                          0.0, ALU.mult, ALU.add))
                step(nc.vector.tensor_tensor(iT[:, 0], iT[:, 0], iT[:, 1], ALU.add))
                dve.wait_ge(bank_free[3], 2)
                step(nc.vector.tensor_tensor(mixT[:, 0:8, :], iT[:, 0], grT, ALU.mult))

                for s in range(4):
                    dve.wait_ge(bank_free[s], 4)
                for a in range(TT):
                    step(nc.vector.tensor_reduce(stat[:, 60 + a:61 + a], gv[:, a, :], AX_X, ALU.add))
                    step(nc.vector.tensor_scalar(stat[:, 62 + a:63 + a], stat[:, 60 + a:61 + a], -1.0 / LRU, None, ALU.mult))
                    nc.vector.tensor_scalar(gv[:, a, :], gv[:, a, :], stat[:, 62 + a:63 + a], None, ALU.add).then_inc(sem("v_centred"), 1)
                reciprocal_rms(dve, 2, LRU)
                dve.wait_ge(sem("ln_loaded"), 48)
                for a in range(TT):
                    step(nc.vector.scalar_tensor_tensor(gv[:, a, :], gv[:, a, :], rms_col(2, a), ln_g, ALU.mult, ALU.mult))
                    nc.vector.tensor_tensor(gv[:, a, :], gv[:, a, :], ln_b, ALU.add).then_inc(sem("v_ready"), 1)
                for j in range(4):
                    dve.wait_ge(sem("mixed"), j + 1)
                    to = mixT[:, 8 + 2 * j:10 + 2 * j, :]
                    step(nc.vector.tensor_tensor(to.rearrange("p h (n t) -> p h n t", n=2),
                                                 aux[j].rearrange("p (h n t) -> p h n t", h=2, n=2),
                                                 bs_bc[:, 2 * j:2 * j + 2, :].unsqueeze(2).broadcast_to([P, 2, 2, P]), ALU.add))
                    step(nc.vector.tensor_tensor(to, to, guT[:, 2 * j:2 * j + 2, :], ALU.mult))

            @block.tensor
            def _(pe):
                pe.wait_ge(sem("cst_loaded"), 16)
                pe.wait_ge(sem("vecs_loaded"), 16 * 11)
                pe.wait_ge(sem("squares_done"), 1)
                nc.tensor.transpose(aux[0][:, 0:A_ROWS], vecs[0:A_ROWS, 0, :], ident[0:A_ROWS, 0:A_ROWS])
                nc.tensor.transpose(aux[1][:, 0:B_ROWS], vecs[0:B_ROWS, 1, :], ident[0:B_ROWS, 0:B_ROWS]).then_inc(sem("vecs_transposed"), 1)
                pe.wait_ge(sem("cols_ready"), 1)
                transpose_tokens(pe, xn, "n1_ready", "n1_transposed", "n1_moved")
                pe.wait_ge(sem("n1_moved"), 8)
                multiply(pe, 0, 2, False, actT)
                pe.wait_ge(sem("gates_loaded"), 64)
                for j in range(16):
                    d, hd = j // 8, j % 8
                    pe.wait_ge(sem("conv_done"), hd + 1 if d == 0 else 8)
                    if j >= 4:
                        pe.wait_ge(sem("gate_read"), j - 3)
                    nc.tensor.matmul(aux[j % 4][:, 0:T], gates[:, 0, d, hd, :], xcT[:, hd, :], start=True, stop=True)
                    nc.tensor.matmul(aux[j % 4][:, T:2 * T], gates[:, 1, d, hd, :], xcT[:, hd, :], start=True, stop=True).then_inc(sem("gate_product"), 1)
                multiply(pe, 2, 1, False, actT)
                multiply(pe, 3, 1, True, actT)
                pe.wait_ge(sem("ws_loaded"), 16)
                pe.wait_ge(sem("gate_read"), 16)
                for hd in range(8):
                    last = nc.tensor.transpose(aux[hd // 4][:, (hd % 4) * P:(hd % 4) * P + P], ws_raw[:, hd, :], ident)
                    if hd % 4 == 3:
                        last.then_inc(sem("ws_transposed"), 1)
                pe.wait_ge(sem("ws_moved"), 2)
                pe.wait_ge(sem("v_ready"), 2)
                for hd in range(8):
                    for n in range(TT):
                        at = (2 * (hd % 2) + n) * P
                        last = nc.tensor.matmul(aux[hd // 2][:, at:at + P], gv[:, n, hd * P:hd * P + P], wsT[:, hd, :],
                                                start=True, stop=True)
                    if hd % 2:
                        last.then_inc(sem("mixed"), 1)

        n2 = area(0, TT, D)
        qT = area(4096, 16, T)
        skT = area(8192, 16, KEYS)
        scores = area(10240, 16, KEYS)
        cand = area(12288, HEADS, TOPK, TOPK)
        hot = area(14336, HEADS, TOPK, TOPK)
        sk_raw = area(18464, 16, P)
        top_s = area(20512, 16, TOPK)
        top_i = area(20768, 16, TOPK, dtype=U32)
        top_f = area(21024, 16, TOPK)
        best = area(21280, HEADS, TOPK)
        pos = area(21408, HEADS, TOPK, dtype=U32)
        pos_part = area(21536, HEADS, TOPK, dtype=U32)
        pos_f = area(21664, HEADS, TOPK)
        chosen = area(21792, 2, HEADS, TOPK)
        total = area(22048, HEADS)
        ffn_row = area(22100, D)
        gate_w = area(24200, TT, SLOTS)
        ids = area(24456, TT, SLOTS, dtype=I32)
        with nc.Block() as block:
            @block.sync
            def _(sp):
                sp.dma_start(ffn_row, ffn_norm_g[0:1, :].broadcast_to([P, D])).then_inc(sem("ffn_row_loaded"), 16)
                sp.dma_start(sk_raw, peer_sub_keys[0].rearrange("h s n k -> n (h s) k")).then_inc(sem("sk_loaded"), 16)
                load_rest(sp, w_out, "out")
                load_first(sp, peer_w_q, "q")
                load_rest(sp, peer_w_q, "q")
                load_first(sp, w_in_2, "in2")

            @block.scalar
            def _(act):
                for j in range(4):
                    act.wait_ge(sem("sk_transposed"), j + 1)
                    nc.scalar.activation(skT[:, 4 * j:4 * j + 4, :], aux[j].rearrange("p (c t) -> p c t", c=4), ACT.Copy).then_inc(sem("sk_moved"), 1)
                act.wait_ge(sem("sk_moved"), 4)
                for s in range(4):
                    act.wait_ge(bank_free[s], sum(turns["out"]))
                squares(act, h, 4, None)
                roots(act, 4)
                for j in range(8):
                    act.wait_ge(sem("n2_transposed"), j + 1)
                    nc.scalar.activation(actT[:, 4 * (j % 4):4 * (j % 4) + 4, (j // 4) * P:(j // 4) * P + P],
                                         aux[j % 4].rearrange("p (c t) -> p c t", c=4), ACT.Copy).then_inc(sem("n2_moved"), 1)
                first, n = turns["q"]
                for turn in range(n):
                    for s in range(4):
                        act.wait_ge(tile_done[s], first + turn + 1)
                        nc.scalar.activation(qT[:, 8 * turn + 2 * s:8 * turn + 2 * s + 2, :],
                                             bank[s][:, :].rearrange("p (a n) -> p a n", a=2), ACT.Copy).then_inc(bank_free[s], 1)
                for a in range(TT):
                    if a:
                        act.wait_ge(sem("searched"), a)
                    for j in range(4):
                        act.wait_ge(sem("score_product"), 4 * a + j + 1)
                        nc.scalar.activation(scores[:, 4 * j:4 * j + 4, :], aux[j].rearrange("p (c t) -> p c t", c=4),
                                             ACT.Copy).then_inc(sem("scores_moved"), 1)
                    act.wait_ge(sem("soft_shifted"), a + 1)
                    nc.scalar.activation(best, best, ACT.Exp).then_inc(sem("soft_exp"), 1)

            @block.vector
            def _(dve):
                def step(instruction):
                    link(dve, instruction)

                first, n = turns["out"]
                for turn in range(n):
                    for s in range(4):
                        dve.wait_ge(tile_done[s], first + turn + 1)
                        col = (4 * turn + s) * NB
                        nc.vector.tensor_tensor(h[:, :, col:col + NB], h[:, :, col:col + NB],
                                                bank[s][:, :].rearrange("p (a n) -> p a n", a=2), ALU.add).then_inc(bank_free[s], 1)
                reciprocal_rms(dve, 4, D)
                dve.wait_ge(sem("ffn_row_loaded"), 16)
                for a in range(TT):
                    nc.vector.scalar_tensor_tensor(n2[:, a, :], h[:, a, :], rms_col(4, a), ffn_row, ALU.mult, ALU.mult).then_inc(sem("n2_ready"), 1)

                def top16(values, index, source):
                    step(nc.vector.max(values[:, 0:8], source))
                    step(nc.vector.max_index(index[:, 0:8], values[:, 0:8], source))
                    step(nc.vector.match_replace(source, values[:, 0:8], source, LOWEST))
                    step(nc.vector.max(values[:, 8:16], source))
                    step(nc.vector.max_index(index[:, 8:16], values[:, 8:16], source))

                for a in range(TT):
                    for g in range(16):
                        dve.wait_ge(sem("scores_moved"), 4 * a + g // 4 + 1)
                        top16(top_s[:, g, :], top_i[:, g, :], scores[:, g, :])
                    dve.nop().then_inc(sem("searched"), 1)
                    step(nc.vector.tensor_copy(top_f, top_i))
                    of = top_s.rearrange("p (h s) k -> p h s k", s=2)
                    step(nc.vector.tensor_tensor(cand, of[:, :, 0, :].unsqueeze(3).broadcast_to([P, HEADS, TOPK, TOPK]),
                                                 of[:, :, 1, :].unsqueeze(2).broadcast_to([P, HEADS, TOPK, TOPK]), ALU.add))
                    for hd in range(HEADS):
                        top16(best[:, hd, :], pos[:, hd, :], cand[:, hd].rearrange("p a b -> p (a b)"))
                    index = top_f.rearrange("p (h s) k -> p h s k", s=2)
                    for part in range(2):
                        if part == 0:
                            step(nc.vector.tensor_scalar(pos_part, pos, 4, None, ALU.logical_shift_right))
                        else:
                            step(nc.vector.tensor_scalar(pos_part, pos, 15, None, ALU.bitwise_and))
                        step(nc.vector.tensor_copy(pos_f, pos_part))
                        iota = cst[:, C_IOTA:C_IOTA + TOPK].unsqueeze(1).broadcast_to([P, SLOTS, TOPK])
                        flat = hot.rearrange("p h j k -> p (h j) k")
                        step(nc.vector.tensor_tensor(flat, iota, pos_f.rearrange("p h j -> p (h j)").unsqueeze(2).broadcast_to([P, SLOTS, TOPK]), ALU.is_equal))
                        step(nc.vector.tensor_tensor(hot, hot, index[:, :, part, :].unsqueeze(2).broadcast_to([P, HEADS, TOPK, TOPK]), ALU.mult))
                        step(nc.vector.tensor_reduce(chosen[:, part].rearrange("p h j -> p (h j)"), flat, AX_X, ALU.add))
                    step(nc.vector.scalar_tensor_tensor(ids[:, a, :], chosen[:, 0].rearrange("p h j -> p (h j)"), float(KEYS),
                                                        chosen[:, 1].rearrange("p h j -> p (h j)"), ALU.mult, ALU.add))
                    step(nc.vector.tensor_copy(total, best[:, :, 0]))
                    nc.vector.tensor_tensor(best, best, total.unsqueeze(2).broadcast_to([P, HEADS, TOPK]), ALU.subtract).then_inc(sem("soft_shifted"), 1)
                    dve.wait_ge(sem("soft_exp"), a + 1)
                    step(nc.vector.tensor_reduce(total, best, AX_X, ALU.add))
                    step(nc.vector.reciprocal(total, total))
                    step(nc.vector.tensor_tensor(gate_w[:, a, :].rearrange("p (h j) -> p h j", h=HEADS), best,
                                                 total.unsqueeze(2).broadcast_to([P, HEADS, TOPK]), ALU.mult))

            @block.tensor
            def _(pe):
                pe.wait_ge(sem("sk_loaded"), 16)
                for g in range(16):
                    last = nc.tensor.transpose(aux[g // 4][:, (g % 4) * P:(g % 4) * P + P], sk_raw[:, g, :], ident)
                    if g % 4 == 3:
                        last.then_inc(sem("sk_transposed"), 1)
                multiply(pe, *turns["out"], True, mixT)
                pe.wait_ge(sem("squares_done"), 3)
                transpose_tokens(pe, n2, "n2_ready", "n2_transposed", "n2_moved")
                pe.wait_ge(sem("n2_moved"), 8)
                multiply(pe, *turns["q"], False, actT)
                for s in range(4):
                    pe.wait_ge(bank_free[s], sum(turns["q"]))
                for a in range(TT):
                    for g in range(16):
                        if a and g % 4 == 0:
                            pe.wait_ge(sem("scores_moved"), g // 4 + 1)
                        last = nc.tensor.matmul(aux[g // 4][:, (g % 4) * KEYS:(g % 4) * KEYS + KEYS], qT[:, g, a * P:a * P + P],
                                                skT[:, g, :], start=True, stop=True)
                        if g % 4 == 3:
                            last.then_inc(sem("score_product"), 1)

        staged = area(24712, 4, dtype=I32)
        dots = area(24720, 4)
        gelud = area(24724, 4)
        diag = area(24728, 4, P)
        ubuf = [area(4096 + D * s, D) for s in range(4)]
        vbuf = [area(4096 + D * (4 + s), D) for s in range(4)]
        products = area(20512, D)
        u_loaded = [sem(f"u_loaded{s}") for s in range(4)]
        v_loaded = [sem(f"v_loaded{s}") for s in range(4)]
        staged_s = [sem(f"staged{s}") for s in range(4)]
        dot_done = [sem(f"dot_done{s}") for s in range(4)]
        gelu_done = [sem(f"gelu_done{s}") for s in range(4)]
        diag_done = [sem(f"diag_done{s}") for s in range(4)]
        v_used = [sem(f"v_used{s}") for s in range(4)]
        ROUNDS = SLOTS // 4
        with nc.Block() as block:
            @block.gpsimd
            def _(pool):
                def gather(a, i, use):
                    for s in range(4):
                        if not starts(use):
                            pool.wait_ge(dot_done[s], use)
                            pool.wait_ge(v_used[s], use)
                        nc.gpsimd.tensor_copy(staged[:, s:s + 1], ids[:, a, bass.ds(i * 4 + s, 1)]).then_inc(staged_s[s], 1)
                        pool.wait_ge(staged_s[s], use + 1)
                        pool.nop(nofuse=True)
                        at = bass.IndirectOffsetOnAxis(ap=staged[:, s:s + 1], axis=0)
                        nc.gpsimd.indirect_dma_start(ubuf[s], None, peer_u[0], at).then_inc(u_loaded[s], 16)
                        nc.gpsimd.indirect_dma_start(vbuf[s], None, peer_v[0], at).then_inc(v_loaded[s], 16)

                gather(0, 0, 0)
                for a in range(TT):
                    with pool.Fori(1 - a, ROUNDS) as i:
                        gather(a, i, i + a * ROUNDS)

            @block.vector
            def _(dve):
                def weigh(a, i, s, use):
                    dve.wait_ge(gelu_done[s], use + 1)
                    if not starts(use):
                        dve.wait_ge(v_used[s], use)
                    nc.vector.tensor_scalar(diag[:, s, :], ident, gelud[:, s:s + 1], gate_w[:, a, bass.ds(i * 4 + s, 1)],
                                            ALU.mult, ALU.mult).then_inc(diag_done[s], 1)

                def round_of(a, i, use):
                    for s in range(4):
                        dve.wait_ge(u_loaded[s], use * 16 + 16)
                        if s or not starts(use):
                            dve.wait_ge(dot_done[s - 1], use + 1 if s else use)
                        if not starts(use):
                            dve.wait_ge(gelu_done[s], use)
                        nc.vector.scalar_tensor_tensor(products, ubuf[s], 1.0, n2[:, a, :], ALU.mult, ALU.mult,
                                                       accum_out=dots[:, s:s + 1]).then_inc(dot_done[s], 1)
                        if s:
                            weigh(a, i, s - 1, use)
                    weigh(a, i, 3, use)

                round_of(0, 0, 0)
                for a in range(TT):
                    with dve.Fori(1 - a, ROUNDS) as i:
                        round_of(a, i, i + a * ROUNDS)
                    for s in range(4):
                        dve.wait_ge(v_used[s], (a + 1) * ROUNDS)
                    nc.vector.tensor_tensor(h[:, a, :], h[:, a, :], aux_t[:, :, :].rearrange("p s n -> p (s n)"), ALU.add).then_inc(sem("peer_added"), 1)

            @block.scalar
            def _(act):
                def gelus(use):
                    for s in range(4):
                        act.wait_ge(dot_done[s], use + 1)
                        if not starts(use):
                            act.wait_ge(diag_done[s], use)
                        nc.scalar.activation(gelud[:, s:s + 1], dots[:, s:s + 1], ACT.Gelu_apprx_tanh).then_inc(gelu_done[s], 1)

                gelus(0)
                with act.Fori(1, TT * ROUNDS) as i:
                    gelus(i)

            @block.tensor
            def _(pe):
                def accumulate(use, s, start, stop):
                    pe.wait_ge(v_loaded[s], use * 16 + 16)
                    pe.wait_ge(diag_done[s], use + 1)
                    for q in range(4):
                        last = nc.tensor.matmul(aux[q], diag[:, s, :], vbuf[s][:, q * 512:q * 512 + 512], start=start, stop=stop)
                    last.then_inc(v_used[s], 1)

                for a in range(TT):
                    if a:
                        pe.wait_ge(sem("peer_added"), a)
                    for s in range(4):
                        accumulate(a * ROUNDS, s, s == 0, False)
                    with pe.Fori(1, ROUNDS - 1) as i:
                        for s in range(4):
                            accumulate(i + a * ROUNDS, s, False, False)
                    for s in range(4):
                        accumulate((a + 1) * ROUNDS - 1, s, False, s == 3)

        aq = area(0, TT, 16, 64)
        ak = area(2048, TT, 16, 64)
        av = area(4096, TT, 1024)
        ag = area(6144, TT, 1024)
        hqT = area(8192, 8, T)
        fT = [area(10240, 8, T), area(12288, 8, T)]
        hv = area(14336, TT, 1024)
        hgT = area(16384, 8, T)
        un = area(8192, TT, D)
        final_row = area(22100, D)
        turned = area(24148, 4, TT, 16, ROT)
        angle = area(25200, 5, TT * ROT)
        cos_t = area(25296, TT, ROT)
        sin_t = area(25312, TT, ROT)
        pos_i = area(25328, TT, dtype=I32)
        pos_x = area(25330, TT)
        lb = vec_t[:, 0:16]
        one_minus_lb = vec_t[:, 16:32]
        with nc.Block() as block:
            @block.sync
            def _(sp):
                sp.dma_start(final_row, final_norm_g.rearrange("(a d) -> a d", a=1).broadcast_to([P, D])).then_inc(sem("final_row_loaded"), 16)
                load_rest(sp, w_in_2, "in2")
                load_first(sp, w_out_2, "out2")

            @block.gpsimd
            def _(pool):
                with nc.allow_non_contiguous_dma(reason="256 positions"):
                    pool.dma_start(pos_i, positions_2[0].rearrange("(a p) -> p a", p=P)).then_inc(sem("positions_loaded"), 16)

            @block.scalar
            def _(act):
                squares(act, h, 6, None)
                roots(act, 6)
                squares(act, h, 8, "h3_ready")
                roots(act, 8)
                act.wait_ge(sem("lb_ready"), 1)
                nc.scalar.activation(lb, lb, ACT.Sigmoid).then_inc(sem("lb_done"), 1)
                act.wait_ge(sem("angle_ready"), 1)
                nc.scalar.activation(sin_t.rearrange("p a e -> p (a e)"), angle[:, 2, :], ACT.Sin).then_inc(sem("trig_ready"), 1)
                nc.scalar.activation(cos_t.rearrange("p a e -> p (a e)"), angle[:, 3, :], ACT.Sin).then_inc(sem("trig_ready"), 1)
                first, _ = turns["in2"]
                for n, (dst, func, token) in enumerate((
                    (aq.rearrange("p a h e -> p a (h e)"), ACT.Copy, True), (ak.rearrange("p a h e -> p a (h e)"), ACT.Copy, True),
                    (av, ACT.Copy, True), (ag, ACT.Silu, True), (hqT, ACT.Silu, False), (fT[0], ACT.Sigmoid, False),
                    (fT[1], ACT.Sigmoid, False), (hv, ACT.Copy, True), (hgT, ACT.Silu, False),
                )):
                    for s in range(4):
                        act.wait_ge(tile_done[s], first + n + 1)
                        part = dst[:, :, s * NB:s * NB + NB] if token else dst[:, 2 * s:2 * s + 2, :]
                        nc.scalar.activation(part, bank[s][:, :].rearrange("p (a n) -> p a n", a=2), func).then_inc(bank_free[s], 1)

            @block.vector
            def _(dve):
                def step(instruction):
                    link(dve, instruction)

                reciprocal_rms(dve, 6, D)
                dve.wait_ge(sem("final_row_loaded"), 16)
                for a in range(TT):
                    nc.vector.scalar_tensor_tensor(h[:, a, :], h[:, a, :], rms_col(6, a), final_row, ALU.mult, ALU.mult).then_inc(sem("h3_ready"), 1)
                reciprocal_rms(dve, 8, D)
                dve.wait_ge(sem("h3_ready"), 2)
                for a in range(TT):
                    nc.vector.tensor_scalar(un[:, a, :], h[:, a, :], rms_col(8, a), None, ALU.mult).then_inc(sem("un_ready"), 1)
                for j in range(8):
                    a, q = j // 4, j % 4
                    dve.wait_ge(sem("un_transposed"), j + 1)
                    nc.vector.tensor_tensor(actT[:, 4 * q:4 * q + 4, a * P:a * P + P], aux[j % 4].rearrange("p (c t) -> p c t", c=4),
                                            colsB[:, B_PRE + 4 * q:B_PRE + 4 * q + 4].unsqueeze(2).broadcast_to([P, 4, P]),
                                            ALU.mult).then_inc(sem("un_moved"), 1)
                step(nc.vector.tensor_tensor(lb[:, 0:8], colsB[:, B_LBF:B_LBF + 8], colsB[:, B_LBF + 8:B_LBF + 16], ALU.subtract))
                nc.vector.tensor_tensor(lb[:, 8:16], colsB[:, B_LBB:B_LBB + 8], colsB[:, B_LBB + 8:B_LBB + 16], ALU.subtract).then_inc(sem("lb_ready"), 1)
                dve.wait_ge(sem("lb_done"), 1)
                step(nc.vector.tensor_scalar(one_minus_lb, lb, -1.0, 1.0, ALU.mult, ALU.add))
                dve.wait_ge(sem("positions_loaded"), 16)
                step(nc.vector.tensor_copy(pos_x, pos_i))
                inv = cst[:, C_INV:C_INV + ROT].unsqueeze(1).broadcast_to([P, TT, ROT])
                step(nc.vector.tensor_tensor(angle[:, 0, :].rearrange("p (a e) -> p a e", a=TT), inv,
                                             pos_x.unsqueeze(2).broadcast_to([P, TT, ROT]), ALU.mult))
                step(nc.vector.tensor_scalar(angle[:, 1, :], angle[:, 0, :], 1.0 / TWO_PI, ROUNDER, ALU.mult, ALU.add))
                step(nc.vector.tensor_scalar(angle[:, 1, :], angle[:, 1, :], -ROUNDER, None, ALU.add))
                step(nc.vector.scalar_tensor_tensor(angle[:, 2, :], angle[:, 1, :], -TURN_PARTS[0], angle[:, 0, :], ALU.mult, ALU.add))
                step(nc.vector.scalar_tensor_tensor(angle[:, 2, :], angle[:, 1, :], -TURN_PARTS[1], angle[:, 2, :], ALU.mult, ALU.add))
                step(nc.vector.scalar_tensor_tensor(angle[:, 2, :], angle[:, 1, :], -TURN_PARTS[2], angle[:, 2, :], ALU.mult, ALU.add))
                step(nc.vector.tensor_scalar(angle[:, 2, :], angle[:, 2, :], 3.1415925, -3.1415925, ALU.min, ALU.max))
                step(nc.vector.tensor_scalar(angle[:, 4, :], angle[:, 2, :], -1.0, None, ALU.mult))
                step(nc.vector.tensor_tensor(angle[:, 3, :], angle[:, 4, :], angle[:, 2, :], ALU.min))
                nc.vector.tensor_scalar(angle[:, 3, :], angle[:, 3, :], float(np.pi / 2), None, ALU.add).then_inc(sem("angle_ready"), 1)
                dve.wait_ge(sem("trig_ready"), 2)
                c = cos_t.unsqueeze(2).broadcast_to([P, TT, 16, ROT])
                sn = sin_t.unsqueeze(2).broadcast_to([P, TT, 16, ROT])
                for n, t in enumerate((aq, ak)):
                    for s in range(4):
                        dve.wait_ge(bank_free[s], turns["in2"][0] + n + 1)
                    x1, x2 = t[:, :, :, 0:ROT], t[:, :, :, ROT:2 * ROT]
                    for m, (u, v) in enumerate(((x1, c), (x2, sn), (x2, c), (x1, sn))):
                        step(nc.vector.tensor_tensor(turned[:, m], u, v, ALU.mult))
                    step(nc.vector.tensor_tensor(x1, turned[:, 0], turned[:, 1], ALU.subtract))
                    step(nc.vector.tensor_tensor(x2, turned[:, 2], turned[:, 3], ALU.add))

            @block.tensor
            def _(pe):
                transpose_tokens(pe, un, "un_ready", "un_transposed", "un_moved")
                pe.wait_ge(sem("un_moved"), 8)
                first, _ = turns["in2"]
                multiply(pe, first, 4, True, actT)
                multiply(pe, first + 4, 3, False, actT)
                multiply(pe, first + 7, 1, True, actT)
                multiply(pe, first + 8, 1, False, actT)

        mix2T = actT
        aqT = area(18432, 8, T)
        akT = area(20480, 8, T)
        logits = [area(22528 + 512 * s, TT, T) for s in range(2)]
        probs = [area(23552 + 512 * s, TT, T) for s in range(2)]
        probsT = [area(24576 + 512 * s, TT, T) for s in range(2)]
        asum = area(25600, 16, TT)
        amax = area(25632, 16, TT)
        arec = area(25664, 16, TT)
        att_o = aq
        att_bias = cst[:, C_BIAS:C_BIAS + TT * T].rearrange("p (a t) -> p a t", a=TT)
        ATT_SCALE = 64 ** -0.5
        with nc.Block() as block:
            @block.scalar
            def _(act):
                for j in range(8):
                    act.wait_ge(sem("qk_transposed"), j + 1)
                    half, a = j % 2, (j // 2) % 2
                    dst = (aqT if j < 4 else akT)[:, 4 * half:4 * half + 4, a * P:a * P + P]
                    nc.scalar.activation(dst, aux[j % 4].rearrange("p (c t) -> p c t", c=4), ACT.Copy,
                                         scale=ATT_SCALE if j < 4 else 1.0).then_inc(sem("qk_moved"), 1)
                for i in range(17):
                    if i < 16:
                        act.wait_ge(sem("att_max"), i + 1)
                        if i >= 2:
                            act.wait_ge(sem("probs_transposed"), i - 1)
                        for a in range(TT):
                            nc.scalar.activation(probs[i % 2][:, a, :], logits[i % 2][:, a, :], ACT.Exp, bias=amax[:, i, a:a + 1],
                                                 accum_out=asum[:, i, a:a + 1]).then_inc(sem("probs_ready"), 1)
                    if i >= 1:
                        hd = i - 1
                        act.wait_ge(sem("probs_transposed"), hd + 1)
                        if hd >= 2:
                            act.wait_ge(sem("att_product"), hd - 1)
                        nc.scalar.activation(probsT[hd % 2], bank[2 + hd % 2][:, :].rearrange("p (c t) -> p c t", c=2),
                                             ACT.Copy).then_inc(sem("probs_moved"), 1)
                for j in range(4):
                    act.wait_ge(sem("yatt_transposed"), j + 1)
                    half, a = j % 2, j // 2
                    nc.scalar.activation(mix2T[:, 4 * half:4 * half + 4, a * P:a * P + P],
                                         aux[j % 4].rearrange("p (c t) -> p c t", c=4), ACT.Copy).then_inc(sem("yatt_moved"), 1)

            @block.vector
            def _(dve):
                def step(instruction):
                    link(dve, instruction)

                for i in range(18):
                    if i < 16:
                        dve.wait_ge(sem("att_scores"), i + 1)
                        if i >= 2:
                            dve.wait_ge(sem("probs_ready"), 2 * (i - 1))
                        nc.vector.tensor_tensor(logits[i % 2], bank[i % 2][:, :].rearrange("p (a t) -> p a t", a=TT), att_bias,
                                                ALU.add).then_inc(sem("logits_ready"), 1)
                        dve.wait_ge(sem("logits_ready"), i + 1)
                        nc.vector.tensor_reduce(amax[:, i, :], logits[i % 2], AX_X, ALU.max, negate=True).then_inc(sem("att_max"), 1)
                    if i >= 2:
                        hd = i - 2
                        dve.wait_ge(sem("att_product"), hd + 1)
                        step(nc.vector.reciprocal(arec[:, hd, :], asum[:, hd, :]))
                        nc.vector.tensor_tensor(att_o[:, :, hd, :], aux[hd % 4][:, 0:P].rearrange("p (a e) -> p a e", a=TT),
                                                arec[:, hd, :].unsqueeze(2).broadcast_to([P, TT, 64]), ALU.mult).then_inc(sem("att_moved"), 1)
                dve.wait_ge(sem("att_moved"), 16)
                for a in range(TT):
                    o = att_o[:, a].rearrange("p h e -> p (h e)")
                    nc.vector.tensor_tensor(o, o, ag[:, a, :], ALU.mult).then_inc(sem("yatt_ready"), 1)

            @block.tensor
            def _(pe):
                for j in range(8):
                    half, a = j % 2, (j // 2) % 2
                    if j >= 4:
                        pe.wait_ge(sem("qk_moved"), j - 3)
                    src = (aq if j < 4 else ak).rearrange("p a h e -> p a (h e)")
                    for c in range(4):
                        last = nc.tensor.transpose(aux[j % 4][:, c * P:c * P + P], src[:, a, (4 * half + c) * P:(4 * half + c) * P + P], ident)
                    last.then_inc(sem("qk_transposed"), 1)
                pe.wait_ge(sem("qk_moved"), 8)
                for i in range(18):
                    if i < 16:
                        lo, c = 64 * (i % 2), i // 2
                        if i >= 2:
                            pe.wait_ge(sem("logits_ready"), i - 1)
                        for a in range(TT):
                            last = nc.tensor.matmul(bank[i % 2][:, a * T:a * T + T], aqT[lo:lo + 64, c, a * P:a * P + P],
                                                    akT[lo:lo + 64, c, :], start=True, stop=True)
                        last.then_inc(sem("att_scores"), 1)
                    if 1 <= i <= 16:
                        hd = i - 1
                        pe.wait_ge(sem("probs_ready"), 2 * hd + 2)
                        if hd >= 2:
                            pe.wait_ge(sem("probs_moved"), hd - 1)
                        for k in range(TT):
                            for a in range(TT):
                                at = k * T + a * P
                                last = nc.tensor.transpose(bank[2 + hd % 2][:, at:at + P], probs[hd % 2][:, a, k * P:k * P + P], ident)
                        last.then_inc(sem("probs_transposed"), 1)
                    if i >= 2:
                        hd = i - 2
                        pe.wait_ge(sem("probs_moved"), hd + 1)
                        if hd >= 4:
                            pe.wait_ge(sem("att_moved"), hd - 3)
                        for a in range(TT):
                            for k in range(TT):
                                last = nc.tensor.matmul(aux[hd % 4][:, a * 64:a * 64 + 64], probsT[hd % 2][:, k, a * P:a * P + P],
                                                        av[:, k, hd * 64:hd * 64 + 64], start=k == 0, stop=k == TT - 1)
                        last.then_inc(sem("att_product"), 1)
                pe.wait_ge(sem("att_moved"), 16)
                transpose_tokens(pe, att_o.rearrange("p a h e -> p a (h e)"), "yatt_ready", "yatt_transposed", "yatt_moved", groups=2)

        klast = area(0, 8, T)
        bsum = area(2048, 8, T)
        qstart = area(4096, 8, T)
        qmid = area(6144, 8, T)
        kmid = area(18432, 8, T)
        ktok = area(20480, TT, 8, P)
        inner = area(22528, 8, T)
        state = [area(24576 + 1024 * s, 8, P) for s in range(2)]
        chunk_decay = vec_t[:, 64:128].rearrange("p (h c) -> p h c", h=8)
        osq = area(0, 4, 512)
        orms = area(2048, 4, 512)
        ones = cst[:, C_ONES:C_ONES + P]

        def by_chunk(v):
            return v.rearrange("p h (c t) -> p (h c) t", t=CHUNK)

        def of_chunk(v, t):
            return by_chunk(v)[:, :, t:t + 1].broadcast_to([P, 8 * NCH, CHUNK])

        with nc.Block() as block:
            @block.gpsimd
            def _(pool):
                for d in range(2):
                    if d:
                        pool.wait_ge(sem("inner_product"), 4)
                    nc.gpsimd.memset(kmid, 1.0).then_inc(sem("scan_mask"), 1)
                    pool.wait_ge(sem("scan_mask"), 2 * d + 1)
                    edge = (CHUNK - 1) if d else 0
                    nc.gpsimd.memset(by_chunk(kmid)[:, :, edge:edge + 1], 0.0).then_inc(sem("scan_mask"), 1)

            @block.scalar
            def _(act):
                for d in range(2):
                    act.wait_ge(sem("forget_ready"), d + 1)
                    nc.scalar.activation(klast, fT[d], ACT.Ln).then_inc(sem("log_ready"), 1)
                    act.wait_ge(sem("sum_ready"), d + 1)
                    if d:
                        act.wait_ge(sem("between"), NCH - 1)
                    nc.scalar.activation(qstart, bsum, ACT.Exp).then_inc(sem("start_exp"), 1)
                    act.wait_ge(sem("from_mid"), d + 1)
                    nc.scalar.activation(kmid, qmid, ACT.Exp, scale=-1.0).then_inc(sem("mid_exp"), 1)
                    act.wait_ge(sem("mid_exp"), 2 * d + 1)
                    nc.scalar.activation(qmid, qmid, ACT.Exp).then_inc(sem("mid_exp"), 1)
                    act.wait_ge(sem("to_last"), d + 1)
                    nc.scalar.activation(klast, klast, ACT.Exp).then_inc(sem("last_exp"), 1)
                    for j in range(4):
                        act.wait_ge(sem("k_transposed"), 4 * d + j + 1)
                        nc.scalar.activation(ktok[:, j // 2, 4 * (j % 2):4 * (j % 2) + 4, :], bank[j][:, :].rearrange("p (c t) -> p c t", c=4),
                                             ACT.Copy).then_inc(sem("k_moved"), 1)
                act.wait_ge(sem("between"), 2 * (NCH - 1))
                for j in range(4):
                    nc.scalar.activation(osq[:, j, :], aux[j], ACT.Square).then_inc(sem("o_squared"), 1)
                act.wait_ge(sem("o_mean"), 1)
                nc.scalar.activation(orms, orms, ACT.Sqrt).then_inc(sem("o_root"), 1)

            @block.vector
            def _(dve):
                def step(instruction):
                    link(dve, instruction)

                for d in range(2):
                    way = slice(None, None, -1) if d else slice(None)
                    last = 0 if d else CHUNK - 1
                    mid = CHUNK // 2 - (0 if d else 1)
                    for hd in range(8):
                        col = 8 * d + hd
                        f = nc.vector.tensor_scalar(fT[d][:, hd, :], fT[d][:, hd, :], one_minus_lb[:, col:col + 1], lb[:, col:col + 1],
                                                    ALU.mult, ALU.add)
                        step(f)
                    dve.nop().then_inc(sem("forget_ready"), 1)
                    dve.wait_ge(sem("log_ready"), d + 1)
                    step(nc.vector.tensor_scalar(fT[d], fT[d], -1.0, 1.0, ALU.mult, ALU.add))
                    dve.wait_ge(sem("scan_mask"), 2 * d + 2)
                    flat = [v.rearrange("p h t -> p (h t)")[:, way] for v in (bsum, kmid, klast)]
                    nc.vector.tensor_tensor_scan(*flat, 0.0, ALU.mult, ALU.add).then_inc(sem("sum_ready"), 1)
                    dve.wait_ge(sem("sum_ready"), d + 1)
                    nc.vector.tensor_tensor(by_chunk(qmid), by_chunk(bsum), of_chunk(bsum, mid), ALU.subtract).then_inc(sem("from_mid"), 1)
                    nc.vector.tensor_tensor(by_chunk(klast), of_chunk(bsum, last), by_chunk(bsum), ALU.subtract).then_inc(sem("to_last"), 1)
                    dve.wait_ge(sem("start_exp"), d + 1)
                    step(nc.vector.tensor_copy(chunk_decay, qstart.rearrange("p h (c t) -> p h c t", t=CHUNK)[:, :, :, last]))
                    step(nc.vector.tensor_tensor(qstart, qstart, hqT, ALU.mult))
                    dve.wait_ge(sem("mid_exp"), 2 * d + 2)
                    step(nc.vector.tensor_tensor(qmid, qmid, hqT, ALU.mult))
                    nc.vector.tensor_tensor(kmid, kmid, fT[d], ALU.mult).then_inc(sem("mid_ready"), 1)
                    dve.wait_ge(sem("last_exp"), d + 1)
                    nc.vector.tensor_tensor(klast, klast, fT[d], ALU.mult).then_inc(sem("last_ready"), 1)
                    for j in range(4):
                        dve.wait_ge(sem("inner_product"), 4 * d + j + 1)
                        mask = cst[:, (C_BWD if d else C_FWD):(C_BWD if d else C_FWD) + P].unsqueeze(1).broadcast_to([P, 4, P])
                        nc.vector.scalar_tensor_tensor(inner[:, 2 * j:2 * j + 2, :].rearrange("p h (a t) -> p (h a) t", a=TT),
                                                       bank[j][:, :].rearrange("p (c t) -> p c t", c=4), 1e30, mask, ALU.min, ALU.mult).then_inc(sem("inner_ready"), 1)
                    for c in range(NCH - 1):
                        chunk = NCH - 1 - c if d else c
                        n = d * (NCH - 1) + c
                        new, old = state[c % 2], state[1 - c % 2]
                        if n > 1:
                            dve.wait_ge(sem("between"), max(n - 1, d * (NCH - 1)))
                        if c:
                            step(nc.vector.tensor_tensor(new, old, chunk_decay[:, :, chunk:chunk + 1].broadcast_to([P, 8, P]), ALU.mult))
                        for half in range(2):
                            dve.wait_ge(sem("outer_product"), 2 * n + half + 1)
                            kv = bank[2 * (c % 2) + half][:, :].rearrange("p (h v) -> p h v", h=4)
                            to = new[:, 4 * half:4 * half + 4, :]
                            if c:
                                nc.vector.tensor_tensor(to, to, kv, ALU.add).then_inc(sem("state_ready"), 1)
                            else:
                                nc.vector.tensor_copy(to, kv).then_inc(sem("state_ready"), 1)
                            dve.wait_ge(sem("state_ready"), 2 * n + half + 1)

                for j in range(4):
                    dve.wait_ge(sem("o_sums"), j + 1)
                    mean = nc.vector.tensor_scalar(orms[:, j, :], bank[j][:, :], 1.0 / P, EPS, ALU.mult, ALU.add)
                    if j < 3:
                        step(mean)
                mean.then_inc(sem("o_mean"), 1)
                dve.wait_ge(sem("o_root"), 1)
                step(nc.vector.reciprocal(orms, orms))
                for j in range(4):
                    step(nc.vector.scalar_tensor_tensor(orms[:, j, :], aux[j], colsB[:, B_HG:B_HG + 1], orms[:, j, :], ALU.mult, ALU.mult))
                step(nc.vector.tensor_tensor(mix2T[:, 8:16, :].rearrange("p h t -> p (h t)"), orms.rearrange("p s n -> p (s n)"),
                                             hgT.rearrange("p h t -> p (h t)"), ALU.mult))

            @block.tensor
            def _(pe):
                for d in range(2):
                    pe.wait_ge(sem("mid_ready"), d + 1)
                    for j in range(4):
                        if d:
                            pe.wait_ge(sem("state_ready"), 2 * (NCH - 1))
                        for c in range(4):
                            hd, a = 2 * j + c // 2, c % 2
                            last = nc.tensor.matmul(bank[j][:, c * P:c * P + P], kmid[:, hd, a * P:a * P + P], qmid[:, hd, a * P:a * P + P],
                                                    start=True, stop=True)
                        last.then_inc(sem("inner_product"), 1)
                    pe.wait_ge(sem("last_ready"), d + 1)
                    for j in range(4):
                        pe.wait_ge(sem("inner_ready"), 4 * d + j + 1)
                        for c in range(4):
                            last = nc.tensor.transpose(bank[j][:, c * P:c * P + P], klast[:, 4 * (j % 2) + c, (j // 2) * P:(j // 2) * P + P], ident)
                        last.then_inc(sem("k_transposed"), 1)
                    for hd in range(8):
                        for a in range(TT):
                            nc.tensor.matmul(aux[hd // 2][:, (hd % 2) * T + a * P:(hd % 2) * T + a * P + P], hv[:, a, hd * P:hd * P + P],
                                             inner[:, hd, a * P:a * P + P], start=d == 0 and hd % 2 == 0 and a == 0, stop=False, skip_group_check=True)
                    pe.wait_ge(sem("k_moved"), 4 * d + 4)
                    for c in range(NCH - 1):
                        n = d * (NCH - 1) + c
                        chunk = NCH - 1 - c if d else c
                        nxt = chunk - 1 if d else chunk + 1
                        lo, a = CHUNK * (chunk % 4), chunk // 4
                        if c >= 2:
                            pe.wait_ge(sem("state_ready"), 2 * n - 2)
                        for hd in range(8):
                            last = nc.tensor.matmul(bank[2 * (c % 2) + hd // 4][:, (hd % 4) * P:(hd % 4) * P + P], ktok[lo:lo + CHUNK, a, hd, :],
                                                    hv[lo:lo + CHUNK, a, hd * P:hd * P + P], start=True, stop=True)
                            if hd % 4 == 3:
                                last.then_inc(sem("outer_product"), 1)
                        for hd in range(8):
                            if hd % 4 == 0:
                                pe.wait_ge(sem("state_ready"), 2 * n + hd // 4 + 1)
                            at = (hd % 2) * T + nxt * CHUNK
                            last = nc.tensor.matmul(aux[hd // 2][:, at:at + CHUNK], state[c % 2][:, hd, :],
                                                    qstart[:, hd, nxt * CHUNK:nxt * CHUNK + CHUNK], start=False,
                                                    stop=d == 1 and c == NCH - 2, skip_group_check=True)
                        last.then_inc(sem("between"), 1)
                for j in range(4):
                    pe.wait_ge(sem("o_squared"), j + 1)
                    nc.tensor.matmul(bank[j][:, :], ones, osq[:, j, :], start=True, stop=True).then_inc(sem("o_sums"), 1)

        y = area(0, TT, D)
        post_row = area(4096, D)
        ple_row = area(6144, D)
        emb = area(8192, TT, D)
        w_pp = area(12288, 2, D)
        p_raw = area(16384, TT, 256)
        pT = area(16896, 2, T)
        with nc.Block() as block:
            @block.sync
            def _(sp):
                sp.dma_start(p_raw, p_2[0, 0].rearrange("(a p) d -> p a d", p=P)).then_inc(sem("p_loaded"), 16)
                sp.dma_start(w_pp, w_pp_2[0].rearrange("(k p) n -> p k n", p=P)).then_inc(sem("w_pp_loaded"), 16)
                load_rest(sp, w_out_2, "out2")
                sp.dma_start(post_row, g_post_2.broadcast_to([P, D])).then_inc(sem("post_row_loaded"), 16)
                sp.dma_start(ple_row, g_ple_2.broadcast_to([P, D])).then_inc(sem("ple_row_loaded"), 16)
                load_first(sp, w_pg_2, "pg")
                load_rest(sp, w_pg_2, "pg")
                for a in range(TT):
                    sp.wait_ge(sem("out_ready"), a + 1)
                    sp.dma_start(out[0, a * P:a * P + P, :], h[:, a, :]).then_inc(sem("out_stored"), 16)
                sp.wait_ge(sem("out_stored"), 16 * TT)

            @block.scalar
            def _(act):
                def read_products(name, func):
                    first, n = turns[name]
                    for turn in range(n):
                        for s in range(4):
                            act.wait_ge(tile_done[s], first + turn + 1)
                            col = (4 * turn + s) * NB
                            nc.scalar.activation(y[:, :, col:col + NB], bank[s][:, :].rearrange("p (a n) -> p a n", a=2),
                                                 func).then_inc(bank_free[s], 1)

                act.wait_ge(sem("p_transposed"), 1)
                nc.scalar.activation(pT, aux[0].rearrange("p (k t) -> p k t", k=2), ACT.Copy).then_inc(sem("p_moved"), 1)
                read_products("out2", ACT.Copy)
                for j in range(8):
                    act.wait_ge(sem("emb_product"), j + 1)
                    nc.scalar.activation(emb[:, j // 4, (j % 4) * 512:(j % 4) * 512 + 512], aux[j % 4], ACT.Copy).then_inc(sem("emb_moved"), 1)
                act.wait_ge(sem("emb_moved"), 8)
                for s in range(4):
                    act.wait_ge(bank_free[s], sum(turns["out2"]))
                squares(act, y, 10, None)
                roots(act, 10)
                for j in range(8):
                    act.wait_ge(sem("h4_transposed"), j + 1)
                    nc.scalar.activation(actT[:, 4 * (j % 4):4 * (j % 4) + 4, (j // 4) * P:(j // 4) * P + P],
                                         aux[j % 4].rearrange("p (c t) -> p c t", c=4), ACT.Copy).then_inc(sem("h4_moved"), 1)
                read_products("pg", ACT.Sigmoid)
                squares(act, y, 12, "gated")
                roots(act, 12)

            @block.vector
            def _(dve):
                def step(instruction):
                    link(dve, instruction)

                reciprocal_rms(dve, 10, D)
                dve.wait_ge(sem("post_row_loaded"), 16)
                for a in range(TT):
                    step(nc.vector.scalar_tensor_tensor(y[:, a, :], y[:, a, :], rms_col(10, a), post_row, ALU.mult, ALU.mult))
                    nc.vector.tensor_tensor(h[:, a, :], h[:, a, :], y[:, a, :], ALU.add).then_inc(sem("h4_ready"), 1)
                for s in range(4):
                    dve.wait_ge(bank_free[s], sum(turns["pg"]))
                for a in range(TT):
                    nc.vector.tensor_tensor(y[:, a, :], y[:, a, :], emb[:, a, :], ALU.mult).then_inc(sem("gated"), 1)
                reciprocal_rms(dve, 12, D)
                dve.wait_ge(sem("ple_row_loaded"), 16)
                for a in range(TT):
                    step(nc.vector.scalar_tensor_tensor(y[:, a, :], y[:, a, :], rms_col(12, a), ple_row, ALU.mult, ALU.mult))
                    dve.wait_ge(sem("h4_ready"), a + 1)
                    nc.vector.tensor_tensor(h[:, a, :], h[:, a, :], y[:, a, :], ALU.add).then_inc(sem("out_ready"), 1)

            @block.tensor
            def _(pe):
                pe.wait_ge(sem("p_loaded"), 16)
                for k in range(2):
                    for a in range(TT):
                        last = nc.tensor.transpose(aux[0][:, k * T + a * P:k * T + a * P + P], p_raw[:, a, k * P:k * P + P], ident)
                last.then_inc(sem("p_transposed"), 1)
                multiply(pe, *turns["out2"], True, mix2T)
                pe.wait_ge(sem("w_pp_loaded"), 16)
                pe.wait_ge(sem("p_moved"), 1)
                for j in range(8):
                    a, q = j // 4, j % 4
                    if j >= 4:
                        pe.wait_ge(sem("emb_moved"), j - 3)
                    for k in range(2):
                        last = nc.tensor.matmul(aux[q], pT[:, k, a * P:a * P + P], w_pp[:, k, q * 512:q * 512 + 512], start=k == 0, stop=k == 1)
                    last.then_inc(sem("emb_product"), 1)
                transpose_tokens(pe, h, "h4_ready", "h4_transposed", "h4_moved")
                pe.wait_ge(sem("h4_moved"), 8)
                multiply(pe, *turns["pg"], True, actT)


_INS = ["x", "mix_norm_g", "w_in", "conv_w", "conv_b", "lru_w_a", "lru_b_a", "lru_w_x", "lru_b_x",
        "lru_lambda", "gmlp_ln_g", "gmlp_ln_b", "gmlp_w_s", "gmlp_b_s", "w_out", "ffn_norm_g",
        "peer_w_q", "peer_sub_keys", "peer_u", "peer_v", "final_norm_g", "p_2", "positions_2",
        "w_in_2", "w_out_2", "g_pre_2", "g_post_2", "g_hg_2", "lb_fwd_2", "lb_bwd_2", "w_pg_2",
        "w_pp_2", "g_ple_2"]


def kernel(**inputs):
    import concourse.bacc as bacc
    from concourse.bass_utils import run_bass_kernel_spmd

    nc = bacc.Bacc("TRN2", target_bir_lowering=False, num_devices=1)
    arrays, args = {}, []
    for name in _INS:
        a = np.ascontiguousarray(inputs[name])
        arrays[f"in_{name}_dram"] = a
        args.append(nc.dram_tensor(f"in_{name}_dram", a.shape, mybir.dt.from_np(a.dtype), kind="ExternalInput").ap())
    arrays["constants_dram"] = shape_constants()
    args.append(nc.dram_tensor("constants_dram", (P, C_END), F32, kind="ExternalInput").ap())
    out = nc.dram_tensor("out_dram", (1, T, D), F32, kind="ExternalOutput").ap()
    build(nc, *args, out)
    r = run_bass_kernel_spmd(nc, [arrays], core_ids=[0])
    return r.results[0]["out_dram"]
```

```python
from contextlib import ExitStack

import numpy as np

import concourse.bass as bass
from concourse import mybir

F32 = mybir.dt.float32
F32R = mybir.dt.float32r
I32 = mybir.dt.int32
U32 = mybir.dt.uint32
ALU = mybir.AluOpType
ACT = mybir.ActivationFunctionType
AX_X = mybir.AxisListType.X

P = 128
D = 2048
T = 256
TT = T // P
KC = D // P
NB = 512
KU = KC // 4
EPS = 1e-6
LRU = 1024
HEADS = 8
KEYS = 128
TOPK = 16
SLOTS = HEADS * TOPK
CHUNK = 32
NCH = T // CHUNK
LRU_C = 8.0
LOWEST = -3.0e38
ROT = 8
TWO_PI = 2 * np.pi
TURN_PARTS = (6.28125, 0.001934051513671875, TWO_PI - 6.28125 - 0.001934051513671875)
ROUNDER = 1.5 * 2.0 ** 23

C_IDENT = 0
C_BIAS = C_IDENT + P
C_IOTA = C_BIAS + TT * T
C_FWD = C_IOTA + TOPK
C_BWD = C_FWD + P
C_INV = C_BWD + P
C_ONES = C_INV + ROT
C_END = C_ONES + P


def shape_constants():
    c = np.zeros((P, C_END), np.float32)
    c[:, C_IDENT:C_IDENT + P] = np.eye(P)
    i, j = np.arange(T)[:, None], np.arange(T)[None, :]
    times = np.zeros((T, T))
    for window, dilation in ((128, 1), (512, 4), (2048, 16)):
        times += (np.abs(i - j) <= window // 2) & ((i - j) % dilation == 0)
    bias = np.where(times > 0, np.log(np.maximum(times, 1)), -1e30)
    c[:, C_BIAS:C_BIAS + TT * T] = bias.reshape(TT, P, T).transpose(1, 0, 2).reshape(P, -1)
    c[:, C_IOTA:C_IOTA + TOPK] = np.arange(TOPK)
    s, t = np.arange(P)[:, None], np.arange(P)[None, :]
    same = s // CHUNK == t // CHUNK
    c[:, C_FWD:C_FWD + P] = same & (s <= t)
    c[:, C_BWD:C_BWD + P] = same & (s >= t)
    exponent = -np.arange(0, 2 * ROT, 2, dtype=np.float32) / np.float32(2 * ROT)
    c[:, C_INV:C_INV + ROT] = np.power(np.float32(500000.0), exponent)
    c[:, C_ONES:C_ONES + P] = 1.0
    return c


A_MIX, A_CONVW, A_CONVB, A_BA, A_BX, A_LAM, A_FFN = 0, 16, 48, 56, 72, 88, 104
A_ROWS = 120
B_LBF, B_LBB, B_PRE, B_HG = 0, 16, 32, 48
B_ROWS = 49


def build(nc, x, mix_norm_g, w_in, conv_w, conv_b, lru_w_a, lru_b_a, lru_w_x, lru_b_x, lru_lambda,
          gmlp_ln_g, gmlp_ln_b, gmlp_w_s, gmlp_b_s, w_out, ffn_norm_g, peer_w_q, peer_sub_keys,
          peer_u, peer_v, final_norm_g, p_2, positions_2, w_in_2, w_out_2, g_pre_2, g_post_2,
          g_hg_2, lb_fwd_2, lb_bwd_2, w_pg_2, w_pp_2, g_ple_2, constants, out):
    ctx = ExitStack()
    with ctx:
        def sbuf(name, words, dtype=F32):
            return ctx.enter_context(nc.sbuf_tensor(name, [P, words], dtype))

        sems = {}

        def sem(name):
            if name not in sems:
                sems[name] = ctx.enter_context(nc.semaphore(name))
            return sems[name]

        h_t = sbuf("residual", TT * D)
        h = h_t[:, :].rearrange("p (a d) -> p a d", a=TT)
        act_hi = ctx.enter_context(nc.sbuf_tensor("act_hi", [P, KC, T], F32R))[:, :, :]
        act_lo = ctx.enter_context(nc.sbuf_tensor("act_lo", [P, KC, T], F32R))[:, :, :]
        w_raw = [ctx.enter_context(nc.sbuf_tensor(f"w_raw{s}", [P, KU, NB], F32)) for s in range(4)]
        w_hi = [ctx.enter_context(nc.sbuf_tensor(f"w_hi{s}", [P, KU, NB], F32R)) for s in range(2)]
        w_lo = [ctx.enter_context(nc.sbuf_tensor(f"w_lo{s}", [P, KU, NB], F32R)) for s in range(2)]
        cst = sbuf("constants_sb", C_END)
        colsA = sbuf("colsA", A_ROWS)
        colsB = sbuf("colsB", B_ROWS)
        stat = sbuf("stat", 64)
        area_t = sbuf("area", 22830)
        vec_t = sbuf("vectors", 2 * P + 128)

        def area(at, *dims, dtype=F32):
            n = int(np.prod(dims))
            v = area_t[:, at:at + n]
            if dtype != F32:
                v = v.bitcast(dtype)
            if len(dims) == 2:
                v = v.rearrange("p (a b) -> p a b", a=dims[0])
            if len(dims) == 3:
                v = v.rearrange("p (a b c) -> p a b c", a=dims[0], b=dims[1])
            if len(dims) == 4:
                v = v.rearrange("p (a b c d) -> p a b c d", a=dims[0], b=dims[1], c=dims[2])
            return v

        bank_t = ctx.enter_context(nc.psum_tensor("banks", [P, 4, 512], F32))
        bank = [bank_t[:, s, :] for s in range(4)]
        pair = [bank_t[:, 2 * j:2 * j + 2, :] for j in range(2)]
        aux_t = ctx.enter_context(nc.psum_tensor("aux", [P, 4, 512], F32))
        aux = [aux_t[:, s, :] for s in range(4)]
        ident = cst[:, C_IDENT:C_IDENT + P]

        chained = {}

        def link(engine, instruction):
            name = f"{engine.engine.name}_own"
            chained[name] = chained.get(name, 0) + 1
            instruction.then_inc(sem(name), 1)
            engine.wait_ge(sem(name), chained[name])

        w_loaded = [sem(f"w_loaded{s}") for s in range(4)]
        hi_ready = [sem(f"hi_ready{b}") for b in range(2)]
        lo_ready = [sem(f"lo_ready{b}") for b in range(2)]
        unit_used = [sem(f"unit_used{b}") for b in range(2)]
        pair_free = [sem(f"pair_free{j}") for j in range(2)]

        turns = {}
        for name, blocks in (("in", 8), ("out", 4), ("q", 4), ("in2", 18), ("out2", 4), ("pg", 4)):
            turns[name] = (sum(n for _, n in turns.values()), blocks // 2)

        def starts(use):
            return isinstance(use, int) and use == 0

        def split_use(turn, j, u):
            return turn * 4 + (2 * j + u // 2)

        def load_block(sp, w, turn, j, col, units=range(4)):
            wv = w[0].rearrange("(k p) n -> p k n", p=P)
            for u in units:
                if not starts(turn * 2 + j):
                    sp.wait_ge(lo_ready[u % 2], split_use(turn, j, u) - 1)
                sp.dma_start(w_raw[u][:, :, :], wv[:, u * KU:u * KU + KU, bass.ds(col + j * NB, NB)]).then_inc(w_loaded[u], 16)

        def load_first(sp, w, name, units=range(4)):
            load_block(sp, w, turns[name][0], 0, 0, units)

        def load_rest(sp, w, name):
            first, n = turns[name]
            load_block(sp, w, first, 1, 0)
            with sp.Fori(1, n) as i:
                load_block(sp, w, i + first, 0, i * (2 * NB))
                load_block(sp, w, i + first, 1, i * (2 * NB))

        def round_block(act, turn, j, units=range(4)):
            for u in units:
                use = split_use(turn, j, u)
                act.wait_ge(w_loaded[u], turn * 32 + (16 * j + 16))
                if not starts(use):
                    act.wait_ge(unit_used[u % 2], use)
                nc.scalar.activation(w_hi[u % 2][:, :, :], w_raw[u][:, :, :], ACT.Copy).then_inc(hi_ready[u % 2], 1)

        def round_all(act, first, n):
            with act.Fori(0, n) as i:
                for j in range(2):
                    round_block(act, i + first, j)

        def round_and_read(act, name, read):
            first, n = turns[name]
            for b in range(2 * n):
                round_block(act, first + b // 2, b % 2, (2, 3))
                if b + 1 < 2 * n:
                    round_block(act, first + (b + 1) // 2, (b + 1) % 2, (0, 1))
                product_done(act, first + b // 2, b % 2)
                read(b, pair[b % 2]).then_inc(pair_free[b % 2], 1)

        def subtract_turn(pool, turn):
            for j in range(2):
                for u in range(4):
                    use = split_use(turn, j, u)
                    pool.wait_ge(hi_ready[u % 2], use + 1)
                    if not starts(use):
                        pool.wait_ge(unit_used[u % 2], use)
                    nc.gpsimd.tensor_tensor(w_lo[u % 2][:, :, :], w_raw[u][:, :, :], w_hi[u % 2][:, :, :], ALU.subtract).then_inc(lo_ready[u % 2], 1)

        def subtract_all(pool, name):
            first, n = turns[name]
            if first == 0:
                subtract_turn(pool, 0)
                first, n = 1, n - 1
            with pool.Fori(0, n) as i:
                subtract_turn(pool, i + first)

        def product_done(engine, turn, j):
            engine.wait_ge(unit_used[1], turn * 4 + (2 * j + 2))

        def multiply_unit(pe, turn, j, u, token):
            use = split_use(turn, j, u)
            if u == 0 and not starts(turn):
                pe.wait_ge(pair_free[j], turn)
            pe.wait_ge(hi_ready[u % 2], use + 1)
            for a, w, lo in ((act_hi, w_hi, False), (act_lo, w_hi, False), (act_hi, w_lo, True)):
                if lo:
                    pe.wait_ge(lo_ready[u % 2], use + 1)
                for part in range(2 if token else 4):
                    to = pair[j][:, part, :] if token else pair[j][:, part // 2, (part % 2) * T:(part % 2) * T + T]
                    for k in range(KU):
                        if token:
                            lhsT, rhs = a[:, u * KU + k, part * P:part * P + P], w[u % 2][:, k, :]
                        else:
                            lhsT, rhs = w[u % 2][:, k, part * P:part * P + P], a[:, u * KU + k, :]
                        clears = u == 0 and k == 0 and a is act_hi and not lo and (token or part % 2 == 0)
                        last = nc.tensor.matmul(to, lhsT, rhs, start=clears, stop=u == 3 and lo and k == KU - 1, skip_group_check=True)
            last.then_inc(unit_used[u % 2], 1)

        def multiply_block(pe, turn, j, token, units=range(4)):
            for u in units:
                multiply_unit(pe, turn, j, u, token)

        def multiply_turn(pe, turn, token):
            for j in range(2):
                multiply_block(pe, turn, j, token)

        def multiply(pe, first, n, token):
            if n == 1 or first == 0:
                multiply_turn(pe, first, token)
                first, n = first + 1, n - 1
            if n:
                with pe.Fori(0, n) as i:
                    multiply_turn(pe, i + first, token)

        def transpose_tokens(pe, src, ready, before, groups=4):
            for a in range(TT):
                pe.wait_ge(sem(ready), a + 1)
                for q in range(groups):
                    j = a * groups + q
                    if j >= 4:
                        pe.wait_ge(sem("tokens_moved"), before + j - 3)
                    for c in range(4):
                        last = nc.tensor.transpose(aux[j % 4][:, c * P:c * P + P],
                                                   src[:, a, (4 * q + c) * P:(4 * q + c) * P + P], ident)
                    last.then_inc(sem("tokens_transposed"), 1)

        def round_transposed(act, before, groups=4):
            for j in range(TT * groups):
                a, q = j // groups, j % groups
                act.wait_ge(sem("tokens_transposed"), before + j + 1)
                nc.scalar.activation(act_hi[:, 4 * q:4 * q + 4, a * P:a * P + P], aux[j % 4].rearrange("p (c t) -> p c t", c=4),
                                     ACT.Copy).then_inc(sem("tokens_rounded"), 1)

        def subtract_transposed(dve, before, groups=4):
            for j in range(TT * groups):
                a, q = j // groups, j % groups
                dve.wait_ge(sem("tokens_rounded"), before + j + 1)
                nc.vector.tensor_tensor(act_lo[:, 4 * q:4 * q + 4, a * P:a * P + P], aux[j % 4].rearrange("p (c t) -> p c t", c=4),
                                        act_hi[:, 4 * q:4 * q + 4, a * P:a * P + P], ALU.subtract).then_inc(sem("tokens_moved"), 1)

        def squares(act, src, n, ready, step=1):
            for a in range(TT):
                if ready:
                    act.wait_ge(sem(ready), step * (a + 1))
                link(act, nc.scalar.activation(aux_t[:, 0:src.shape[2] // 512, :].rearrange("p s n -> p (s n)"),
                                               src[:, a, :], ACT.Square, accum_out=stat[:, n + a:n + a + 1]))
            act.nop().then_inc(sem("squares_done"), 1)

        def roots(act, n):
            act.wait_ge(sem("mean_done"), n // 2 + 1)
            nc.scalar.activation(stat[:, 16 + n:18 + n], stat[:, n:n + 2], ACT.Sqrt).then_inc(sem("root_done"), 1)

        def reciprocal_rms(dve, n, width):
            dve.wait_ge(sem("squares_done"), n // 2 + 1)
            nc.vector.tensor_scalar(stat[:, n:n + 2], stat[:, n:n + 2], 1.0 / width, EPS, ALU.mult, ALU.add).then_inc(sem("mean_done"), 1)
            dve.wait_ge(sem("root_done"), n // 2 + 1)
            link(dve, nc.vector.reciprocal(stat[:, 32 + n:34 + n], stat[:, 16 + n:18 + n]))

        def rms_col(n, a):
            return stat[:, 32 + n + a:33 + n + a]

        decay = area(0, 8, T)
        mix_row = area(0, D)
        grT = area(2048, 8, T)
        guT = area(4096, 8, T)
        gv = area(6144, TT, LRU)
        xrp = area(8192, 8, T + 3)
        ws_raw = area(8192, 8, P)
        xcT = area(10272, 8, T)
        gates = area(12320, 2, 2, 8, P)
        ln_g = area(12320, LRU)
        ln_b = area(13344, LRU)
        bs_bc = area(14368, 8, P)
        wsT = area(15392, 8, P)
        xn = area(16416, TT, D)
        rT = area(16416, 8, T)
        iT = area(18464, 8, T)
        hsum = area(20512, 8, T)
        vecs = vec_t[:, 0:2 * P].rearrange("p (a c) -> p a c", a=2)
        lam = vec_t[:, 2 * P:2 * P + 128].rearrange("p (a c) -> p a c", a=8)

        with nc.Block() as block:
            @block.sync
            def _(sp):
                sp.dma_start(h, x[0].rearrange("(a p) d -> p a d", p=P)).then_inc(sem("x_loaded"), 16)
                sp.dma_start(mix_row, mix_norm_g.broadcast_to([P, D])).then_inc(sem("mix_row_loaded"), 16)
                load_first(sp, w_in, "in")
                load_rest(sp, w_in, "in")
                load_first(sp, w_out, "out")

            @block.gpsimd
            def _(pool):
                nc.gpsimd.memset(xrp[:, :, 0:2], 0.0).then_inc(sem("padded"), 1)
                nc.gpsimd.memset(xrp[:, :, T + 2:T + 3], 0.0).then_inc(sem("padded"), 1)
                subtract_all(pool, "in")

            @block.scalar
            def _(act):
                def load(dst, src, name):
                    act.dma_start(dst, src).then_inc(sem(name), 16)

                load(cst[:, :], constants, "cst_loaded")
                for which, row, src in (
                    (0, A_MIX, mix_norm_g[0].rearrange("(r c) -> r c", c=P)),
                    (0, A_CONVW, conv_w[0].rearrange("k (r c) -> (k r) c", c=P)),
                    (0, A_CONVB, conv_b[0].rearrange("(r c) -> r c", c=P)),
                    (0, A_BA, lru_b_a[0].rearrange("d (r c) -> (d r) c", c=P)),
                    (0, A_BX, lru_b_x[0].rearrange("d (r c) -> (d r) c", c=P)),
                    (0, A_LAM, lru_lambda[0].rearrange("d (r c) -> (d r) c", c=P)),
                    (0, A_FFN, ffn_norm_g[0].rearrange("(r c) -> r c", c=P)),
                    (1, B_LBF, lb_fwd_2.rearrange("l (r c) -> (l r) c", c=P)),
                    (1, B_LBB, lb_bwd_2.rearrange("l (r c) -> (l r) c", c=P)),
                    (1, B_PRE, g_pre_2[0].rearrange("(r c) -> r c", c=P)),
                    (1, B_HG, g_hg_2),
                ):
                    load(vecs[row:row + src.shape[0], which, :], src, "vecs_loaded")
                for g, w in ((0, lru_w_a), (1, lru_w_x)):
                    for d in range(2):
                        load(gates[:, g, d, :, :], w[0, d].rearrange("h c e -> c h e"), "gates_loaded")

                act.wait_ge(sem("x_loaded"), 16)
                squares(act, h, 0, None)
                roots(act, 0)
                act.wait_ge(sem("lam_abs"), 1)
                nc.scalar.activation(lam[:, 1, :], lam[:, 0, :], ACT.Exp).then_inc(sem("lam_exp"), 1)

                def read_product(turn, j, dst, func):
                    product_done(act, turn, j)
                    src = pair[j] if dst.shape[1] == TT else pair[j].rearrange("p b (c t) -> p (b c) t", c=2)
                    nc.scalar.activation(dst, src, func).then_inc(pair_free[j], 1)

                round_transposed(act, 0)
                round_block(act, 0, 0)
                round_block(act, 0, 1)
                act.wait_ge(sem("padded"), 2)
                read_product(0, 0, xrp[:, 0:4, 2:2 + T], ACT.Copy)
                round_block(act, 1, 0)
                read_product(0, 1, xrp[:, 4:8, 2:2 + T], ACT.Copy)
                round_block(act, 1, 1)
                read_product(1, 0, grT[:, 0:4, :], ACT.Gelu_apprx_tanh)
                round_block(act, 2, 0, (0, 1))
                read_product(1, 1, grT[:, 4:8, :], ACT.Gelu_apprx_tanh)

                def sigmoids(d):
                    for hd in range(8):
                        n = 8 * d + hd
                        act.wait_ge(sem("gate_product"), n + 1)
                        nc.scalar.activation(rT[:, hd, :], aux[hd % 4][:, 0:T], ACT.Sigmoid,
                                             bias=colsA[:, A_BA + n:A_BA + n + 1]).then_inc(sem("r_ready"), 1)
                        nc.scalar.activation(iT[:, hd, :], aux[hd % 4][:, T:2 * T], ACT.Sigmoid,
                                             bias=colsA[:, A_BX + n:A_BX + n + 1]).then_inc(sem("gate_read"), 1)
                    act.wait_ge(sem("lam_done"), 1)
                    act.wait_ge(sem("r_ready"), 8 * d + 8)
                    for hd in range(8):
                        nc.scalar.activation(rT[:, hd, :], rT[:, hd, :], ACT.Tanh,
                                             scale=lam[:, 7, 8 * d + hd:8 * d + hd + 1]).then_inc(sem("tanh_ready"), 1)

                def root_of_tanh(d):
                    act.wait_ge(sem("plus_one"), d + 1)
                    act.wait_ge(sem("tanh_ready"), 8 * d + 8)
                    nc.scalar.activation(rT, rT, ACT.Sqrt).then_inc(sem("tanh_root"), 1)

                sigmoids(0)
                round_block(act, 2, 0, (2, 3))
                root_of_tanh(0)
                round_block(act, 2, 1)
                read_product(2, 0, guT[:, 0:4, :], ACT.Gelu_apprx_tanh)
                round_block(act, 3, 0, (0, 1))
                read_product(2, 1, guT[:, 4:8, :], ACT.Gelu_apprx_tanh)
                act.wait_ge(sem("forward_done"), 1)
                sigmoids(1)
                round_block(act, 3, 0, (2, 3))
                root_of_tanh(1)
                round_block(act, 3, 1)
                load(ln_g, gmlp_ln_g.broadcast_to([P, LRU]), "ln_loaded")
                load(ln_b, gmlp_ln_b.broadcast_to([P, LRU]), "ln_loaded")
                load(bs_bc, gmlp_b_s[0:1].broadcast_to([P, 8, P]), "ln_loaded")
                load(ws_raw, gmlp_w_s[0].rearrange("h p q -> p h q"), "ws_loaded")
                read_product(3, 0, gv[:, :, 0:NB], ACT.Gelu_apprx_tanh)
                read_product(3, 1, gv[:, :, NB:2 * NB], ACT.Gelu_apprx_tanh)
                for j in range(2):
                    act.wait_ge(sem("ws_transposed"), j + 1)
                    nc.scalar.activation(wsT[:, 4 * j:4 * j + 4, :], aux[j].rearrange("p (c t) -> p c t", c=4), ACT.Copy).then_inc(sem("ws_moved"), 1)
                act.wait_ge(sem("ws_moved"), 2)
                squares(act, gv, 2, "v_centred")
                roots(act, 2)
                act.wait_ge(sem("lru_mixed"), 1)
                nc.scalar.activation(act_hi[:, 0:8, :], hsum, ACT.Copy).then_inc(sem("mix_rounded"), 1)
                for j in range(4):
                    act.wait_ge(sem("gmlp_mixed"), j + 1)
                    nc.scalar.activation(act_hi[:, 8 + 2 * j:10 + 2 * j, :], guT[:, 2 * j:2 * j + 2, :], ACT.Copy).then_inc(sem("mix_rounded"), 1)

            @block.vector
            def _(dve):
                def step(instruction):
                    link(dve, instruction)

                dve.wait_ge(sem("vecs_transposed"), 1)
                step(nc.vector.tensor_copy(colsA[:, :], aux[0][:, 0:A_ROWS]))
                step(nc.vector.tensor_copy(colsB[:, :], aux[1][:, 0:B_ROWS]))
                dve.nop().then_inc(sem("cols_ready"), 1)
                lam0 = colsA[:, A_LAM:A_LAM + 16]
                step(nc.vector.tensor_scalar(lam[:, 2, :], lam0, -1.0, None, ALU.mult))
                nc.vector.tensor_tensor(lam[:, 0, :], lam0, lam[:, 2, :], ALU.min).then_inc(sem("lam_abs"), 1)
                reciprocal_rms(dve, 0, D)
                dve.wait_ge(sem("mix_row_loaded"), 16)
                for a in range(TT):
                    nc.vector.scalar_tensor_tensor(xn[:, a, :], h[:, a, :], rms_col(0, a), mix_row, ALU.mult, ALU.mult).then_inc(sem("n1_ready"), 1)
                subtract_transposed(dve, 0)
                dve.wait_ge(sem("lam_exp"), 1)
                step(nc.vector.tensor_scalar(lam[:, 3, :], lam[:, 1, :], 2.0, None, ALU.add))
                step(nc.vector.reciprocal(lam[:, 3, :], lam[:, 3, :]))
                step(nc.vector.tensor_tensor(lam[:, 3, :], lam[:, 3, :], lam[:, 1, :], ALU.mult))
                step(nc.vector.tensor_tensor(lam[:, 4, :], lam[:, 3, :], lam[:, 3, :], ALU.mult))
                step(nc.vector.memset(lam[:, 5, :], 1.0 / 19))
                for n in range(17, 0, -2):
                    step(nc.vector.tensor_tensor(lam[:, 5, :], lam[:, 5, :], lam[:, 4, :], ALU.mult))
                    step(nc.vector.tensor_scalar(lam[:, 5, :], lam[:, 5, :], 1.0 / n, None, ALU.add))
                step(nc.vector.tensor_tensor(lam[:, 5, :], lam[:, 5, :], lam[:, 3, :], ALU.mult))
                step(nc.vector.tensor_scalar(lam[:, 2, :], lam[:, 2, :], 0.0, None, ALU.max))
                step(nc.vector.scalar_tensor_tensor(lam[:, 6, :], lam[:, 5, :], 2.0, lam[:, 2, :], ALU.mult, ALU.add))
                nc.vector.tensor_scalar(lam[:, 7, :], lam[:, 6, :], LRU_C / 2, None, ALU.mult).then_inc(sem("lam_done"), 1)

                for c in range(8):
                    dve.wait_ge(pair_free[c // 4], 1)
                    step(nc.vector.tensor_scalar(xcT[:, c, :], xrp[:, c, 0:T], colsA[:, A_CONVW + c:A_CONVW + c + 1],
                                                 colsA[:, A_CONVB + c:A_CONVB + c + 1], ALU.mult, ALU.add))
                    for k in (1, 2, 3):
                        tap = nc.vector.scalar_tensor_tensor(xcT[:, c, :], xrp[:, c, k:k + T],
                                                             colsA[:, A_CONVW + 8 * k + c:A_CONVW + 8 * k + c + 1],
                                                             xcT[:, c, :], ALU.mult, ALU.add)
                        if k < 3:
                            step(tap)
                    tap.then_inc(sem("conv_done"), 1)

                for d in range(2):
                    dve.wait_ge(sem("tanh_ready"), 8 * d + 8)
                    nc.vector.tensor_scalar(decay, rT, 1.0, None, ALU.add).then_inc(sem("plus_one"), 1)
                    dve.wait_ge(sem("plus_one"), d + 1)
                    step(nc.vector.reciprocal(decay, decay))
                    dve.wait_ge(sem("tanh_root"), d + 1)
                    step(nc.vector.scalar_tensor_tensor(rT, decay, 2.0, rT, ALU.mult, ALU.mult))
                    step(nc.vector.tensor_scalar(decay, decay, 2.0, -1.0, ALU.mult, ALU.add))
                    dve.wait_ge(sem("gate_read"), 8 * d + 8)
                    step(nc.vector.tensor_tensor(rT, rT, iT, ALU.mult))
                    step(nc.vector.tensor_tensor(rT, rT, xcT, ALU.mult))
                    to = iT if d else hsum
                    way = slice(None, None, -1) if d else slice(None)
                    for hd in range(8):
                        step(nc.vector.tensor_tensor_scan(to[:, hd, way], decay[:, hd, way], rT[:, hd, way], 0.0, ALU.mult, ALU.add))
                    if d == 0:
                        dve.nop().then_inc(sem("forward_done"), 1)
                step(nc.vector.tensor_tensor(hsum, hsum, iT, ALU.add))
                for j in range(2):
                    dve.wait_ge(pair_free[j], 2)
                nc.vector.tensor_tensor(hsum, hsum, grT, ALU.mult).then_inc(sem("lru_mixed"), 1)

                for j in range(2):
                    dve.wait_ge(pair_free[j], 4)
                for a in range(TT):
                    step(nc.vector.tensor_reduce(stat[:, 60 + a:61 + a], gv[:, a, :], AX_X, ALU.add))
                    step(nc.vector.tensor_scalar(stat[:, 62 + a:63 + a], stat[:, 60 + a:61 + a], -1.0 / LRU, None, ALU.mult))
                    nc.vector.tensor_scalar(gv[:, a, :], gv[:, a, :], stat[:, 62 + a:63 + a], None, ALU.add).then_inc(sem("v_centred"), 1)
                reciprocal_rms(dve, 2, LRU)
                dve.wait_ge(sem("ln_loaded"), 48)
                for a in range(TT):
                    step(nc.vector.scalar_tensor_tensor(gv[:, a, :], gv[:, a, :], rms_col(2, a), ln_g, ALU.mult, ALU.mult))
                    nc.vector.tensor_tensor(gv[:, a, :], gv[:, a, :], ln_b, ALU.add).then_inc(sem("v_ready"), 1)
                dve.wait_ge(sem("mix_rounded"), 1)
                step(nc.vector.tensor_tensor(act_lo[:, 0:8, :], hsum, act_hi[:, 0:8, :], ALU.subtract))
                for j in range(4):
                    dve.wait_ge(sem("mixed"), j + 1)
                    g = guT[:, 2 * j:2 * j + 2, :]
                    step(nc.vector.tensor_tensor(aux[j].rearrange("p (h n t) -> p h n t", h=2, n=2),
                                                 aux[j].rearrange("p (h n t) -> p h n t", h=2, n=2),
                                                 bs_bc[:, 2 * j:2 * j + 2, :].unsqueeze(2).broadcast_to([P, 2, 2, P]), ALU.add))
                    nc.vector.tensor_tensor(g, g, aux[j].rearrange("p (h t) -> p h t", h=2), ALU.mult).then_inc(sem("gmlp_mixed"), 1)
                for j in range(4):
                    dve.wait_ge(sem("mix_rounded"), j + 2)
                    step(nc.vector.tensor_tensor(act_lo[:, 8 + 2 * j:10 + 2 * j, :], guT[:, 2 * j:2 * j + 2, :],
                                                 act_hi[:, 8 + 2 * j:10 + 2 * j, :], ALU.subtract))

            @block.tensor
            def _(pe):
                pe.wait_ge(sem("cst_loaded"), 16)
                pe.wait_ge(sem("vecs_loaded"), 16 * 11)
                pe.wait_ge(sem("squares_done"), 1)
                nc.tensor.transpose(aux[0][:, 0:A_ROWS], vecs[0:A_ROWS, 0, :], ident[0:A_ROWS, 0:A_ROWS])
                nc.tensor.transpose(aux[1][:, 0:B_ROWS], vecs[0:B_ROWS, 1, :], ident[0:B_ROWS, 0:B_ROWS]).then_inc(sem("vecs_transposed"), 1)
                pe.wait_ge(sem("cols_ready"), 1)
                transpose_tokens(pe, xn, "n1_ready", 0)
                pe.wait_ge(sem("tokens_moved"), 8)
                multiply(pe, 0, 2, False)
                pe.wait_ge(sem("gates_loaded"), 64)

                def gate_products(d):
                    for hd in range(8):
                        n = 8 * d + hd
                        pe.wait_ge(sem("conv_done"), hd + 1 if d == 0 else 8)
                        if n >= 4:
                            pe.wait_ge(sem("gate_read"), n - 3)
                        nc.tensor.matmul(aux[hd % 4][:, 0:T], gates[:, 0, d, hd, :], xcT[:, hd, :], start=True, stop=True)
                        nc.tensor.matmul(aux[hd % 4][:, T:2 * T], gates[:, 1, d, hd, :], xcT[:, hd, :], start=True, stop=True).then_inc(sem("gate_product"), 1)

                gate_products(0)
                multiply(pe, 2, 1, False)
                gate_products(1)
                multiply(pe, 3, 1, True)
                pe.wait_ge(sem("ws_loaded"), 16)
                pe.wait_ge(sem("gate_read"), 16)
                for hd in range(8):
                    last = nc.tensor.transpose(aux[hd // 4][:, (hd % 4) * P:(hd % 4) * P + P], ws_raw[:, hd, :], ident)
                    if hd % 4 == 3:
                        last.then_inc(sem("ws_transposed"), 1)
                pe.wait_ge(sem("ws_moved"), 2)
                pe.wait_ge(sem("v_ready"), 2)
                for hd in range(8):
                    for n in range(TT):
                        at = (2 * (hd % 2) + n) * P
                        last = nc.tensor.matmul(aux[hd // 2][:, at:at + P], gv[:, n, hd * P:hd * P + P], wsT[:, hd, :],
                                                start=True, stop=True)
                    if hd % 2:
                        last.then_inc(sem("mixed"), 1)

        n2 = area(0, TT, D)
        q_block = [area(4096 + 4 * T * s, 4, T) for s in range(2)]
        skT = area(6144, 16, KEYS)
        sk_raw = area(8192, 16, P)
        scores_0 = [area(10240 + 4 * KEYS * s, 4, KEYS) for s in range(2)]
        ffn_row = area(12288, D)
        scores_1 = area(16384, 16, KEYS)
        cand = area(18432, TOPK, TOPK)
        hot = area(18688, TOPK, TOPK)
        top_s = area(18944, 2, TOPK)
        top_i = area(18976, 2, TOPK, dtype=U32)
        top_f = area(19008, 2, TOPK)
        pos = area(19040, TOPK, dtype=U32)
        pos_part = area(19056, TOPK, dtype=U32)
        pos_f = area(19072, TOPK)
        chosen = area(19088, 2, TOPK)
        gate_w = area(20480, TT, SLOTS)
        ids = area(20736, TT, SLOTS, dtype=I32)
        best = area(20992, HEADS, TOPK)
        total = area(21120, HEADS)

        def top16(step, values, index, source):
            step(nc.vector.max(values[:, 0:8], source))
            step(nc.vector.max_index(index[:, 0:8], values[:, 0:8], source))
            step(nc.vector.match_replace(source, values[:, 0:8], source, LOWEST))
            step(nc.vector.max(values[:, 8:16], source))
            step(nc.vector.max_index(index[:, 8:16], values[:, 8:16], source))

        def route(step, a, hd, score):
            for g in range(2):
                top16(step, top_s[:, g, :], top_i[:, g, :], score[:, g, :])
            step(nc.vector.tensor_copy(top_f, top_i))
            step(nc.vector.tensor_tensor(cand, top_s[:, 0, :].unsqueeze(2).broadcast_to([P, TOPK, TOPK]),
                                         top_s[:, 1, :].unsqueeze(1).broadcast_to([P, TOPK, TOPK]), ALU.add))
            top16(step, best[:, hd, :], pos, cand.rearrange("p a b -> p (a b)"))
            for part in range(2):
                if part == 0:
                    step(nc.vector.tensor_scalar(pos_part, pos, 4, None, ALU.logical_shift_right))
                else:
                    step(nc.vector.tensor_scalar(pos_part, pos, 15, None, ALU.bitwise_and))
                step(nc.vector.tensor_copy(pos_f, pos_part))
                iota = cst[:, C_IOTA:C_IOTA + TOPK].unsqueeze(1).broadcast_to([P, TOPK, TOPK])
                step(nc.vector.tensor_tensor(hot, iota, pos_f.unsqueeze(2).broadcast_to([P, TOPK, TOPK]), ALU.is_equal))
                step(nc.vector.tensor_tensor(hot, hot, top_f[:, part, :].unsqueeze(1).broadcast_to([P, TOPK, TOPK]), ALU.mult))
                step(nc.vector.tensor_reduce(chosen[:, part, :], hot, AX_X, ALU.add))
            step(nc.vector.scalar_tensor_tensor(ids[:, a, TOPK * hd:TOPK * hd + TOPK], chosen[:, 0, :], float(KEYS),
                                                chosen[:, 1, :], ALU.mult, ALU.add))

        def soften(dve, step, a):
            step(nc.vector.tensor_copy(total, best[:, :, 0]))
            nc.vector.tensor_tensor(best, best, total.unsqueeze(2).broadcast_to([P, HEADS, TOPK]), ALU.subtract).then_inc(sem("soft_shifted"), 1)
            dve.wait_ge(sem("soft_exp"), a + 1)
            step(nc.vector.tensor_reduce(total, best, AX_X, ALU.add))
            step(nc.vector.reciprocal(total, total))
            nc.vector.tensor_tensor(gate_w[:, a, :].rearrange("p (h j) -> p h j", h=HEADS), best,
                                    total.unsqueeze(2).broadcast_to([P, HEADS, TOPK]), ALU.mult).then_inc(sem("routed"), 1)
            dve.wait_ge(sem("routed"), a + 1)

        def soften_exp(act, a):
            act.wait_ge(sem("soft_shifted"), a + 1)
            nc.scalar.activation(best, best, ACT.Exp).then_inc(sem("soft_exp"), 1)

        with nc.Block() as block:
            @block.sync
            def _(sp):
                sp.dma_start(ffn_row, ffn_norm_g[0:1, :].broadcast_to([P, D])).then_inc(sem("ffn_row_loaded"), 16)
                sp.dma_start(sk_raw, peer_sub_keys[0].rearrange("h s n k -> n (h s) k")).then_inc(sem("sk_loaded"), 16)
                load_rest(sp, w_out, "out")
                load_first(sp, peer_w_q, "q")
                load_rest(sp, peer_w_q, "q")
                load_first(sp, w_in_2, "in2", (0, 1))

            @block.gpsimd
            def _(pool):
                subtract_all(pool, "out")
                subtract_all(pool, "q")

            @block.scalar
            def _(act):
                first, n = turns["q"]
                round_block(act, turns["out"][0], 0)
                for j in range(4):
                    act.wait_ge(sem("sk_transposed"), j + 1)
                    nc.scalar.activation(skT[:, 4 * j:4 * j + 4, :], aux[j].rearrange("p (c t) -> p c t", c=4), ACT.Copy).then_inc(sem("sk_moved"), 1)
                act.wait_ge(sem("sk_moved"), 4)
                round_block(act, turns["out"][0], 1)
                round_all(act, turns["out"][0] + 1, turns["out"][1] - 1)
                round_block(act, first, 0, (0, 1))
                for j in range(2):
                    act.wait_ge(pair_free[j], sum(turns["out"]))
                squares(act, h, 4, None)
                roots(act, 4)
                round_transposed(act, 8)
                for b in range(2 * n):
                    turn, j = first + b // 2, b % 2
                    round_block(act, turn, j, (2, 3))
                    if b + 1 < 2 * n:
                        round_block(act, first + (b + 1) // 2, (b + 1) % 2, (0, 1))
                    product_done(act, turn, j)
                    if b >= 2:
                        act.wait_ge(sem("score_product"), 2 * (b - 1))
                    nc.scalar.activation(q_block[b % 2], pair[j].rearrange("p b (c t) -> p (b c) t", c=2), ACT.Copy).then_inc(pair_free[j], 1)
                    for a in range(TT):
                        act.wait_ge(sem("score_product"), TT * b + a + 1)
                        if a == 0 and b >= 2:
                            act.wait_ge(sem("searched"), b - 1)
                        dst = scores_1[:, 4 * b:4 * b + 4, :] if a else scores_0[b % 2]
                        nc.scalar.activation(dst, aux[TT * (b % 2) + a].rearrange("p (c t) -> p c t", c=4), ACT.Copy).then_inc(sem("scores_moved"), 1)
                soften_exp(act, 0)

            @block.vector
            def _(dve):
                def step(instruction):
                    link(dve, instruction)

                first, n = turns["out"]
                for b in range(2 * n):
                    turn, j = first + b // 2, b % 2
                    product_done(dve, turn, j)
                    nc.vector.tensor_tensor(h[:, :, b * NB:b * NB + NB], h[:, :, b * NB:b * NB + NB], pair[j], ALU.add).then_inc(pair_free[j], 1)
                reciprocal_rms(dve, 4, D)
                dve.wait_ge(sem("ffn_row_loaded"), 16)
                for a in range(TT):
                    nc.vector.scalar_tensor_tensor(n2[:, a, :], h[:, a, :], rms_col(4, a), ffn_row, ALU.mult, ALU.mult).then_inc(sem("n2_ready"), 1)
                subtract_transposed(dve, 8)
                for b in range(2 * turns["q"][1]):
                    dve.wait_ge(sem("scores_moved"), TT * b + 1)
                    for hd in range(2):
                        route(step, 0, 2 * b + hd, scores_0[b % 2][:, 2 * hd:2 * hd + 2, :])
                    dve.nop().then_inc(sem("searched"), 1)
                soften(dve, step, 0)

            @block.tensor
            def _(pe):
                pe.wait_ge(sem("sk_loaded"), 16)
                for g in range(16):
                    last = nc.tensor.transpose(aux[g // 4][:, (g % 4) * P:(g % 4) * P + P], sk_raw[:, g, :], ident)
                    if g % 4 == 3:
                        last.then_inc(sem("sk_transposed"), 1)
                multiply(pe, *turns["out"], True)
                pe.wait_ge(sem("squares_done"), 3)
                transpose_tokens(pe, n2, "n2_ready", 8)
                pe.wait_ge(sem("tokens_moved"), 16)
                first, n = turns["q"]

                def score(b):
                    pe.wait_ge(pair_free[b % 2], first + b // 2 + 1)
                    for a in range(TT):
                        if b >= 2:
                            pe.wait_ge(sem("scores_moved"), TT * (b - 2) + a + 1)
                        for c in range(4):
                            last = nc.tensor.matmul(aux[TT * (b % 2) + a][:, c * KEYS:c * KEYS + KEYS], q_block[b % 2][:, c, a * P:a * P + P],
                                                    skT[:, 4 * b + c, :], start=True, stop=True)
                        last.then_inc(sem("score_product"), 1)

                for b in range(2 * n):
                    turn, j = first + b // 2, b % 2
                    multiply_block(pe, turn, j, False, (0, 1))
                    if b:
                        score(b - 1)
                    multiply_block(pe, turn, j, False, (2, 3))
                score(2 * n - 1)

        staged = area(21128, 4, dtype=I32)
        dots = area(21132, 4)
        gelud = area(21136, 4)
        diag = area(21140, 4, P)
        ubuf = [area(4096 + D * s, D) for s in range(4)]
        vbuf = [area(12288 + D * s, D) for s in range(2)] + [w_raw[s][:, :, :].rearrange("p k n -> p (k n)") for s in (2, 3)]
        products = bank_t[:, :, :].rearrange("p s n -> p (s n)")
        u_loaded = [sem(f"u_loaded{s}") for s in range(4)]
        v_loaded = [sem(f"v_loaded{s}") for s in range(4)]
        staged_s = [sem(f"staged{s}") for s in range(4)]
        dot_done = [sem(f"dot_done{s}") for s in range(4)]
        gelu_done = [sem(f"gelu_done{s}") for s in range(4)]
        diag_done = [sem(f"diag_done{s}") for s in range(4)]
        v_used = [sem(f"v_used{s}") for s in range(4)]
        ROUNDS = SLOTS // 4
        with nc.Block() as block:
            @block.gpsimd
            def _(pool):
                def gather(a, i, use):
                    for s in range(4):
                        if not starts(use):
                            pool.wait_ge(dot_done[s], use)
                            pool.wait_ge(v_used[s], use)
                        nc.gpsimd.tensor_copy(staged[:, s:s + 1], ids[:, a, bass.ds(i * 4 + s, 1)]).then_inc(staged_s[s], 1)
                        pool.wait_ge(staged_s[s], use + 1)
                        pool.nop(nofuse=True)
                        at = bass.IndirectOffsetOnAxis(ap=staged[:, s:s + 1], axis=0)
                        nc.gpsimd.indirect_dma_start(ubuf[s], None, peer_u[0], at).then_inc(u_loaded[s], 16)
                        nc.gpsimd.indirect_dma_start(vbuf[s], None, peer_v[0], at).then_inc(v_loaded[s], 16)

                gather(0, 0, 0)
                for a in range(TT):
                    if a:
                        pool.wait_ge(sem("routed"), TT)
                    with pool.Fori(1 - a, ROUNDS) as i:
                        gather(a, i, i + a * ROUNDS)

            @block.vector
            def _(dve):
                def weigh(a, i, s, use):
                    dve.wait_ge(gelu_done[s], use + 1)
                    if not starts(use):
                        dve.wait_ge(v_used[s], use)
                    nc.vector.tensor_scalar(diag[:, s, :], ident, gelud[:, s:s + 1], gate_w[:, a, bass.ds(i * 4 + s, 1)],
                                            ALU.mult, ALU.mult).then_inc(diag_done[s], 1)

                def round_of(a, i, use):
                    for s in range(4):
                        dve.wait_ge(u_loaded[s], use * 16 + 16)
                        if s or not starts(use):
                            dve.wait_ge(dot_done[s - 1], use + 1 if s else use)
                        if not starts(use):
                            dve.wait_ge(gelu_done[s], use)
                        nc.vector.scalar_tensor_tensor(products, ubuf[s], 1.0, n2[:, a, :], ALU.mult, ALU.mult,
                                                       accum_out=dots[:, s:s + 1]).then_inc(dot_done[s], 1)
                        if s:
                            weigh(a, i, s - 1, use)
                    weigh(a, i, 3, use)

                def step(instruction):
                    link(dve, instruction)

                for hd in range(HEADS):
                    round_of(0, hd, hd)
                    route(step, 1, hd, scores_1[:, 2 * hd:2 * hd + 2, :])
                soften(dve, step, 1)
                for a in range(TT):
                    with dve.Fori(0 if a else HEADS, ROUNDS) as i:
                        round_of(a, i, i + a * ROUNDS)
                    for s in range(4):
                        dve.wait_ge(v_used[s], (a + 1) * ROUNDS)
                    nc.vector.tensor_tensor(h[:, a, :], h[:, a, :], aux_t[:, :, :].rearrange("p s n -> p (s n)"), ALU.add).then_inc(sem("peer_added"), 1)

            @block.scalar
            def _(act):
                def gelus(use):
                    for s in range(4):
                        act.wait_ge(dot_done[s], use + 1)
                        if not starts(use):
                            act.wait_ge(diag_done[s], use)
                        nc.scalar.activation(gelud[:, s:s + 1], dots[:, s:s + 1], ACT.Gelu_apprx_tanh).then_inc(gelu_done[s], 1)

                for i in range(HEADS):
                    gelus(i)
                soften_exp(act, 1)
                with act.Fori(HEADS, TT * ROUNDS) as i:
                    gelus(i)

            @block.tensor
            def _(pe):
                def accumulate(use, s, start, stop):
                    pe.wait_ge(v_loaded[s], use * 16 + 16)
                    pe.wait_ge(diag_done[s], use + 1)
                    for q in range(4):
                        last = nc.tensor.matmul(aux[q], diag[:, s, :], vbuf[s][:, q * 512:q * 512 + 512], start=start, stop=stop)
                    last.then_inc(v_used[s], 1)

                for a in range(TT):
                    if a:
                        pe.wait_ge(sem("peer_added"), a)
                    for s in range(4):
                        accumulate(a * ROUNDS, s, s == 0, False)
                    with pe.Fori(1, ROUNDS - 1) as i:
                        for s in range(4):
                            accumulate(i + a * ROUNDS, s, False, False)
                    for s in range(4):
                        accumulate((a + 1) * ROUNDS - 1, s, False, s == 3)

        aq = area(0, TT, 16, 64)
        ak = area(2048, TT, 16, 64)
        av = area(4096, TT, 1024)
        ag = area(6144, TT, 1024)
        hqT = area(8192, 8, T)
        fT = [area(10240, 8, T), area(12288, 8, T)]
        hv = area(14336, TT, 1024)
        hgT = area(16384, 8, T)
        un = area(8192, TT, D)
        final_row = area(18432, D)
        pre_row = area(20480, D)
        turned = area(18432, 4, TT, 16, ROT)
        angle = area(22528, 5, TT * ROT)
        cos_t = area(22608, TT, ROT)
        sin_t = area(22624, TT, ROT)
        pos_i = area(22640, TT, dtype=I32)
        pos_x = area(22642, TT)
        lb = vec_t[:, 0:16]
        one_minus_lb = vec_t[:, 16:32]
        with nc.Block() as block:
            @block.sync
            def _(sp):
                sp.dma_start(final_row, final_norm_g.rearrange("(a d) -> a d", a=1).broadcast_to([P, D])).then_inc(sem("final_row_loaded"), 16)
                sp.dma_start(pre_row, g_pre_2.broadcast_to([P, D])).then_inc(sem("pre_row_loaded"), 16)
                load_block(sp, w_in_2, turns["in2"][0], 0, 0, (2, 3))
                load_rest(sp, w_in_2, "in2")
                load_first(sp, w_out_2, "out2")

            @block.gpsimd
            def _(pool):
                with nc.allow_non_contiguous_dma(reason="256 positions"):
                    pool.dma_start(pos_i, positions_2[0].rearrange("(a p) -> p a", p=P)).then_inc(sem("positions_loaded"), 16)
                subtract_all(pool, "in2")

            @block.scalar
            def _(act):
                squares(act, h, 6, None)
                roots(act, 6)
                squares(act, h, 8, "h3_ready")
                roots(act, 8)
                round_block(act, turns["in2"][0], 0, (0, 1))
                round_transposed(act, 16)
                act.wait_ge(sem("lb_ready"), 1)
                nc.scalar.activation(lb, lb, ACT.Sigmoid).then_inc(sem("lb_done"), 1)
                act.wait_ge(sem("angle_ready"), 1)
                nc.scalar.activation(sin_t.rearrange("p a e -> p (a e)"), angle[:, 2, :], ACT.Sin).then_inc(sem("trig_ready"), 1)
                nc.scalar.activation(cos_t.rearrange("p a e -> p (a e)"), angle[:, 3, :], ACT.Sin).then_inc(sem("trig_ready"), 1)
                groups = (
                    (aq.rearrange("p a h e -> p a (h e)"), ACT.Copy, True), (ak.rearrange("p a h e -> p a (h e)"), ACT.Copy, True),
                    (av, ACT.Copy, True), (ag, ACT.Silu, True), (hqT, ACT.Silu, False), (fT[0], ACT.Sigmoid, False),
                    (fT[1], ACT.Sigmoid, False), (hv, ACT.Copy, True), (hgT, ACT.Silu, False),
                )

                def read(b, product):
                    dst, func, token = groups[b // 2]
                    if token:
                        return nc.scalar.activation(dst[:, :, (b % 2) * NB:(b % 2) * NB + NB], product, func)
                    return nc.scalar.activation(dst[:, 4 * (b % 2):4 * (b % 2) + 4, :], product.rearrange("p b (c t) -> p (b c) t", c=2), func)

                round_and_read(act, "in2", read)

            @block.vector
            def _(dve):
                def step(instruction):
                    link(dve, instruction)

                reciprocal_rms(dve, 6, D)
                dve.wait_ge(sem("final_row_loaded"), 16)
                for a in range(TT):
                    nc.vector.scalar_tensor_tensor(h[:, a, :], h[:, a, :], rms_col(6, a), final_row, ALU.mult, ALU.mult).then_inc(sem("h3_ready"), 1)
                reciprocal_rms(dve, 8, D)
                dve.wait_ge(sem("h3_ready"), 2)
                dve.wait_ge(sem("pre_row_loaded"), 16)
                for a in range(TT):
                    nc.vector.scalar_tensor_tensor(un[:, a, :], h[:, a, :], rms_col(8, a), pre_row, ALU.mult, ALU.mult).then_inc(sem("un_ready"), 1)
                subtract_transposed(dve, 16)
                step(nc.vector.tensor_tensor(lb[:, 0:8], colsB[:, B_LBF:B_LBF + 8], colsB[:, B_LBF + 8:B_LBF + 16], ALU.subtract))
                nc.vector.tensor_tensor(lb[:, 8:16], colsB[:, B_LBB:B_LBB + 8], colsB[:, B_LBB + 8:B_LBB + 16], ALU.subtract).then_inc(sem("lb_ready"), 1)
                dve.wait_ge(sem("lb_done"), 1)
                step(nc.vector.tensor_scalar(one_minus_lb, lb, -1.0, 1.0, ALU.mult, ALU.add))
                dve.wait_ge(sem("positions_loaded"), 16)
                step(nc.vector.tensor_copy(pos_x, pos_i))
                inv = cst[:, C_INV:C_INV + ROT].unsqueeze(1).broadcast_to([P, TT, ROT])
                step(nc.vector.tensor_tensor(angle[:, 0, :].rearrange("p (a e) -> p a e", a=TT), inv,
                                             pos_x.unsqueeze(2).broadcast_to([P, TT, ROT]), ALU.mult))
                step(nc.vector.tensor_scalar(angle[:, 1, :], angle[:, 0, :], 1.0 / TWO_PI, ROUNDER, ALU.mult, ALU.add))
                step(nc.vector.tensor_scalar(angle[:, 1, :], angle[:, 1, :], -ROUNDER, None, ALU.add))
                step(nc.vector.scalar_tensor_tensor(angle[:, 2, :], angle[:, 1, :], -TURN_PARTS[0], angle[:, 0, :], ALU.mult, ALU.add))
                step(nc.vector.scalar_tensor_tensor(angle[:, 2, :], angle[:, 1, :], -TURN_PARTS[1], angle[:, 2, :], ALU.mult, ALU.add))
                step(nc.vector.scalar_tensor_tensor(angle[:, 2, :], angle[:, 1, :], -TURN_PARTS[2], angle[:, 2, :], ALU.mult, ALU.add))
                step(nc.vector.tensor_scalar(angle[:, 2, :], angle[:, 2, :], 3.1415925, -3.1415925, ALU.min, ALU.max))
                step(nc.vector.tensor_scalar(angle[:, 4, :], angle[:, 2, :], -1.0, None, ALU.mult))
                step(nc.vector.tensor_tensor(angle[:, 3, :], angle[:, 4, :], angle[:, 2, :], ALU.min))
                nc.vector.tensor_scalar(angle[:, 3, :], angle[:, 3, :], float(np.pi / 2), None, ALU.add).then_inc(sem("angle_ready"), 1)
                dve.wait_ge(sem("trig_ready"), 2)
                c = cos_t.unsqueeze(2).broadcast_to([P, TT, 16, ROT])
                sn = sin_t.unsqueeze(2).broadcast_to([P, TT, 16, ROT])
                for n, t in enumerate((aq, ak)):
                    for j in range(2):
                        dve.wait_ge(pair_free[j], turns["in2"][0] + n + 1)
                    x1, x2 = t[:, :, :, 0:ROT], t[:, :, :, ROT:2 * ROT]
                    for m, (u, v) in enumerate(((x1, c), (x2, sn), (x2, c), (x1, sn))):
                        step(nc.vector.tensor_tensor(turned[:, m], u, v, ALU.mult))
                    step(nc.vector.tensor_tensor(x1, turned[:, 0], turned[:, 1], ALU.subtract))
                    step(nc.vector.tensor_tensor(x2, turned[:, 2], turned[:, 3], ALU.add))

            @block.tensor
            def _(pe):
                transpose_tokens(pe, un, "un_ready", 16)
                pe.wait_ge(sem("tokens_moved"), 24)
                first, _ = turns["in2"]
                multiply(pe, first, 4, True)
                multiply(pe, first + 4, 3, False)
                multiply(pe, first + 7, 1, True)
                multiply(pe, first + 8, 1, False)

        aqT = area(18432, 8, T)
        akT = area(20480, 8, T)
        probs = [area(2048 + 512 * s, TT, T) for s in range(2)]
        probsT = [area(3072 + 512 * s, TT, T) for s in range(2)]
        asum = area(22528, 16, TT)
        amax = area(22560, 16, TT)
        arec = area(22592, 16, TT)
        att_o = aq
        att_bias = cst[:, C_BIAS:C_BIAS + TT * T].rearrange("p (a t) -> p a t", a=TT)
        ATT_SCALE = 64 ** -0.5
        with nc.Block() as block:
            @block.scalar
            def _(act):
                for j in range(8):
                    act.wait_ge(sem("qk_transposed"), j + 1)
                    half, a = j % 2, (j // 2) % 2
                    dst = (aqT if j < 4 else akT)[:, 4 * half:4 * half + 4, a * P:a * P + P]
                    nc.scalar.activation(dst, aux[j % 4].rearrange("p (c t) -> p c t", c=4), ACT.Copy,
                                         scale=ATT_SCALE if j < 4 else 1.0).then_inc(sem("qk_moved"), 1)
                for i in range(17):
                    if i < 16:
                        act.wait_ge(sem("att_max"), i + 1)
                        for a in range(TT):
                            nc.scalar.activation(probs[i % 2][:, a, :], probs[i % 2][:, a, :], ACT.Exp, bias=amax[:, i, a:a + 1],
                                                 accum_out=asum[:, i, a:a + 1]).then_inc(sem("probs_ready"), 1)
                    if i >= 1:
                        hd = i - 1
                        act.wait_ge(sem("probs_transposed"), hd + 1)
                        if hd >= 2:
                            act.wait_ge(sem("att_product"), hd - 1)
                        nc.scalar.activation(probsT[hd % 2], bank[2 + hd % 2][:, :].rearrange("p (c t) -> p c t", c=2),
                                             ACT.Copy).then_inc(sem("probs_moved"), 1)
                round_transposed(act, 24, groups=2)

            @block.vector
            def _(dve):
                def step(instruction):
                    link(dve, instruction)

                for i in range(18):
                    if i < 16:
                        dve.wait_ge(sem("att_scores"), i + 1)
                        if i >= 2:
                            dve.wait_ge(sem("probs_transposed"), i - 1)
                        nc.vector.tensor_tensor(probs[i % 2], bank[i % 2][:, :].rearrange("p (a t) -> p a t", a=TT), att_bias,
                                                ALU.add).then_inc(sem("logits_ready"), 1)
                        dve.wait_ge(sem("logits_ready"), i + 1)
                        nc.vector.tensor_reduce(amax[:, i, :], probs[i % 2], AX_X, ALU.max, negate=True).then_inc(sem("att_max"), 1)
                    if i >= 2:
                        hd = i - 2
                        dve.wait_ge(sem("att_product"), hd + 1)
                        step(nc.vector.reciprocal(arec[:, hd, :], asum[:, hd, :]))
                        nc.vector.tensor_tensor(att_o[:, :, hd, :], aux[hd % 4][:, 0:P].rearrange("p (a e) -> p a e", a=TT),
                                                arec[:, hd, :].unsqueeze(2).broadcast_to([P, TT, 64]), ALU.mult).then_inc(sem("att_moved"), 1)
                dve.wait_ge(sem("att_moved"), 16)
                for a in range(TT):
                    o = att_o[:, a].rearrange("p h e -> p (h e)")
                    nc.vector.tensor_tensor(o, o, ag[:, a, :], ALU.mult).then_inc(sem("yatt_ready"), 1)
                subtract_transposed(dve, 24, groups=2)

            @block.tensor
            def _(pe):
                for j in range(8):
                    half, a = j % 2, (j // 2) % 2
                    if j >= 4:
                        pe.wait_ge(sem("qk_moved"), j - 3)
                    src = (aq if j < 4 else ak).rearrange("p a h e -> p a (h e)")
                    for c in range(4):
                        last = nc.tensor.transpose(aux[j % 4][:, c * P:c * P + P], src[:, a, (4 * half + c) * P:(4 * half + c) * P + P], ident)
                    last.then_inc(sem("qk_transposed"), 1)
                pe.wait_ge(sem("qk_moved"), 8)
                for i in range(18):
                    if i < 16:
                        lo, c = 64 * (i % 2), i // 2
                        if i >= 2:
                            pe.wait_ge(sem("logits_ready"), i - 1)
                        for a in range(TT):
                            last = nc.tensor.matmul(bank[i % 2][:, a * T:a * T + T], aqT[lo:lo + 64, c, a * P:a * P + P],
                                                    akT[lo:lo + 64, c, :], start=True, stop=True)
                        last.then_inc(sem("att_scores"), 1)
                    if 1 <= i <= 16:
                        hd = i - 1
                        pe.wait_ge(sem("probs_ready"), 2 * hd + 2)
                        if hd >= 2:
                            pe.wait_ge(sem("probs_moved"), hd - 1)
                        for k in range(TT):
                            for a in range(TT):
                                at = k * T + a * P
                                last = nc.tensor.transpose(bank[2 + hd % 2][:, at:at + P], probs[hd % 2][:, a, k * P:k * P + P], ident)
                        last.then_inc(sem("probs_transposed"), 1)
                    if i >= 2:
                        hd = i - 2
                        pe.wait_ge(sem("probs_moved"), hd + 1)
                        if hd >= 4:
                            pe.wait_ge(sem("att_moved"), hd - 3)
                        for a in range(TT):
                            for k in range(TT):
                                last = nc.tensor.matmul(aux[hd % 4][:, a * 64:a * 64 + 64], probsT[hd % 2][:, k, a * P:a * P + P],
                                                        av[:, k, hd * 64:hd * 64 + 64], start=k == 0, stop=k == TT - 1)
                        last.then_inc(sem("att_product"), 1)
                pe.wait_ge(sem("att_moved"), 16)
                transpose_tokens(pe, att_o.rearrange("p a h e -> p a (h e)"), "yatt_ready", 24, groups=2)

        klast = area(0, 8, T)
        bsum = area(2048, 8, T)
        qstart = area(4096, 8, T)
        qmid = area(6144, 8, T)
        kmid = area(18432, 8, T)
        ktok = area(20480, TT, 8, P)
        inner = bsum
        state = [area(1024 * s, 8, P) for s in range(2)]
        chunk_decay = vec_t[:, 64:128].rearrange("p (h c) -> p h c", h=8)
        osq = area(0, 4, 512)
        orms = area(2048, 4, 512)
        ones = cst[:, C_ONES:C_ONES + P]

        def by_chunk(v):
            return v.rearrange("p h (c t) -> p (h c) t", t=CHUNK)

        def of_chunk(v, t):
            return by_chunk(v)[:, :, t:t + 1].broadcast_to([P, 8 * NCH, CHUNK])

        with nc.Block() as block:
            @block.gpsimd
            def _(pool):
                for d in range(2):
                    if d:
                        pool.wait_ge(sem("inner_product"), 4)
                    nc.gpsimd.memset(kmid, 1.0).then_inc(sem("scan_mask"), 1)
                    pool.wait_ge(sem("scan_mask"), 2 * d + 1)
                    edge = (CHUNK - 1) if d else 0
                    nc.gpsimd.memset(by_chunk(kmid)[:, :, edge:edge + 1], 0.0).then_inc(sem("scan_mask"), 1)

            @block.scalar
            def _(act):
                for d in range(2):
                    act.wait_ge(sem("forget_ready"), d + 1)
                    if d:
                        act.wait_ge(sem("between"), NCH - 1)
                    nc.scalar.activation(klast, fT[d], ACT.Ln).then_inc(sem("log_ready"), 1)
                    act.wait_ge(sem("sum_ready"), d + 1)
                    nc.scalar.activation(qstart, bsum, ACT.Exp).then_inc(sem("start_exp"), 1)
                    act.wait_ge(sem("from_mid"), d + 1)
                    nc.scalar.activation(kmid, qmid, ACT.Exp, scale=-1.0).then_inc(sem("mid_exp"), 1)
                    act.wait_ge(sem("mid_exp"), 2 * d + 1)
                    nc.scalar.activation(qmid, qmid, ACT.Exp).then_inc(sem("mid_exp"), 1)
                    act.wait_ge(sem("to_last"), d + 1)
                    nc.scalar.activation(klast, klast, ACT.Exp).then_inc(sem("last_exp"), 1)
                    for j in range(4):
                        act.wait_ge(sem("k_transposed"), 4 * d + j + 1)
                        nc.scalar.activation(ktok[:, j // 2, 4 * (j % 2):4 * (j % 2) + 4, :], bank[j][:, :].rearrange("p (c t) -> p c t", c=4),
                                             ACT.Copy).then_inc(sem("k_moved"), 1)
                act.wait_ge(sem("between"), 2 * (NCH - 1))
                for j in range(4):
                    nc.scalar.activation(osq[:, j, :], aux[j], ACT.Square).then_inc(sem("o_squared"), 1)
                act.wait_ge(sem("o_mean"), 1)
                nc.scalar.activation(orms, orms, ACT.Sqrt).then_inc(sem("o_root"), 1)
                for j in range(4):
                    act.wait_ge(sem("hg_ready"), j + 1)
                    nc.scalar.activation(act_hi[:, 8 + 2 * j:10 + 2 * j, :].rearrange("p h t -> p (h t)"), orms[:, j, :],
                                         ACT.Copy).then_inc(sem("hg_rounded"), 1)

            @block.vector
            def _(dve):
                def step(instruction):
                    link(dve, instruction)

                for d in range(2):
                    way = slice(None, None, -1) if d else slice(None)
                    last = 0 if d else CHUNK - 1
                    mid = CHUNK // 2 - (0 if d else 1)
                    for hd in range(8):
                        col = 8 * d + hd
                        f = nc.vector.tensor_scalar(fT[d][:, hd, :], fT[d][:, hd, :], one_minus_lb[:, col:col + 1], lb[:, col:col + 1],
                                                    ALU.mult, ALU.add)
                        step(f)
                    dve.nop().then_inc(sem("forget_ready"), 1)
                    dve.wait_ge(sem("log_ready"), d + 1)
                    step(nc.vector.tensor_scalar(fT[d], fT[d], -1.0, 1.0, ALU.mult, ALU.add))
                    dve.wait_ge(sem("scan_mask"), 2 * d + 2)
                    flat = [v.rearrange("p h t -> p (h t)")[:, way] for v in (bsum, kmid, klast)]
                    nc.vector.tensor_tensor_scan(*flat, 0.0, ALU.mult, ALU.add).then_inc(sem("sum_ready"), 1)
                    dve.wait_ge(sem("sum_ready"), d + 1)
                    nc.vector.tensor_tensor(by_chunk(qmid), by_chunk(bsum), of_chunk(bsum, mid), ALU.subtract).then_inc(sem("from_mid"), 1)
                    nc.vector.tensor_tensor(by_chunk(klast), of_chunk(bsum, last), by_chunk(bsum), ALU.subtract).then_inc(sem("to_last"), 1)
                    dve.wait_ge(sem("start_exp"), d + 1)
                    step(nc.vector.tensor_copy(chunk_decay, qstart.rearrange("p h (c t) -> p h c t", t=CHUNK)[:, :, :, last]))
                    step(nc.vector.tensor_tensor(qstart, qstart, hqT, ALU.mult))
                    dve.wait_ge(sem("mid_exp"), 2 * d + 2)
                    step(nc.vector.tensor_tensor(qmid, qmid, hqT, ALU.mult))
                    nc.vector.tensor_tensor(kmid, kmid, fT[d], ALU.mult).then_inc(sem("mid_ready"), 1)
                    dve.wait_ge(sem("last_exp"), d + 1)
                    nc.vector.tensor_tensor(klast, klast, fT[d], ALU.mult).then_inc(sem("last_ready"), 1)
                    for j in range(4):
                        dve.wait_ge(sem("inner_product"), 4 * d + j + 1)
                        mask = cst[:, (C_BWD if d else C_FWD):(C_BWD if d else C_FWD) + P].unsqueeze(1).broadcast_to([P, 4, P])
                        nc.vector.scalar_tensor_tensor(inner[:, 2 * j:2 * j + 2, :].rearrange("p h (a t) -> p (h a) t", a=TT),
                                                       bank[j][:, :].rearrange("p (c t) -> p c t", c=4), 1e30, mask, ALU.min, ALU.mult).then_inc(sem("inner_ready"), 1)
                    for c in range(NCH - 1):
                        chunk = NCH - 1 - c if d else c
                        n = d * (NCH - 1) + c
                        new, old = state[c % 2], state[1 - c % 2]
                        if n > 1:
                            dve.wait_ge(sem("between"), max(n - 1, d * (NCH - 1)))
                        if c:
                            step(nc.vector.tensor_tensor(new, old, chunk_decay[:, :, chunk:chunk + 1].broadcast_to([P, 8, P]), ALU.mult))
                        for half in range(2):
                            dve.wait_ge(sem("outer_product"), 2 * n + half + 1)
                            kv = bank[2 * (c % 2) + half][:, :].rearrange("p (h v) -> p h v", h=4)
                            to = new[:, 4 * half:4 * half + 4, :]
                            if c:
                                nc.vector.tensor_tensor(to, to, kv, ALU.add).then_inc(sem("state_ready"), 1)
                            else:
                                nc.vector.tensor_copy(to, kv).then_inc(sem("state_ready"), 1)
                            dve.wait_ge(sem("state_ready"), 2 * n + half + 1)

                for j in range(4):
                    dve.wait_ge(sem("o_sums"), j + 1)
                    mean = nc.vector.tensor_scalar(orms[:, j, :], bank[j][:, :], 1.0 / P, EPS, ALU.mult, ALU.add)
                    if j < 3:
                        step(mean)
                mean.then_inc(sem("o_mean"), 1)
                dve.wait_ge(sem("o_root"), 1)
                step(nc.vector.reciprocal(orms, orms))
                for j in range(4):
                    step(nc.vector.scalar_tensor_tensor(orms[:, j, :], aux[j], colsB[:, B_HG:B_HG + 1], orms[:, j, :], ALU.mult, ALU.mult))
                    nc.vector.tensor_tensor(orms[:, j, :], orms[:, j, :], hgT[:, 2 * j:2 * j + 2, :].rearrange("p h t -> p (h t)"),
                                            ALU.mult).then_inc(sem("hg_ready"), 1)
                for j in range(4):
                    dve.wait_ge(sem("hg_rounded"), j + 1)
                    nc.vector.tensor_tensor(act_lo[:, 8 + 2 * j:10 + 2 * j, :].rearrange("p h t -> p (h t)"), orms[:, j, :],
                                            act_hi[:, 8 + 2 * j:10 + 2 * j, :].rearrange("p h t -> p (h t)"), ALU.subtract)

            @block.tensor
            def _(pe):
                for d in range(2):
                    pe.wait_ge(sem("mid_ready"), d + 1)
                    for j in range(4):
                        if d:
                            pe.wait_ge(sem("state_ready"), 2 * (NCH - 1))
                        for c in range(4):
                            hd, a = 2 * j + c // 2, c % 2
                            last = nc.tensor.matmul(bank[j][:, c * P:c * P + P], kmid[:, hd, a * P:a * P + P], qmid[:, hd, a * P:a * P + P],
                                                    start=True, stop=True)
                        last.then_inc(sem("inner_product"), 1)
                    pe.wait_ge(sem("last_ready"), d + 1)
                    for j in range(4):
                        pe.wait_ge(sem("inner_ready"), 4 * d + j + 1)
                        for c in range(4):
                            last = nc.tensor.transpose(bank[j][:, c * P:c * P + P], klast[:, 4 * (j % 2) + c, (j // 2) * P:(j // 2) * P + P], ident)
                        last.then_inc(sem("k_transposed"), 1)
                    for hd in range(8):
                        for a in range(TT):
                            nc.tensor.matmul(aux[hd // 2][:, (hd % 2) * T + a * P:(hd % 2) * T + a * P + P], hv[:, a, hd * P:hd * P + P],
                                             inner[:, hd, a * P:a * P + P], start=d == 0 and hd % 2 == 0 and a == 0, stop=False, skip_group_check=True)
                    pe.wait_ge(sem("k_moved"), 4 * d + 4)
                    for c in range(NCH - 1):
                        n = d * (NCH - 1) + c
                        chunk = NCH - 1 - c if d else c
                        nxt = chunk - 1 if d else chunk + 1
                        lo, a = CHUNK * (chunk % 4), chunk // 4
                        if c >= 2:
                            pe.wait_ge(sem("state_ready"), 2 * n - 2)
                        for hd in range(8):
                            last = nc.tensor.matmul(bank[2 * (c % 2) + hd // 4][:, (hd % 4) * P:(hd % 4) * P + P], ktok[lo:lo + CHUNK, a, hd, :],
                                                    hv[lo:lo + CHUNK, a, hd * P:hd * P + P], start=True, stop=True)
                            if hd % 4 == 3:
                                last.then_inc(sem("outer_product"), 1)
                        for hd in range(8):
                            if hd % 4 == 0:
                                pe.wait_ge(sem("state_ready"), 2 * n + hd // 4 + 1)
                            at = (hd % 2) * T + nxt * CHUNK
                            last = nc.tensor.matmul(aux[hd // 2][:, at:at + CHUNK], state[c % 2][:, hd, :],
                                                    qstart[:, hd, nxt * CHUNK:nxt * CHUNK + CHUNK], start=False,
                                                    stop=d == 1 and c == NCH - 2, skip_group_check=True)
                        last.then_inc(sem("between"), 1)
                for j in range(4):
                    pe.wait_ge(sem("o_squared"), j + 1)
                    nc.tensor.matmul(bank[j][:, :], ones, osq[:, j, :], start=True, stop=True).then_inc(sem("o_sums"), 1)

        y = area(0, TT, D)
        post_row = area(4096, D)
        ple_row = area(6144, D)
        emb = area(8192, TT, D)
        w_pp = area(12288, 2, D)
        p_raw = area(16384, TT, 256)
        pT = area(16896, 2, T)
        with nc.Block() as block:
            @block.sync
            def _(sp):
                sp.dma_start(p_raw, p_2[0, 0].rearrange("(a p) d -> p a d", p=P)).then_inc(sem("p_loaded"), 16)
                sp.dma_start(w_pp, w_pp_2[0].rearrange("(k p) n -> p k n", p=P)).then_inc(sem("w_pp_loaded"), 16)
                load_rest(sp, w_out_2, "out2")
                sp.dma_start(post_row, g_post_2.broadcast_to([P, D])).then_inc(sem("post_row_loaded"), 16)
                sp.dma_start(ple_row, g_ple_2.broadcast_to([P, D])).then_inc(sem("ple_row_loaded"), 16)
                load_first(sp, w_pg_2, "pg")
                load_rest(sp, w_pg_2, "pg")
                for a in range(TT):
                    sp.wait_ge(sem("out_ready"), a + 1)
                    sp.dma_start(out[0, a * P:a * P + P, :], h[:, a, :]).then_inc(sem("out_stored"), 16)
                sp.wait_ge(sem("out_stored"), 16 * TT)

            @block.gpsimd
            def _(pool):
                subtract_all(pool, "out2")
                subtract_all(pool, "pg")

            @block.scalar
            def _(act):
                def read(func):
                    return lambda b, product: nc.scalar.activation(y[:, :, b * NB:b * NB + NB], product, func)

                act.wait_ge(sem("p_transposed"), 1)
                nc.scalar.activation(pT, aux[0].rearrange("p (k t) -> p k t", k=2), ACT.Copy).then_inc(sem("p_moved"), 1)
                round_block(act, turns["out2"][0], 0, (0, 1))
                round_and_read(act, "out2", read(ACT.Copy))
                round_block(act, turns["pg"][0], 0, (0, 1))
                for j in range(8):
                    act.wait_ge(sem("emb_product"), j + 1)
                    nc.scalar.activation(emb[:, j // 4, (j % 4) * 512:(j % 4) * 512 + 512], aux[j % 4], ACT.Copy).then_inc(sem("emb_moved"), 1)
                act.wait_ge(sem("emb_moved"), 8)
                for j in range(2):
                    act.wait_ge(pair_free[j], sum(turns["out2"]))
                squares(act, y, 10, None)
                roots(act, 10)
                round_transposed(act, 28)
                round_and_read(act, "pg", read(ACT.Sigmoid))
                squares(act, y, 12, "gated")
                roots(act, 12)

            @block.vector
            def _(dve):
                def step(instruction):
                    link(dve, instruction)

                reciprocal_rms(dve, 10, D)
                dve.wait_ge(sem("post_row_loaded"), 16)
                for a in range(TT):
                    step(nc.vector.scalar_tensor_tensor(y[:, a, :], y[:, a, :], rms_col(10, a), post_row, ALU.mult, ALU.mult))
                    nc.vector.tensor_tensor(h[:, a, :], h[:, a, :], y[:, a, :], ALU.add).then_inc(sem("h4_ready"), 1)
                subtract_transposed(dve, 28)
                for j in range(2):
                    dve.wait_ge(pair_free[j], sum(turns["pg"]))
                for a in range(TT):
                    nc.vector.tensor_tensor(y[:, a, :], y[:, a, :], emb[:, a, :], ALU.mult).then_inc(sem("gated"), 1)
                reciprocal_rms(dve, 12, D)
                dve.wait_ge(sem("ple_row_loaded"), 16)
                for a in range(TT):
                    step(nc.vector.scalar_tensor_tensor(y[:, a, :], y[:, a, :], rms_col(12, a), ple_row, ALU.mult, ALU.mult))
                    dve.wait_ge(sem("h4_ready"), a + 1)
                    nc.vector.tensor_tensor(h[:, a, :], h[:, a, :], y[:, a, :], ALU.add).then_inc(sem("out_ready"), 1)

            @block.tensor
            def _(pe):
                pe.wait_ge(sem("p_loaded"), 16)
                for k in range(2):
                    for a in range(TT):
                        last = nc.tensor.transpose(aux[0][:, k * T + a * P:k * T + a * P + P], p_raw[:, a, k * P:k * P + P], ident)
                last.then_inc(sem("p_transposed"), 1)
                multiply(pe, *turns["out2"], True)
                pe.wait_ge(sem("w_pp_loaded"), 16)
                pe.wait_ge(sem("p_moved"), 1)
                for j in range(8):
                    a, q = j // 4, j % 4
                    if j >= 4:
                        pe.wait_ge(sem("emb_moved"), j - 3)
                    for k in range(2):
                        last = nc.tensor.matmul(aux[q], pT[:, k, a * P:a * P + P], w_pp[:, k, q * 512:q * 512 + 512], start=k == 0, stop=k == 1)
                    last.then_inc(sem("emb_product"), 1)
                transpose_tokens(pe, h, "h4_ready", 28)
                pe.wait_ge(sem("tokens_moved"), 36)
                multiply(pe, *turns["pg"], True)


_INS = ["x", "mix_norm_g", "w_in", "conv_w", "conv_b", "lru_w_a", "lru_b_a", "lru_w_x", "lru_b_x",
        "lru_lambda", "gmlp_ln_g", "gmlp_ln_b", "gmlp_w_s", "gmlp_b_s", "w_out", "ffn_norm_g",
        "peer_w_q", "peer_sub_keys", "peer_u", "peer_v", "final_norm_g", "p_2", "positions_2",
        "w_in_2", "w_out_2", "g_pre_2", "g_post_2", "g_hg_2", "lb_fwd_2", "lb_bwd_2", "w_pg_2",
        "w_pp_2", "g_ple_2"]


def kernel(**inputs):
    import concourse.bacc as bacc
    from concourse.bass_utils import run_bass_kernel_spmd

    nc = bacc.Bacc("TRN2", target_bir_lowering=False, num_devices=1)
    arrays, args = {}, []
    for name in _INS:
        a = np.ascontiguousarray(inputs[name])
        arrays[f"in_{name}_dram"] = a
        args.append(nc.dram_tensor(f"in_{name}_dram", a.shape, mybir.dt.from_np(a.dtype), kind="ExternalInput").ap())
    arrays["constants_dram"] = shape_constants()
    args.append(nc.dram_tensor("constants_dram", (P, C_END), F32, kind="ExternalInput").ap())
    out = nc.dram_tensor("out_dram", (1, T, D), F32, kind="ExternalOutput").ap()
    build(nc, *args, out)
    r = run_bass_kernel_spmd(nc, [arrays], core_ids=[0])
    return r.results[0]["out_dram"]
```

```python
from contextlib import ExitStack

import numpy as np

import concourse.bass as bass
from concourse import mybir

F32 = mybir.dt.float32
F32R = mybir.dt.float32r
I32 = mybir.dt.int32
U32 = mybir.dt.uint32
ALU = mybir.AluOpType
ACT = mybir.ActivationFunctionType
AX_X = mybir.AxisListType.X

P = 128
D = 2048
T = 256
TT = T // P
KC = D // P
NB = 512
KU = KC // 4
EPS = 1e-6
LRU = 1024
HEADS = 8
KEYS = 128
TOPK = 16
SLOTS = HEADS * TOPK
CHUNK = 32
NCH = T // CHUNK
LRU_C = 8.0
LOWEST = -3.0e38
ROT = 8
TWO_PI = 2 * np.pi
TURN_PARTS = (6.28125, 0.001934051513671875, TWO_PI - 6.28125 - 0.001934051513671875)
ROUNDER = 1.5 * 2.0 ** 23

C_IDENT = 0
C_BIAS = C_IDENT + P
C_IOTA = C_BIAS + TT * T
C_FWD = C_IOTA + TOPK
C_BWD = C_FWD + P
C_INV = C_BWD + P
C_ONES = C_INV + ROT
C_END = C_ONES + P


def shape_constants():
    c = np.zeros((P, C_END), np.float32)
    c[:, C_IDENT:C_IDENT + P] = np.eye(P)
    i, j = np.arange(T)[:, None], np.arange(T)[None, :]
    times = np.zeros((T, T))
    for window, dilation in ((128, 1), (512, 4), (2048, 16)):
        times += (np.abs(i - j) <= window // 2) & ((i - j) % dilation == 0)
    bias = np.where(times > 0, np.log(np.maximum(times, 1)), -1e30)
    c[:, C_BIAS:C_BIAS + TT * T] = bias.reshape(TT, P, T).transpose(1, 0, 2).reshape(P, -1)
    c[:, C_IOTA:C_IOTA + TOPK] = np.arange(TOPK)
    s, t = np.arange(P)[:, None], np.arange(P)[None, :]
    same = s // CHUNK == t // CHUNK
    c[:, C_FWD:C_FWD + P] = same & (s <= t)
    c[:, C_BWD:C_BWD + P] = same & (s >= t)
    exponent = -np.arange(0, 2 * ROT, 2, dtype=np.float32) / np.float32(2 * ROT)
    c[:, C_INV:C_INV + ROT] = np.power(np.float32(500000.0), exponent)
    c[:, C_ONES:C_ONES + P] = 1.0
    return c


A_CONVW, A_CONVB, A_BA, A_BX, A_LAM = 0, 32, 40, 56, 72
A_ROWS = 88
B_LBF, B_LBB, B_HG = 0, 16, 32
B_ROWS = 33


def build(nc, x, mix_norm_g, w_in, conv_w, conv_b, lru_w_a, lru_b_a, lru_w_x, lru_b_x, lru_lambda,
          gmlp_ln_g, gmlp_ln_b, gmlp_w_s, gmlp_b_s, w_out, ffn_norm_g, peer_w_q, peer_sub_keys,
          peer_u, peer_v, final_norm_g, p_2, positions_2, w_in_2, w_out_2, g_pre_2, g_post_2,
          g_hg_2, lb_fwd_2, lb_bwd_2, w_pg_2, w_pp_2, g_ple_2, constants, out):
    ctx = ExitStack()
    with ctx:
        def sbuf(name, words, dtype=F32):
            return ctx.enter_context(nc.sbuf_tensor(name, [P, words], dtype))

        sems = {}

        def sem(name):
            if name not in sems:
                sems[name] = ctx.enter_context(nc.semaphore(name))
            return sems[name]

        h_t = sbuf("residual", TT * D)
        h = h_t[:, :].rearrange("p (a d) -> p a d", a=TT)
        act_hi = ctx.enter_context(nc.sbuf_tensor("act_hi", [P, KC, T], F32R))[:, :, :]
        act_lo = ctx.enter_context(nc.sbuf_tensor("act_lo", [P, KC, T], F32R))[:, :, :]
        w_raw = [ctx.enter_context(nc.sbuf_tensor(f"w_raw{s}", [P, KU, NB], F32)) for s in range(4)]
        w_hi = [ctx.enter_context(nc.sbuf_tensor(f"w_hi{s}", [P, KU, NB], F32R)) for s in range(2)]
        w_lo = [ctx.enter_context(nc.sbuf_tensor(f"w_lo{s}", [P, KU, NB], F32R)) for s in range(2)]
        cst = sbuf("constants_sb", C_END)
        colsA = sbuf("colsA", A_ROWS)
        colsB = sbuf("colsB", B_ROWS)
        stat = sbuf("stat", 64)
        area_t = sbuf("area", 22830)
        vec_t = sbuf("vectors", 2 * P + 128)

        def area(at, *dims, dtype=F32):
            n = int(np.prod(dims))
            v = area_t[:, at:at + n]
            if dtype != F32:
                v = v.bitcast(dtype)
            if len(dims) == 2:
                v = v.rearrange("p (a b) -> p a b", a=dims[0])
            if len(dims) == 3:
                v = v.rearrange("p (a b c) -> p a b c", a=dims[0], b=dims[1])
            if len(dims) == 4:
                v = v.rearrange("p (a b c d) -> p a b c d", a=dims[0], b=dims[1], c=dims[2])
            return v

        bank_t = ctx.enter_context(nc.psum_tensor("banks", [P, 4, 512], F32))
        bank = [bank_t[:, s, :] for s in range(4)]
        pair = [bank_t[:, 2 * j:2 * j + 2, :] for j in range(2)]
        aux_t = ctx.enter_context(nc.psum_tensor("aux", [P, 4, 512], F32))
        aux = [aux_t[:, s, :] for s in range(4)]
        ident = cst[:, C_IDENT:C_IDENT + P]

        chained = {}

        def link(engine, instruction):
            name = f"{engine.engine.name}_own"
            chained[name] = chained.get(name, 0) + 1
            instruction.then_inc(sem(name), 1)
            engine.wait_ge(sem(name), chained[name])

        w_loaded = [sem(f"w_loaded{s}") for s in range(4)]
        hi_ready = [sem(f"hi_ready{b}") for b in range(2)]
        lo_ready = [sem(f"lo_ready{b}") for b in range(2)]
        unit_used = [sem(f"unit_used{b}") for b in range(2)]
        pair_free = [sem(f"pair_free{j}") for j in range(2)]

        turns = {}
        for name, blocks in (("in", 8), ("out", 4), ("q", 4), ("in2", 18), ("out2", 4), ("pg", 4)):
            turns[name] = (sum(n for _, n in turns.values()), blocks // 2)

        def starts(use):
            return isinstance(use, int) and use == 0

        def split_use(turn, j, u):
            return turn * 4 + (2 * j + u // 2)

        def load_block(sp, w, turn, j, col, units=range(4)):
            wv = w[0].rearrange("(k p) n -> p k n", p=P)
            for u in units:
                if not starts(turn * 2 + j):
                    sp.wait_ge(lo_ready[u % 2], split_use(turn, j, u) - 1)
                sp.dma_start(w_raw[u][:, :, :], wv[:, u * KU:u * KU + KU, bass.ds(col + j * NB, NB)]).then_inc(w_loaded[u], 16)

        def load_first(sp, w, name, units=range(4)):
            load_block(sp, w, turns[name][0], 0, 0, units)

        def load_rest(sp, w, name):
            first, n = turns[name]
            load_block(sp, w, first, 1, 0)
            with sp.Fori(1, n) as i:
                load_block(sp, w, i + first, 0, i * (2 * NB))
                load_block(sp, w, i + first, 1, i * (2 * NB))

        def round_block(act, turn, j, units=range(4)):
            for u in units:
                use = split_use(turn, j, u)
                act.wait_ge(w_loaded[u], turn * 32 + (16 * j + 16))
                if not starts(use):
                    act.wait_ge(unit_used[u % 2], use)
                nc.scalar.activation(w_hi[u % 2][:, :, :], w_raw[u][:, :, :], ACT.Copy).then_inc(hi_ready[u % 2], 1)

        def round_unit(act, turn, j, u):
            round_block(act, turn, j, (u,))

        def round_all(act, first, n):
            with act.Fori(0, n) as i:
                for j in range(2):
                    round_block(act, i + first, j)

        def round_and_read(act, name, read):
            first, n = turns[name]
            for b in range(2 * n):
                round_block(act, first + b // 2, b % 2, (2, 3))
                if b + 1 < 2 * n:
                    round_block(act, first + (b + 1) // 2, (b + 1) % 2, (0, 1))
                product_done(act, first + b // 2, b % 2)
                read(b, pair[b % 2]).then_inc(pair_free[b % 2], 1)

        def subtract_turn(pool, turn):
            for j in range(2):
                subtract_block(pool, turn, j)

        def subtract_block(pool, turn, j, units=range(4)):
            for u in units:
                use = split_use(turn, j, u)
                pool.wait_ge(hi_ready[u % 2], use + 1)
                if not starts(use):
                    pool.wait_ge(unit_used[u % 2], use)
                nc.gpsimd.tensor_tensor(w_lo[u % 2][:, :, :], w_raw[u][:, :, :], w_hi[u % 2][:, :, :], ALU.subtract).then_inc(lo_ready[u % 2], 1)

        def subtract_rest(pool, name):
            first, n = turns[name]
            subtract_block(pool, first, 0, (2, 3))
            subtract_block(pool, first, 1)
            with pool.Fori(1, n) as i:
                subtract_turn(pool, i + first)

        def subtract_all(pool, name):
            first, n = turns[name]
            if first == 0:
                subtract_turn(pool, 0)
                first, n = 1, n - 1
            with pool.Fori(0, n) as i:
                subtract_turn(pool, i + first)

        def product_done(engine, turn, j):
            engine.wait_ge(unit_used[1], turn * 4 + (2 * j + 2))

        def multiply_unit(pe, turn, j, u, token):
            use = split_use(turn, j, u)
            if u == 0 and not starts(turn):
                pe.wait_ge(pair_free[j], turn)
            pe.wait_ge(hi_ready[u % 2], use + 1)
            for a, w, lo in ((act_hi, w_hi, False), (act_lo, w_hi, False), (act_hi, w_lo, True)):
                if lo:
                    pe.wait_ge(lo_ready[u % 2], use + 1)
                for part in range(2 if token else 4):
                    to = pair[j][:, part, :] if token else pair[j][:, part // 2, (part % 2) * T:(part % 2) * T + T]
                    for k in range(KU):
                        if token:
                            lhsT, rhs = a[:, u * KU + k, part * P:part * P + P], w[u % 2][:, k, :]
                        else:
                            lhsT, rhs = w[u % 2][:, k, part * P:part * P + P], a[:, u * KU + k, :]
                        clears = u == 0 and k == 0 and a is act_hi and not lo and (token or part % 2 == 0)
                        last = nc.tensor.matmul(to, lhsT, rhs, start=clears, stop=u == 3 and lo and k == KU - 1, skip_group_check=True)
            last.then_inc(unit_used[u % 2], 1)

        def multiply_block(pe, turn, j, token, units=range(4)):
            for u in units:
                multiply_unit(pe, turn, j, u, token)

        def multiply_turn(pe, turn, token):
            for j in range(2):
                multiply_block(pe, turn, j, token)

        def multiply(pe, first, n, token):
            if n == 1 or first == 0:
                multiply_turn(pe, first, token)
                first, n = first + 1, n - 1
            if n:
                with pe.Fori(0, n) as i:
                    multiply_turn(pe, i + first, token)

        BEFORE_N1 = 0
        BEFORE_N2 = BEFORE_N1 + 4 * TT
        BEFORE_UN = BEFORE_N2 + 4 * TT
        BEFORE_ATT = BEFORE_UN + 4 * TT
        BEFORE_H4 = BEFORE_ATT + 2 * TT
        AFTER_H4 = BEFORE_H4 + 4 * TT

        def transpose_tokens(pe, src, ready, before, groups=4):
            for a in range(TT):
                pe.wait_ge(sem(ready), a + 1)
                for q in range(groups):
                    j = a * groups + q
                    if j >= 4:
                        pe.wait_ge(sem("tokens_moved"), before + j - 3)
                    for c in range(4):
                        last = nc.tensor.transpose(aux[j % 4][:, c * P:c * P + P],
                                                   src[:, a, (4 * q + c) * P:(4 * q + c) * P + P], ident)
                    last.then_inc(sem("tokens_transposed"), 1)

        def round_transposed(act, before, groups=4):
            for j in range(TT * groups):
                a, q = j // groups, j % groups
                act.wait_ge(sem("tokens_transposed"), before + j + 1)
                nc.scalar.activation(act_hi[:, 4 * q:4 * q + 4, a * P:a * P + P], aux[j % 4].rearrange("p (c t) -> p c t", c=4),
                                     ACT.Copy).then_inc(sem("tokens_rounded"), 1)

        def subtract_transposed(dve, before, groups=4):
            for j in range(TT * groups):
                a, q = j // groups, j % groups
                dve.wait_ge(sem("tokens_rounded"), before + j + 1)
                nc.vector.tensor_tensor(act_lo[:, 4 * q:4 * q + 4, a * P:a * P + P], aux[j % 4].rearrange("p (c t) -> p c t", c=4),
                                        act_hi[:, 4 * q:4 * q + 4, a * P:a * P + P], ALU.subtract).then_inc(sem("tokens_moved"), 1)

        def squares(act, src, n, ready=None, count=1, squared=None):
            nc.scalar.activation(stat[:, 59:60], stat[:, 58:59], ACT.Sqrt)
            if ready:
                act.wait_ge(sem(ready), count)
            if squared is None:
                squared = aux_t[:, 0:src.shape[2] // 512, :].rearrange("p s n -> p (s n)")
            nc.scalar.activation(squared, src[:, 0, :], ACT.Square, accum_out=stat[:, n:n + 1]).then_inc(sem("squares_done"), 1)

        def roots(act, n):
            act.wait_ge(sem("mean_done"), n // 2 + 1)
            nc.scalar.activation(stat[:, 16 + n:18 + n], stat[:, n:n + 2], ACT.Sqrt).then_inc(sem("root_done"), 1)

        def reciprocal_rms(dve, src, n, squared=None):
            width = src.shape[2]
            if squared is None:
                squared = bank_t[:, 0:width // 512, :].rearrange("p s n -> p (s n)")
            link(dve, nc.vector.scalar_tensor_tensor(squared, src[:, 1, :], 1.0, src[:, 1, :], ALU.mult, ALU.mult,
                                                     accum_out=stat[:, n + 1:n + 2]))
            dve.wait_ge(sem("squares_done"), n // 2 + 1)
            nc.vector.tensor_scalar(stat[:, n:n + 2], stat[:, n:n + 2], 1.0 / width, EPS, ALU.mult, ALU.add).then_inc(sem("mean_done"), 1)
            dve.wait_ge(sem("root_done"), n // 2 + 1)
            link(dve, nc.vector.reciprocal(stat[:, 32 + n:34 + n], stat[:, 16 + n:18 + n]))

        def rms_col(n, a):
            return stat[:, 32 + n + a:33 + n + a]

        decay = area(0, 8, T)
        mix_row = area(0, D)
        grT = area(2048, 8, T)
        guT = area(4096, 8, T)
        gv = area(6144, TT, LRU)
        xrp = area(8192, 8, T + 3)
        ws_raw = area(8192, 8, P)
        v_squared = [area(LRU * a, LRU) for a in range(TT)]
        xcT = area(10272, 8, T)
        gates = area(12320, 2, 2, 8, P)
        ln_g = area(12320, LRU)
        ln_b = area(13344, LRU)
        bs_bc = area(14368, 8, P)
        wsT = area(15392, 8, P)
        xn = area(16416, TT, D)
        rT = area(16416, 8, T)
        iT = area(18464, 8, T)
        hsum = area(20512, 8, T)
        vecs = vec_t[:, 0:2 * P].rearrange("p (a c) -> p a c", a=2)
        lam = vec_t[:, 2 * P:2 * P + 128].rearrange("p (a c) -> p a c", a=8)

        with nc.Block() as block:
            @block.sync
            def _(sp):
                def load(dst, src, name):
                    sp.dma_start(dst, src).then_inc(sem(name), 16)

                load(h[:, 0, :], x[0, 0:P, :], "x_loaded0")
                load(h[:, 1, :], x[0, P:2 * P, :], "x_loaded1")
                load(mix_row, mix_norm_g.broadcast_to([P, D]), "mix_row_loaded")
                load(cst[:, :], constants, "cst_loaded")
                load_first(sp, w_in, "in")
                for which, row, src in (
                    (0, A_CONVW, conv_w[0].rearrange("k (r c) -> (k r) c", c=P)),
                    (0, A_CONVB, conv_b[0].rearrange("(r c) -> r c", c=P)),
                    (0, A_BA, lru_b_a[0].rearrange("d (r c) -> (d r) c", c=P)),
                    (0, A_BX, lru_b_x[0].rearrange("d (r c) -> (d r) c", c=P)),
                    (0, A_LAM, lru_lambda[0].rearrange("d (r c) -> (d r) c", c=P)),
                    (1, B_LBF, lb_fwd_2.rearrange("l (r c) -> (l r) c", c=P)),
                    (1, B_LBB, lb_bwd_2.rearrange("l (r c) -> (l r) c", c=P)),
                    (1, B_HG, g_hg_2),
                ):
                    load(vecs[row:row + src.shape[0], which, :], src, "vecs_loaded")
                for turn, part in enumerate((0, 1, 3, 2)):
                    for j in range(0 if turn else 1, 2):
                        load_block(sp, w_in, turn, j, part * 2 * NB)
                    if turn == 0:
                        for g, w in ((0, lru_w_a), (1, lru_w_x)):
                            for d in range(2):
                                load(gates[:, g, d, :, :], w[0, d].rearrange("h c e -> c h e"), "gates_loaded")
                load_first(sp, w_out, "out")

            @block.gpsimd
            def _(pool):
                nc.gpsimd.memset(stat[:, 58:59], 1.0).then_inc(sem("stat_cleared"), 1)
                nc.gpsimd.memset(xrp[:, :, 0:2], 0.0).then_inc(sem("padded"), 1)
                nc.gpsimd.memset(xrp[:, :, T + 2:T + 3], 0.0).then_inc(sem("padded"), 1)
                subtract_all(pool, "in")
                subtract_block(pool, turns["out"][0], 0, (0,))
                pool.wait_ge(sem("mix_rounded"), 1)
                nc.gpsimd.tensor_tensor(act_lo[:, 0:8, :], hsum, act_hi[:, 0:8, :], ALU.subtract)

            @block.scalar
            def _(act):
                def load(dst, src, name):
                    act.dma_start(dst, src).then_inc(sem(name), 16)

                act.wait_ge(sem("stat_cleared"), 1)
                squares(act, h, 0, "x_loaded0", 16)
                roots(act, 0)

                def read_product(turn, j, dst, func):
                    product_done(act, turn, j)
                    src = pair[j] if dst.shape[1] == TT else pair[j].rearrange("p b (c t) -> p (b c) t", c=2)
                    nc.scalar.activation(dst, src, func).then_inc(pair_free[j], 1)

                round_transposed(act, BEFORE_N1)
                round_block(act, 0, 0)
                round_block(act, 0, 1)
                act.wait_ge(sem("padded"), 2)
                read_product(0, 0, xrp[:, 0:4, 2:2 + T], ACT.Copy)
                round_block(act, 1, 0)
                read_product(0, 1, xrp[:, 4:8, 2:2 + T], ACT.Copy)
                act.wait_ge(sem("lam_abs"), 1)
                nc.scalar.activation(lam[:, 1, :], lam[:, 0, :], ACT.Exp).then_inc(sem("lam_exp"), 1)
                round_block(act, 1, 1)
                read_product(1, 0, grT[:, 0:4, :], ACT.Gelu_apprx_tanh)
                round_block(act, 2, 0, (0, 1))
                read_product(1, 1, grT[:, 4:8, :], ACT.Gelu_apprx_tanh)

                def sigmoids(d):
                    for hd in range(8):
                        n = 8 * d + hd
                        act.wait_ge(sem("gate_product"), n + 1)
                        nc.scalar.activation(rT[:, hd, :], aux[hd % 4][:, 0:T], ACT.Sigmoid,
                                             bias=colsA[:, A_BA + n:A_BA + n + 1]).then_inc(sem("r_ready"), 1)
                        nc.scalar.activation(iT[:, hd, :], aux[hd % 4][:, T:2 * T], ACT.Sigmoid,
                                             bias=colsA[:, A_BX + n:A_BX + n + 1]).then_inc(sem("gate_read"), 1)
                    act.wait_ge(sem("lam_done"), 1)
                    act.wait_ge(sem("r_ready"), 8 * d + 8)
                    for hd in range(8):
                        nc.scalar.activation(decay[:, hd, :], rT[:, hd, :], ACT.Exp,
                                             scale=lam[:, 3, 8 * d + hd:8 * d + hd + 1]).then_inc(sem("decay_ready"), 1)
                    act.wait_ge(sem("decay_ready"), 8 * d + 8)
                    for hd in range(8):
                        nc.scalar.activation(rT[:, hd, :], rT[:, hd, :], ACT.Tanh,
                                             scale=lam[:, 7, 8 * d + hd:8 * d + hd + 1]).then_inc(sem("tanh_ready"), 1)

                def root_of_tanh(d):
                    act.wait_ge(sem("tanh_ready"), 8 * d + 8)
                    nc.scalar.activation(rT, rT, ACT.Sqrt).then_inc(sem("tanh_root"), 1)

                sigmoids(0)
                round_block(act, 2, 0, (2, 3))
                root_of_tanh(0)
                round_block(act, 2, 1)
                read_product(2, 0, gv[:, :, 0:NB], ACT.Gelu_apprx_tanh)
                round_block(act, 3, 0, (0, 1))
                read_product(2, 1, gv[:, :, NB:2 * NB], ACT.Gelu_apprx_tanh)
                act.wait_ge(sem("forward_done"), 1)
                sigmoids(1)
                load(ln_g, gmlp_ln_g.broadcast_to([P, LRU]), "ln_loaded")
                load(ln_b, gmlp_ln_b.broadcast_to([P, LRU]), "ln_loaded")
                load(bs_bc, gmlp_b_s[0:1].broadcast_to([P, 8, P]), "ln_loaded")
                load(ws_raw, gmlp_w_s[0].rearrange("h p q -> p h q"), "ws_loaded")
                round_block(act, 3, 0, (2, 3))
                root_of_tanh(1)
                round_block(act, 3, 1, (0, 1))
                for j in range(2):
                    act.wait_ge(sem("ws_transposed"), j + 1)
                    nc.scalar.activation(wsT[:, 4 * j:4 * j + 4, :], aux[j].rearrange("p (c t) -> p c t", c=4), ACT.Copy).then_inc(sem("ws_moved"), 1)
                act.wait_ge(sem("ws_moved"), 2)
                read_product(3, 0, guT[:, 0:4, :], ACT.Gelu_apprx_tanh)
                round_block(act, 3, 1, (2, 3))
                squares(act, gv, 2, "v_centred", squared=v_squared[0])
                roots(act, 2)
                act.wait_ge(sem("lru_mixed"), 1)
                round_block(act, 4, 0, (0,))
                read_product(3, 1, guT[:, 4:8, :], ACT.Gelu_apprx_tanh)
                nc.scalar.activation(act_hi[:, 0:8, :], hsum, ACT.Copy).then_inc(sem("mix_rounded"), 1)
                for j in range(4):
                    act.wait_ge(sem("gmlp_mixed"), j + 1)
                    nc.scalar.activation(act_hi[:, 8 + 2 * j:10 + 2 * j, :], guT[:, 2 * j:2 * j + 2, :], ACT.Copy).then_inc(sem("mix_rounded"), 1)
                round_block(act, 4, 0, (1,))

            @block.vector
            def _(dve):
                def step(instruction):
                    link(dve, instruction)

                dve.wait_ge(sem("x_loaded1"), 16)
                reciprocal_rms(dve, h, 0)
                dve.wait_ge(sem("x_loaded0"), 16)
                dve.wait_ge(sem("mix_row_loaded"), 16)
                for a in range(TT):
                    nc.vector.scalar_tensor_tensor(xn[:, a, :], h[:, a, :], rms_col(0, a), mix_row, ALU.mult, ALU.mult).then_inc(sem("n1_ready"), 1)
                subtract_transposed(dve, BEFORE_N1)
                dve.wait_ge(sem("vecs_transposed"), 1)
                step(nc.vector.tensor_copy(colsA[:, :], aux[0][:, 0:A_ROWS]))
                step(nc.vector.tensor_copy(colsB[:, :], aux[1][:, 0:B_ROWS]))
                dve.nop().then_inc(sem("cols_ready"), 1)
                lam0 = colsA[:, A_LAM:A_LAM + 16]
                step(nc.vector.tensor_scalar(lam[:, 2, :], lam0, -1.0, None, ALU.mult))
                nc.vector.tensor_tensor(lam[:, 0, :], lam0, lam[:, 2, :], ALU.min).then_inc(sem("lam_abs"), 1)
                dve.wait_ge(sem("lam_exp"), 1)
                step(nc.vector.tensor_scalar(lam[:, 3, :], lam[:, 1, :], 2.0, None, ALU.add))
                step(nc.vector.reciprocal(lam[:, 3, :], lam[:, 3, :]))
                step(nc.vector.tensor_tensor(lam[:, 3, :], lam[:, 3, :], lam[:, 1, :], ALU.mult))
                step(nc.vector.tensor_tensor(lam[:, 4, :], lam[:, 3, :], lam[:, 3, :], ALU.mult))
                step(nc.vector.memset(lam[:, 5, :], 1.0 / 19))
                for n in range(17, 0, -2):
                    step(nc.vector.tensor_tensor(lam[:, 5, :], lam[:, 5, :], lam[:, 4, :], ALU.mult))
                    step(nc.vector.tensor_scalar(lam[:, 5, :], lam[:, 5, :], 1.0 / n, None, ALU.add))
                step(nc.vector.tensor_tensor(lam[:, 5, :], lam[:, 5, :], lam[:, 3, :], ALU.mult))
                step(nc.vector.tensor_scalar(lam[:, 2, :], lam[:, 2, :], 0.0, None, ALU.max))
                step(nc.vector.scalar_tensor_tensor(lam[:, 6, :], lam[:, 5, :], 2.0, lam[:, 2, :], ALU.mult, ALU.add))
                step(nc.vector.tensor_scalar(lam[:, 3, :], lam[:, 6, :], -LRU_C, None, ALU.mult))
                nc.vector.tensor_scalar(lam[:, 7, :], lam[:, 6, :], LRU_C / 2, None, ALU.mult).then_inc(sem("lam_done"), 1)

                for c in range(8):
                    dve.wait_ge(pair_free[c // 4], 1)
                    step(nc.vector.tensor_scalar(xcT[:, c, :], xrp[:, c, 0:T], colsA[:, A_CONVW + c:A_CONVW + c + 1],
                                                 colsA[:, A_CONVB + c:A_CONVB + c + 1], ALU.mult, ALU.add))
                    for k in (1, 2, 3):
                        tap = nc.vector.scalar_tensor_tensor(xcT[:, c, :], xrp[:, c, k:k + T],
                                                             colsA[:, A_CONVW + 8 * k + c:A_CONVW + 8 * k + c + 1],
                                                             xcT[:, c, :], ALU.mult, ALU.add)
                        if k < 3:
                            step(tap)
                    tap.then_inc(sem("conv_done"), 1)

                for d in range(2):
                    dve.wait_ge(sem("decay_ready"), 8 * d + 8)
                    dve.wait_ge(sem("tanh_root"), d + 1)
                    step(nc.vector.scalar_tensor_tensor(rT, decay, 1.0, rT, ALU.add, ALU.mult))
                    dve.wait_ge(sem("gate_read"), 8 * d + 8)
                    step(nc.vector.tensor_tensor(rT, rT, iT, ALU.mult))
                    step(nc.vector.tensor_tensor(rT, rT, xcT, ALU.mult))
                    to = iT if d else hsum
                    way = slice(None, None, -1) if d else slice(None)
                    for hd in range(8):
                        step(nc.vector.tensor_tensor_scan(to[:, hd, way], decay[:, hd, way], rT[:, hd, way], 0.0, ALU.mult, ALU.add))
                    if d == 0:
                        dve.nop().then_inc(sem("forward_done"), 1)
                step(nc.vector.tensor_tensor(hsum, hsum, iT, ALU.add))
                for j in range(2):
                    dve.wait_ge(pair_free[j], 2)
                nc.vector.tensor_tensor(hsum, hsum, grT, ALU.mult).then_inc(sem("lru_mixed"), 1)

                for j in range(2):
                    dve.wait_ge(pair_free[j], 3)
                for a in range(TT):
                    step(nc.vector.tensor_reduce(stat[:, 60 + a:61 + a], gv[:, a, :], AX_X, ALU.add))
                    step(nc.vector.tensor_scalar(stat[:, 62 + a:63 + a], stat[:, 60 + a:61 + a], -1.0 / LRU, None, ALU.mult))
                    nc.vector.tensor_scalar(gv[:, a, :], gv[:, a, :], stat[:, 62 + a:63 + a], None, ALU.add).then_inc(sem("v_centred"), 1)
                dve.wait_ge(sem("v_centred"), 2)
                reciprocal_rms(dve, gv, 2, v_squared[1])
                dve.wait_ge(sem("ln_loaded"), 48)
                for a in range(TT):
                    step(nc.vector.scalar_tensor_tensor(gv[:, a, :], gv[:, a, :], rms_col(2, a), ln_g, ALU.mult, ALU.mult))
                    nc.vector.tensor_tensor(gv[:, a, :], gv[:, a, :], ln_b, ALU.add).then_inc(sem("v_ready"), 1)
                for j in range(4):
                    dve.wait_ge(sem("mixed"), j + 1)
                    step(nc.vector.tensor_tensor(aux[j].rearrange("p (h n t) -> p h n t", h=2, n=2),
                                                 aux[j].rearrange("p (h n t) -> p h n t", h=2, n=2),
                                                 bs_bc[:, 2 * j:2 * j + 2, :].unsqueeze(2).broadcast_to([P, 2, 2, P]), ALU.add))
                for j in range(4):
                    dve.wait_ge(pair_free[j // 2], 4)
                    g = guT[:, 2 * j:2 * j + 2, :]
                    nc.vector.tensor_tensor(g, g, aux[j].rearrange("p (h t) -> p h t", h=2), ALU.mult).then_inc(sem("gmlp_mixed"), 1)
                for j in range(4):
                    dve.wait_ge(sem("mix_rounded"), j + 2)
                    step(nc.vector.tensor_tensor(act_lo[:, 8 + 2 * j:10 + 2 * j, :], guT[:, 2 * j:2 * j + 2, :],
                                                 act_hi[:, 8 + 2 * j:10 + 2 * j, :], ALU.subtract))

            @block.tensor
            def _(pe):
                pe.wait_ge(sem("cst_loaded"), 16)
                pe.wait_ge(sem("squares_done"), 1)
                transpose_tokens(pe, xn, "n1_ready", BEFORE_N1)
                pe.wait_ge(sem("tokens_moved"), BEFORE_N2)
                multiply_turn(pe, 0, False)
                pe.wait_ge(sem("vecs_loaded"), 16 * 8)
                nc.tensor.transpose(aux[0][:, 0:A_ROWS], vecs[0:A_ROWS, 0, :], ident[0:A_ROWS, 0:A_ROWS])
                nc.tensor.transpose(aux[1][:, 0:B_ROWS], vecs[0:B_ROWS, 1, :], ident[0:B_ROWS, 0:B_ROWS]).then_inc(sem("vecs_transposed"), 1)
                multiply_turn(pe, 1, False)
                pe.wait_ge(sem("cols_ready"), 1)
                pe.wait_ge(sem("gates_loaded"), 64)

                def gate_products(d):
                    for hd in range(8):
                        n = 8 * d + hd
                        pe.wait_ge(sem("conv_done"), hd + 1 if d == 0 else 8)
                        if n >= 4:
                            pe.wait_ge(sem("gate_read"), n - 3)
                        nc.tensor.matmul(aux[hd % 4][:, 0:T], gates[:, 0, d, hd, :], xcT[:, hd, :], start=True, stop=True)
                        nc.tensor.matmul(aux[hd % 4][:, T:2 * T], gates[:, 1, d, hd, :], xcT[:, hd, :], start=True, stop=True).then_inc(sem("gate_product"), 1)

                gate_products(0)
                multiply_turn(pe, 2, True)
                gate_products(1)
                multiply_block(pe, 3, 0, False)
                pe.wait_ge(sem("ws_loaded"), 16)
                pe.wait_ge(sem("gate_read"), 16)
                for hd in range(8):
                    last = nc.tensor.transpose(aux[hd // 4][:, (hd % 4) * P:(hd % 4) * P + P], ws_raw[:, hd, :], ident)
                    if hd % 4 == 3:
                        last.then_inc(sem("ws_transposed"), 1)
                multiply_block(pe, 3, 1, False)
                pe.wait_ge(sem("ws_moved"), 2)
                pe.wait_ge(sem("v_ready"), 2)
                for hd in range(8):
                    for n in range(TT):
                        at = (2 * (hd % 2) + n) * P
                        last = nc.tensor.matmul(aux[hd // 2][:, at:at + P], gv[:, n, hd * P:hd * P + P], wsT[:, hd, :],
                                                start=True, stop=True)
                    if hd % 2:
                        last.then_inc(sem("mixed"), 1)

        n2 = area(0, TT, D)
        ffn_row = area(4096, D)
        sk_raw = area(6144, 16, P)
        q_block = [area(12288 + 4 * T * s, 4, T) for s in range(2)]
        skT = area(14336, 16, KEYS)
        scores_1 = area(16384, 16, KEYS)
        scores_0 = [area(18432 + 4 * KEYS * s, 4, KEYS) for s in range(2)]
        cand = area(19456, TOPK, TOPK)
        hot = area(19712, TOPK, TOPK)
        top_s = area(19968, 2, TOPK)
        top_i = area(20000, 2, TOPK, dtype=U32)
        top_f = area(20032, 2, TOPK)
        pos = area(20064, TOPK, dtype=U32)
        pos_part = area(20080, TOPK, dtype=U32)
        pos_f = area(20096, TOPK)
        chosen = area(20112, 2, TOPK)
        gate_w = area(20480, TT, SLOTS)
        ids = area(20736, TT, SLOTS, dtype=I32)
        best = area(20992, HEADS, TOPK)
        total = area(21120, HEADS)
        staged = area(21128, 4, dtype=I32)
        ubuf = [area(4096 + D * s, D) for s in range(4)]
        vbuf = [area(12288 + D * s, D) for s in range(2)] + [w_raw[s][:, :, :].rearrange("p k n -> p (k n)") for s in (2, 3)]
        u_loaded = [sem(f"u_loaded{s}") for s in range(4)]
        v_loaded = [sem(f"v_loaded{s}") for s in range(4)]
        staged_s = [sem(f"staged{s}") for s in range(4)]
        EARLY = HEADS // 2

        def top16(step, values, index, source):
            step(nc.vector.max(values[:, 0:8], source))
            step(nc.vector.max_index(index[:, 0:8], values[:, 0:8], source))
            step(nc.vector.match_replace(source, values[:, 0:8], source, LOWEST))
            step(nc.vector.max(values[:, 8:16], source))
            step(nc.vector.max_index(index[:, 8:16], values[:, 8:16], source))

        def route(dve, step, a, hd, score):
            for g in range(2):
                top16(step, top_s[:, g, :], top_i[:, g, :], score[:, g, :])
            step(nc.vector.tensor_copy(top_f, top_i))
            step(nc.vector.tensor_tensor(cand, top_s[:, 0, :].unsqueeze(2).broadcast_to([P, TOPK, TOPK]),
                                         top_s[:, 1, :].unsqueeze(1).broadcast_to([P, TOPK, TOPK]), ALU.add))
            top16(step, best[:, hd, :], pos, cand.rearrange("p a b -> p (a b)"))
            for part in range(2):
                if part == 0:
                    step(nc.vector.tensor_scalar(pos_part, pos, 4, None, ALU.logical_shift_right))
                else:
                    step(nc.vector.tensor_scalar(pos_part, pos, 15, None, ALU.bitwise_and))
                step(nc.vector.tensor_copy(pos_f, pos_part))
                iota = cst[:, C_IOTA:C_IOTA + TOPK].unsqueeze(1).broadcast_to([P, TOPK, TOPK])
                step(nc.vector.tensor_tensor(hot, iota, pos_f.unsqueeze(2).broadcast_to([P, TOPK, TOPK]), ALU.is_equal))
                step(nc.vector.tensor_tensor(hot, hot, top_f[:, part, :].unsqueeze(1).broadcast_to([P, TOPK, TOPK]), ALU.mult))
                step(nc.vector.tensor_reduce(chosen[:, part, :], hot, AX_X, ALU.add))
            nc.vector.scalar_tensor_tensor(ids[:, a, TOPK * hd:TOPK * hd + TOPK], chosen[:, 0, :], float(KEYS),
                                           chosen[:, 1, :], ALU.mult, ALU.add).then_inc(sem("routed"), 1)
            dve.wait_ge(sem("routed"), HEADS * a + hd + 1)

        def soften(dve, step, n, a, lo, hi):
            v, m = best[:, lo:hi, :], total[:, lo:hi]
            over = m.unsqueeze(2).broadcast_to([P, hi - lo, TOPK])
            step(nc.vector.tensor_copy(m, v[:, :, 0]))
            nc.vector.tensor_tensor(v, v, over, ALU.subtract).then_inc(sem("soft_shifted"), 1)
            dve.wait_ge(sem("soft_exp"), n)
            step(nc.vector.tensor_reduce(m, v, AX_X, ALU.add))
            step(nc.vector.reciprocal(m, m))
            step(nc.vector.tensor_tensor(gate_w[:, a, TOPK * lo:TOPK * hi].rearrange("p (h j) -> p h j", j=TOPK), v, over, ALU.mult))

        def soften_exp(act, n, lo, hi):
            act.wait_ge(sem("soft_shifted"), n)
            nc.scalar.activation(best[:, lo:hi, :], best[:, lo:hi, :], ACT.Exp).then_inc(sem("soft_exp"), 1)

        def gather_u(pool, a, i, s, use):
            nc.gpsimd.tensor_copy(staged[:, s:s + 1], ids[:, a, bass.ds(i * 4 + s, 1)]).then_inc(staged_s[s], 1)
            pool.wait_ge(staged_s[s], use + 1)
            pool.nop(nofuse=True)
            nc.gpsimd.indirect_dma_start(ubuf[s], None, peer_u[0], bass.IndirectOffsetOnAxis(ap=staged[:, s:s + 1], axis=0)).then_inc(u_loaded[s], 16)

        def gather_v(s):
            nc.gpsimd.indirect_dma_start(vbuf[s], None, peer_v[0], bass.IndirectOffsetOnAxis(ap=staged[:, s:s + 1], axis=0)).then_inc(v_loaded[s], 16)

        with nc.Block() as block:
            @block.sync
            def _(sp):
                load_block(sp, w_out, turns["out"][0], 1, 0)
                sp.dma_start(ffn_row, ffn_norm_g[0:1, :].broadcast_to([P, D])).then_inc(sem("ffn_row_loaded"), 16)
                sp.dma_start(sk_raw, peer_sub_keys[0].rearrange("h s n k -> n (h s) k")).then_inc(sem("sk_loaded"), 16)
                for j in range(2):
                    load_block(sp, w_out, turns["out"][0] + 1, j, 2 * NB)
                load_first(sp, peer_w_q, "q")
                load_rest(sp, peer_w_q, "q")
                load_first(sp, w_in_2, "in2", (0, 1))

            @block.gpsimd
            def _(pool):
                subtract_block(pool, turns["out"][0], 0, (1,))
                subtract_rest(pool, "out")
                last = sum(turns["q"]) - 1
                subtract_turn(pool, last - 1)
                subtract_block(pool, last, 0)
                pool.wait_ge(sem("routed"), 1)
                for s in range(4):
                    gather_u(pool, 0, 0, s, 0)
                    subtract_block(pool, last, 1, (s,))
                for s in (2, 3):
                    pool.wait_ge(lo_ready[s % 2], 4 * last + 4)
                    gather_v(s)

            @block.scalar
            def _(act):
                first, n = turns["q"]
                round_block(act, turns["out"][0], 0, (2, 3))
                round_block(act, turns["out"][0], 1)
                round_all(act, turns["out"][0] + 1, turns["out"][1] - 1)
                round_block(act, first, 0, (0, 1))
                for j in range(2):
                    act.wait_ge(pair_free[j], sum(turns["out"]))
                squares(act, h, 4)
                roots(act, 4)
                round_transposed(act, BEFORE_N2)
                for j in range(4):
                    act.wait_ge(sem("sk_transposed"), j + 1)
                    nc.scalar.activation(skT[:, 4 * j:4 * j + 4, :], aux[j].rearrange("p (c t) -> p c t", c=4), ACT.Copy).then_inc(sem("sk_moved"), 1)
                for b in range(2 * n):
                    turn, j = first + b // 2, b % 2
                    round_block(act, turn, j, (3,) if b else (2, 3))
                    if b + 1 < 2 * n:
                        round_block(act, first + (b + 1) // 2, (b + 1) % 2, (0, 1))
                    else:
                        soften_exp(act, 1, 0, EARLY)
                    product_done(act, turn, j)
                    if b >= 2:
                        act.wait_ge(sem("score_product"), 2 * (b - 1))
                    nc.scalar.activation(q_block[b % 2], pair[j].rearrange("p b (c t) -> p (b c) t", c=2), ACT.Copy).then_inc(pair_free[j], 1)
                    if b + 1 < 2 * n:
                        round_block(act, first + (b + 1) // 2, (b + 1) % 2, (2,))
                    for a in range(TT):
                        act.wait_ge(sem("score_product"), TT * b + a + 1)
                        if a == 0 and b >= 2:
                            act.wait_ge(sem("searched"), b - 1)
                        dst = scores_1[:, 4 * b:4 * b + 4, :] if a else scores_0[b % 2]
                        nc.scalar.activation(dst, aux[TT * (b % 2) + a].rearrange("p (c t) -> p c t", c=4), ACT.Copy).then_inc(sem("scores_moved"), 1)

            @block.vector
            def _(dve):
                def step(instruction):
                    link(dve, instruction)

                first, n = turns["out"]
                for b in range(2 * n):
                    turn, j = first + b // 2, b % 2
                    product_done(dve, turn, j)
                    nc.vector.tensor_tensor(h[:, :, b * NB:b * NB + NB], h[:, :, b * NB:b * NB + NB], pair[j], ALU.add).then_inc(pair_free[j], 1)
                for j in range(2):
                    dve.wait_ge(pair_free[j], sum(turns["out"]))
                reciprocal_rms(dve, h, 4)
                dve.wait_ge(sem("ffn_row_loaded"), 16)
                for a in range(TT):
                    nc.vector.scalar_tensor_tensor(n2[:, a, :], h[:, a, :], rms_col(4, a), ffn_row, ALU.mult, ALU.mult).then_inc(sem("n2_ready"), 1)
                subtract_transposed(dve, BEFORE_N2)
                for b in range(EARLY // 2):
                    dve.wait_ge(sem("scores_moved"), TT * b + 1)
                    for hd in range(2):
                        route(dve, step, 0, 2 * b + hd, scores_0[b % 2][:, 2 * hd:2 * hd + 2, :])
                    dve.nop().then_inc(sem("searched"), 1)
                soften(dve, step, 1, 0, 0, EARLY)

            @block.tensor
            def _(pe):
                multiply(pe, *turns["out"], True)
                pe.wait_ge(sem("squares_done"), 3)
                transpose_tokens(pe, n2, "n2_ready", BEFORE_N2)
                pe.wait_ge(sem("tokens_moved"), BEFORE_UN)
                pe.wait_ge(sem("sk_loaded"), 16)
                for g in range(16):
                    last = nc.tensor.transpose(aux[g // 4][:, (g % 4) * P:(g % 4) * P + P], sk_raw[:, g, :], ident)
                    if g % 4 == 3:
                        last.then_inc(sem("sk_transposed"), 1)
                first, n = turns["q"]

                def score(b):
                    if b == 0:
                        pe.wait_ge(sem("sk_moved"), 4)
                    pe.wait_ge(pair_free[b % 2], first + b // 2 + 1)
                    for a in range(TT):
                        if b >= 2:
                            pe.wait_ge(sem("scores_moved"), TT * (b - 2) + a + 1)
                        for c in range(4):
                            last = nc.tensor.matmul(aux[TT * (b % 2) + a][:, c * KEYS:c * KEYS + KEYS], q_block[b % 2][:, c, a * P:a * P + P],
                                                    skT[:, 4 * b + c, :], start=True, stop=True)
                        last.then_inc(sem("score_product"), 1)

                for b in range(2 * n):
                    turn, j = first + b // 2, b % 2
                    multiply_block(pe, turn, j, False, (0, 1))
                    if b:
                        score(b - 1)
                    multiply_block(pe, turn, j, False, (2, 3))
                score(2 * n - 1)

        dots = area(21132, 4)
        gelud = area(21136, 4)
        diag = area(21140, 4, P)
        products = bank_t[:, :, :].rearrange("p s n -> p (s n)")
        dot_done = [sem(f"dot_done{s}") for s in range(4)]
        gelu_done = [sem(f"gelu_done{s}") for s in range(4)]
        diag_done = [sem(f"diag_done{s}") for s in range(4)]
        v_used = [sem(f"v_used{s}") for s in range(4)]
        ROUNDS = SLOTS // 4
        final_row = area(16384, D)
        pre_row = area(18432, D)
        with nc.Block() as block:
            @block.sync
            def _(sp):
                sp.wait_ge(sem("routed"), TT * HEADS)
                sp.wait_ge(v_loaded[2], 16 * TT * ROUNDS)
                sp.dma_start(final_row, final_norm_g.rearrange("(a d) -> a d", a=1).broadcast_to([P, D])).then_inc(sem("gain_rows_loaded"), 16)
                sp.dma_start(pre_row, g_pre_2.broadcast_to([P, D])).then_inc(sem("gain_rows_loaded"), 16)

            @block.gpsimd
            def _(pool):
                def gather(a, i, use):
                    for s in range(4):
                        pool.wait_ge(dot_done[s], use)
                        pool.wait_ge(v_loaded[s], use * 16)
                        gather_u(pool, a, i, s, use)
                        pool.wait_ge(v_used[s], use)
                        pool.nop(nofuse=True)
                        gather_v(s)

                for s in range(2):
                    gather_v(s)
                for a, lo, hi in ((0, 1, ROUNDS // 2), (0, ROUNDS // 2, ROUNDS), (1, 0, ROUNDS)):
                    pool.wait_ge(sem("routed"), HEADS * a + (EARLY if hi < ROUNDS else HEADS))
                    with pool.Fori(lo, hi) as i:
                        gather(a, i, i + a * ROUNDS)

            @block.vector
            def _(dve):
                def weigh(a, i, s, use):
                    dve.wait_ge(gelu_done[s], use + 1)
                    if not starts(use):
                        dve.wait_ge(v_used[s], use)
                    nc.vector.tensor_scalar(diag[:, s, :], ident, gelud[:, s:s + 1], gate_w[:, a, bass.ds(i * 4 + s, 1)],
                                            ALU.mult, ALU.mult).then_inc(diag_done[s], 1)

                def round_of(a, i, use):
                    for s in range(4):
                        dve.wait_ge(u_loaded[s], use * 16 + 16)
                        if s or not starts(use):
                            dve.wait_ge(dot_done[s - 1], use + 1 if s else use)
                        if not starts(use):
                            dve.wait_ge(gelu_done[s], use)
                        nc.vector.scalar_tensor_tensor(products, ubuf[s], 1.0, n2[:, a, :], ALU.mult, ALU.mult,
                                                       accum_out=dots[:, s:s + 1]).then_inc(dot_done[s], 1)
                        if s:
                            weigh(a, i, s - 1, use)
                    weigh(a, i, 3, use)

                def step(instruction):
                    link(dve, instruction)

                left = [(0, hd) for hd in range(EARLY, HEADS)] + [(1, hd) for hd in range(HEADS)]
                for i, (a, hd) in enumerate(left):
                    round_of(0, i, i)
                    score = scores_1[:, 2 * hd:2 * hd + 2, :] if a else scores_0[hd // 2 % 2][:, 2 * (hd % 2):2 * (hd % 2) + 2, :]
                    route(dve, step, a, hd, score)
                    if (a, hd) == (0, HEADS - 1):
                        soften(dve, step, 2, 0, EARLY, HEADS)
                soften(dve, step, 3, 1, 0, HEADS)
                for a in range(TT):
                    with dve.Fori(0 if a else len(left), ROUNDS) as i:
                        round_of(a, i, i + a * ROUNDS)
                    for s in range(4):
                        dve.wait_ge(v_used[s], (a + 1) * ROUNDS)
                    nc.vector.tensor_tensor(h[:, a, :], h[:, a, :], aux_t[:, :, :].rearrange("p s n -> p (s n)"), ALU.add).then_inc(sem("peer_added"), 1)

            @block.scalar
            def _(act):
                def gelus(use):
                    for s in range(4):
                        act.wait_ge(dot_done[s], use + 1)
                        if not starts(use):
                            act.wait_ge(diag_done[s], use)
                        nc.scalar.activation(gelud[:, s:s + 1], dots[:, s:s + 1], ACT.Gelu_apprx_tanh).then_inc(gelu_done[s], 1)

                left = 2 * HEADS - EARLY
                for i in range(left):
                    gelus(i)
                    if i == HEADS - EARLY - 1:
                        soften_exp(act, 2, EARLY, HEADS)
                soften_exp(act, 3, 0, HEADS)
                with act.Fori(left, TT * ROUNDS) as i:
                    gelus(i)

            @block.tensor
            def _(pe):
                def accumulate(use, s, start, stop):
                    pe.wait_ge(v_loaded[s], use * 16 + 16)
                    pe.wait_ge(diag_done[s], use + 1)
                    for q in range(4):
                        last = nc.tensor.matmul(aux[q], diag[:, s, :], vbuf[s][:, q * 512:q * 512 + 512], start=start, stop=stop)
                    last.then_inc(v_used[s], 1)

                for a in range(TT):
                    if a:
                        pe.wait_ge(sem("peer_added"), a)
                    for s in range(4):
                        accumulate(a * ROUNDS, s, s == 0, False)
                    with pe.Fori(1, ROUNDS - 1) as i:
                        for s in range(4):
                            accumulate(i + a * ROUNDS, s, False, False)
                    for s in range(4):
                        accumulate((a + 1) * ROUNDS - 1, s, False, s == 3)

        aq = area(0, TT, 16, 64)
        ak = area(2048, TT, 16, 64)
        av = area(4096, TT, 1024)
        ag = area(6144, TT, 1024)
        hqT = area(8192, 8, T)
        fT = [area(10240, 8, T), area(12288, 8, T)]
        hv = area(14336, TT, 1024)
        hgT = area(16384, 8, T)
        hf = area(8192, TT, D)
        un = area(4096, TT, D)
        turned = area(18432, 4, TT, 16, ROT)
        angle = area(22528, 5, TT * ROT)
        cos_t = area(22608, TT, ROT)
        sin_t = area(22624, TT, ROT)
        pos_i = area(22640, TT, dtype=I32)
        pos_x = area(22642, TT)
        aqT = area(18432, 8, T)
        akT = area(20480, 8, T)
        probs = [area(2048 + 512 * s, TT, T) for s in range(2)]
        probsT = [area(3072 + 512 * s, TT, T) for s in range(2)]
        asum = area(22644, 16, TT)
        amax = area(22676, 16, TT)
        arec = area(22708, 16, TT)
        att_o = aq
        att_bias = cst[:, C_BIAS:C_BIAS + TT * T].rearrange("p (a t) -> p a t", a=TT)
        ATT_SCALE = 64 ** -0.5
        UNITS = 8 * turns["in2"][1]
        QK_UNIT, HEAD_UNIT = 24, 32
        Y_UNIT = HEAD_UNIT + 18
        PREP_UNIT = 8 * 7

        def qk_group(unit):
            return unit - QK_UNIT if QK_UNIT <= unit < HEAD_UNIT else None

        def head_step(unit):
            return unit - HEAD_UNIT if HEAD_UNIT <= unit < Y_UNIT else None

        def place(unit):
            return turns["in2"][0] + unit // 8, unit // 4 % 2, unit % 4

        lb = vec_t[:, 0:16]
        one_minus_lb = vec_t[:, 16:32]

        spare = [w_raw[s][:, :, :].rearrange("p k (c t) -> p (k c) t", t=T) for s in range(4)]
        klast = [area(0, 8, T), spare[1]]
        bsum = [area(2048, 8, T), spare[2]]
        qstart = [area(4096, 8, T), spare[3]]
        qmid = area(6144, 8, T)
        kmid = area(18432, 8, T)
        passed = [fT[0], spare[0]]
        chunk_decay = [vec_t[:, 64 * (d + 1):64 * (d + 2)].rearrange("p (h c) -> p h c", h=8) for d in range(2)]

        def by_chunk(v):
            return v.rearrange("p h (c t) -> p (h c) t", t=CHUNK)

        def of_chunk(v, t):
            return by_chunk(v)[:, :, t:t + 1].broadcast_to([P, 8 * NCH, CHUNK])

        def last_of(d):
            return 0 if d else CHUNK - 1

        CPT = P // CHUNK

        def chunk_at(d, n):
            return CPT - 1 - n if d else n

        def tokens_of(d, lo, hi):
            return slice(P - CHUNK * hi, P - CHUNK * lo) if d else slice(CHUNK * lo, CHUNK * hi)

        def by_tile(v):
            return v.rearrange("p h (a t) -> p h a t", a=TT)

        def pass_keys(dve, d, n):
            new, old = by_tile(passed[(n - 1) % 2]), by_tile(passed[n % 2])
            if n > 1:
                earlier = tokens_of(d, 0, n - 1)
                decay = by_tile(chunk_decay[d])[:, :, :, chunk_at(d, n - 1)].unsqueeze(3).broadcast_to([P, 8, TT, CHUNK * (n - 1)])
                link(dve, nc.vector.tensor_tensor(new[:, :, :, earlier], old[:, :, :, earlier], decay, ALU.mult))
            latest = tokens_of(d, n - 1, n)
            nc.vector.tensor_copy(new[:, :, :, latest], by_tile(klast[d])[:, :, :, latest]).then_inc(sem("keys_passed"), 1)
            dve.wait_ge(sem("keys_passed"), CPT * d + n)

        def forget(dve, d):
            for hd in range(8):
                col = 8 * d + hd
                link(dve, nc.vector.tensor_scalar(fT[d][:, hd, :], fT[d][:, hd, :], one_minus_lb[:, col:col + 1], lb[:, col:col + 1],
                                                  ALU.mult, ALU.add))
            dve.nop().then_inc(sem("forget_ready"), 1)

        def complement(dve, d):
            dve.wait_ge(sem("log_ready"), d + 1)
            link(dve, nc.vector.tensor_scalar(fT[d], fT[d], -1.0, 1.0, ALU.mult, ALU.add))

        def sum_logs(dve, d):
            way = slice(None, None, -1) if d else slice(None)
            flat = [v.rearrange("p h t -> p (h t)")[:, way] for v in (bsum[d], kmid, klast[d])]
            nc.vector.tensor_tensor_scan(*flat, 0.0, ALU.mult, ALU.add).then_inc(sem("sum_ready"), 1)
            dve.wait_ge(sem("sum_ready"), d + 1)

        def less_mid(d):
            mid = CHUNK // 2 - (0 if d else 1)
            nc.vector.tensor_tensor(by_chunk(qmid), by_chunk(bsum[d]), of_chunk(bsum[d], mid), ALU.subtract).then_inc(sem("from_mid"), 1)

        def to_last(d):
            nc.vector.tensor_tensor(by_chunk(klast[d]), of_chunk(bsum[d], last_of(d)), by_chunk(bsum[d]), ALU.subtract).then_inc(sem("to_last"), 1)

        def decays(dve, d):
            dve.wait_ge(sem("start_exp"), d + 1)
            link(dve, nc.vector.tensor_copy(chunk_decay[d], qstart[d].rearrange("p h (c t) -> p h c t", t=CHUNK)[:, :, :, last_of(d)]))

        def take_log(act, d):
            act.wait_ge(sem("forget_ready"), d + 1)
            nc.scalar.activation(klast[d], fT[d], ACT.Ln).then_inc(sem("log_ready"), 1)

        def start_exp(act, d):
            act.wait_ge(sem("sum_ready"), d + 1)
            nc.scalar.activation(qstart[d], bsum[d], ACT.Exp).then_inc(sem("start_exp"), 1)

        def kmid_exp(act, d):
            act.wait_ge(sem("from_mid"), d + 1)
            nc.scalar.activation(kmid, qmid, ACT.Exp, scale=-1.0).then_inc(sem("mid_exp"), 1)

        def qmid_exp(act, d):
            act.wait_ge(sem("mid_exp"), 2 * d + 1)
            nc.scalar.activation(qmid, qmid, ACT.Exp).then_inc(sem("mid_exp"), 1)

        def last_exp(act, d):
            act.wait_ge(sem("to_last"), d + 1)
            nc.scalar.activation(klast[d], klast[d], ACT.Exp).then_inc(sem("last_exp"), 1)

        with nc.Block() as block:
            @block.sync
            def _(sp):
                load_block(sp, w_in_2, turns["in2"][0], 0, 0, (2, 3))
                load_rest(sp, w_in_2, "in2")

            @block.gpsimd
            def _(pool):
                with nc.allow_non_contiguous_dma(reason="256 positions"):
                    pool.dma_start(pos_i, positions_2[0].rearrange("(a p) -> p a", p=P)).then_inc(sem("positions_loaded"), 16)
                subtract_all(pool, "in2")

            @block.scalar
            def _(act):
                def square(row, to):
                    return nc.scalar.activation(aux_t[:, :, :].rearrange("p s n -> p (s n)"), row, ACT.Square, accum_out=to)

                nc.scalar.activation(stat[:, 59:60], stat[:, 58:59], ACT.Sqrt)
                link(act, square(h[:, 0, :], stat[:, 6:7]))
                square(h[:, 1, :], stat[:, 7:8]).then_inc(sem("squares_done"), 1)
                act.wait_ge(sem("squares_done"), 4)
                act.wait_ge(sem("hf_ready"), 1)
                square(hf[:, 0, :], stat[:, 8:9]).then_inc(sem("squares_done"), 1)
                roots(act, 6)
                roots(act, 8)
                round_block(act, turns["in2"][0], 0, (0, 1))
                round_transposed(act, BEFORE_UN)
                for a in range(TT):
                    nc.scalar.activation(h[:, a, :], hf[:, a, :], ACT.Copy, scale=rms_col(6, a))
                act.wait_ge(sem("lb_ready"), 1)
                nc.scalar.activation(lb, lb, ACT.Sigmoid).then_inc(sem("lb_done"), 1)
                act.wait_ge(sem("angle_ready"), 1)
                nc.scalar.activation(sin_t.rearrange("p a e -> p (a e)"), angle[:, 2, :], ACT.Sin).then_inc(sem("trig_ready"), 1)
                nc.scalar.activation(cos_t.rearrange("p a e -> p (a e)"), angle[:, 3, :], ACT.Sin).then_inc(sem("trig_ready"), 1)
                groups = (
                    (aq.rearrange("p a h e -> p a (h e)"), ACT.Copy, True), (ak.rearrange("p a h e -> p a (h e)"), ACT.Copy, True),
                    (av, ACT.Copy, True), (ag, ACT.Silu, True), (hqT, ACT.Silu, False), (fT[0], ACT.Sigmoid, False),
                    (fT[1], ACT.Sigmoid, False), (hv, ACT.Copy, True), (hgT, ACT.Silu, False),
                )

                def read(b, product):
                    dst, func, token = groups[b // 2]
                    if token:
                        return nc.scalar.activation(dst[:, :, (b % 2) * NB:(b % 2) * NB + NB], product, func)
                    return nc.scalar.activation(dst[:, 4 * (b % 2):4 * (b % 2) + 4, :], product.rearrange("p b (c t) -> p (b c) t", c=2), func)

                def read_block(b):
                    product_done(act, turns["in2"][0] + b // 2, b % 2)
                    read(b, pair[b % 2]).then_inc(pair_free[b % 2], 1)

                for unit in range(UNITS):
                    if 0 < unit < UNITS - 1:
                        round_unit(act, *place(unit + 1))
                    if unit and unit % 4 == 0:
                        read_block(unit // 4 - 1)
                    j = qk_group(unit)
                    if j is not None:
                        act.wait_ge(sem("qk_transposed"), j + 1)
                        half, a = j % 2, (j // 2) % 2
                        dst = (aqT if j < 4 else akT)[:, 4 * half:4 * half + 4, a * P:a * P + P]
                        nc.scalar.activation(dst, aux[j % 4].rearrange("p (c t) -> p c t", c=4), ACT.Copy,
                                             scale=ATT_SCALE if j < 4 else 1.0).then_inc(sem("qk_moved"), 1)
                    i = head_step(unit)
                    if i is not None and i < 16:
                        act.wait_ge(sem("att_max"), i + 1)
                        for a in range(TT):
                            nc.scalar.activation(probs[i % 2][:, a, :], probs[i % 2][:, a, :], ACT.Exp, bias=amax[:, i, a:a + 1],
                                                 accum_out=asum[:, i, a:a + 1]).then_inc(sem("probs_ready"), 1)
                    if i is not None and 1 <= i <= 16:
                        hd = i - 1
                        act.wait_ge(sem("probs_transposed"), hd + 1)
                        if hd >= 2:
                            act.wait_ge(sem("att_product"), hd - 1)
                        nc.scalar.activation(probsT[hd % 2], aux[2].rearrange("p (c t) -> p c t", c=2), ACT.Copy).then_inc(sem("probs_moved"), 1)
                    if unit == PREP_UNIT:
                        act.wait_ge(sem("tokens_transposed"), BEFORE_H4)
                        take_log(act, 0)
                    if unit == PREP_UNIT + 2:
                        start_exp(act, 0)
                    if unit == PREP_UNIT + 3:
                        kmid_exp(act, 0)
                    if unit == PREP_UNIT + 4:
                        qmid_exp(act, 0)
                    if unit == PREP_UNIT + 5:
                        last_exp(act, 0)
                read_block(UNITS // 4 - 1)

            @block.vector
            def _(dve):
                def step(instruction):
                    link(dve, instruction)

                dve.wait_ge(sem("gain_rows_loaded"), 32)
                for a in range(TT):
                    nc.vector.tensor_tensor(hf[:, a, :], h[:, a, :], final_row, ALU.mult).then_inc(sem("hf_ready"), 1)
                dve.wait_ge(sem("squares_done"), 4)
                nc.vector.tensor_scalar(stat[:, 6:8], stat[:, 6:8], 1.0 / D, EPS, ALU.mult, ALU.add).then_inc(sem("mean_done"), 1)
                dve.wait_ge(sem("hf_ready"), 2)
                step(nc.vector.scalar_tensor_tensor(bank_t[:, :, :].rearrange("p s n -> p (s n)"), hf[:, 1, :], 1.0, hf[:, 1, :],
                                                    ALU.mult, ALU.mult, accum_out=stat[:, 9:10]))
                dve.wait_ge(sem("root_done"), 4)
                r6, r6_squared, r8, r6_r8 = stat[:, 38:40], stat[:, 50:52], stat[:, 40:42], stat[:, 48:50]
                step(nc.vector.reciprocal(r6, stat[:, 22:24]))
                step(nc.vector.tensor_tensor(r6_squared, r6, r6, ALU.mult))
                dve.wait_ge(sem("squares_done"), 5)
                step(nc.vector.tensor_tensor(stat[:, 8:10], stat[:, 8:10], r6_squared, ALU.mult))
                nc.vector.tensor_scalar(stat[:, 8:10], stat[:, 8:10], 1.0 / D, EPS, ALU.mult, ALU.add).then_inc(sem("mean_done"), 1)
                dve.wait_ge(sem("root_done"), 5)
                step(nc.vector.reciprocal(r8, stat[:, 24:26]))
                step(nc.vector.tensor_tensor(r6_r8, r6, r8, ALU.mult))
                for a in range(TT):
                    nc.vector.scalar_tensor_tensor(un[:, a, :], hf[:, a, :], stat[:, 48 + a:49 + a], pre_row, ALU.mult, ALU.mult).then_inc(sem("un_ready"), 1)
                subtract_transposed(dve, BEFORE_UN)
                step(nc.vector.tensor_tensor(lb[:, 0:8], colsB[:, B_LBF:B_LBF + 8], colsB[:, B_LBF + 8:B_LBF + 16], ALU.subtract))
                nc.vector.tensor_tensor(lb[:, 8:16], colsB[:, B_LBB:B_LBB + 8], colsB[:, B_LBB + 8:B_LBB + 16], ALU.subtract).then_inc(sem("lb_ready"), 1)
                dve.wait_ge(sem("lb_done"), 1)
                step(nc.vector.tensor_scalar(one_minus_lb, lb, -1.0, 1.0, ALU.mult, ALU.add))
                dve.wait_ge(sem("positions_loaded"), 16)
                step(nc.vector.tensor_copy(pos_x, pos_i))
                inv = cst[:, C_INV:C_INV + ROT].unsqueeze(1).broadcast_to([P, TT, ROT])
                step(nc.vector.tensor_tensor(angle[:, 0, :].rearrange("p (a e) -> p a e", a=TT), inv,
                                             pos_x.unsqueeze(2).broadcast_to([P, TT, ROT]), ALU.mult))
                step(nc.vector.tensor_scalar(angle[:, 1, :], angle[:, 0, :], 1.0 / TWO_PI, ROUNDER, ALU.mult, ALU.add))
                step(nc.vector.tensor_scalar(angle[:, 1, :], angle[:, 1, :], -ROUNDER, None, ALU.add))
                step(nc.vector.scalar_tensor_tensor(angle[:, 2, :], angle[:, 1, :], -TURN_PARTS[0], angle[:, 0, :], ALU.mult, ALU.add))
                step(nc.vector.scalar_tensor_tensor(angle[:, 2, :], angle[:, 1, :], -TURN_PARTS[1], angle[:, 2, :], ALU.mult, ALU.add))
                step(nc.vector.scalar_tensor_tensor(angle[:, 2, :], angle[:, 1, :], -TURN_PARTS[2], angle[:, 2, :], ALU.mult, ALU.add))
                step(nc.vector.tensor_scalar(angle[:, 2, :], angle[:, 2, :], 3.1415925, -3.1415925, ALU.min, ALU.max))
                step(nc.vector.tensor_scalar(angle[:, 4, :], angle[:, 2, :], -1.0, None, ALU.mult))
                step(nc.vector.tensor_tensor(angle[:, 3, :], angle[:, 4, :], angle[:, 2, :], ALU.min))
                nc.vector.tensor_scalar(angle[:, 3, :], angle[:, 3, :], float(np.pi / 2), None, ALU.add).then_inc(sem("angle_ready"), 1)
                dve.wait_ge(sem("trig_ready"), 2)
                c = cos_t.unsqueeze(2).broadcast_to([P, TT, 16, ROT])
                sn = sin_t.unsqueeze(2).broadcast_to([P, TT, 16, ROT])
                for n, t in enumerate((aq, ak)):
                    for j in range(2):
                        dve.wait_ge(pair_free[j], turns["in2"][0] + n + 1)
                    x1, x2 = t[:, :, :, 0:ROT], t[:, :, :, ROT:2 * ROT]
                    for m, (u, v) in enumerate(((x1, c), (x2, sn), (x2, c), (x1, sn))):
                        step(nc.vector.tensor_tensor(turned[:, m], u, v, ALU.mult))
                    step(nc.vector.tensor_tensor(x1, turned[:, 0], turned[:, 1], ALU.subtract))
                    nc.vector.tensor_tensor(x2, turned[:, 2], turned[:, 3], ALU.add).then_inc(sem("rotated"), 1)
                    dve.wait_ge(sem("rotated"), n + 1)
                for i in range(18):
                    if i < 16:
                        dve.wait_ge(sem("att_scores"), i + 1)
                        if i >= 2:
                            dve.wait_ge(sem("probs_transposed"), i - 1)
                        nc.vector.tensor_tensor(probs[i % 2], aux[i % 2].rearrange("p (a t) -> p a t", a=TT), att_bias,
                                                ALU.add).then_inc(sem("logits_ready"), 1)
                        dve.wait_ge(sem("logits_ready"), i + 1)
                        nc.vector.tensor_reduce(amax[:, i, :], probs[i % 2], AX_X, ALU.max, negate=True).then_inc(sem("att_max"), 1)
                    if i >= 2:
                        hd = i - 2
                        dve.wait_ge(sem("att_product"), hd + 1)
                        step(nc.vector.reciprocal(arec[:, hd, :], asum[:, hd, :]))
                        nc.vector.tensor_tensor(att_o[:, :, hd, :], aux[3][:, 0:P].rearrange("p (a e) -> p a e", a=TT),
                                                arec[:, hd, :].unsqueeze(2).broadcast_to([P, TT, 64]), ALU.mult).then_inc(sem("att_moved"), 1)
                dve.wait_ge(sem("att_moved"), 16)
                for a in range(TT):
                    o = att_o[:, a].rearrange("p h e -> p (h e)")
                    nc.vector.tensor_tensor(o, o, ag[:, a, :], ALU.mult).then_inc(sem("yatt_ready"), 1)
                dve.wait_ge(sem("yatt_ready"), 2)
                for j in range(2):
                    dve.wait_ge(pair_free[j], turns["in2"][0] + 7)
                forget(dve, 0)
                step(nc.vector.memset(kmid, 1.0))
                step(nc.vector.memset(by_chunk(kmid)[:, :, 0:1], 0.0))
                complement(dve, 0)
                sum_logs(dve, 0)
                less_mid(0)
                to_last(0)
                decays(dve, 0)
                step(nc.vector.tensor_tensor(qstart[0], qstart[0], hqT, ALU.mult))
                dve.wait_ge(sem("mid_exp"), 2)
                step(nc.vector.tensor_tensor(qmid, qmid, hqT, ALU.mult))
                step(nc.vector.tensor_tensor(kmid, kmid, fT[0], ALU.mult))
                dve.wait_ge(sem("last_exp"), 1)
                step(nc.vector.tensor_tensor(klast[0], klast[0], fT[0], ALU.mult))
                step(nc.vector.memset(passed[0], 0.0))
                pass_keys(dve, 0, 1)
                forget(dve, 1)

            @block.tensor
            def _(pe):
                transpose_tokens(pe, un, "un_ready", BEFORE_UN)
                pe.wait_ge(sem("tokens_moved"), BEFORE_ATT)
                first, _ = turns["in2"]
                multiply(pe, first, 3, True)
                for unit in range(8 * 3, UNITS):
                    j = qk_group(unit)
                    if j is not None:
                        half, a = j % 2, (j // 2) % 2
                        pe.wait_ge(sem("rotated"), 2)
                        if j >= 4:
                            pe.wait_ge(sem("qk_moved"), j - 3)
                        src = (aq if j < 4 else ak).rearrange("p a h e -> p a (h e)")
                        for c in range(4):
                            last = nc.tensor.transpose(aux[j % 4][:, c * P:c * P + P], src[:, a, (4 * half + c) * P:(4 * half + c) * P + P], ident)
                        last.then_inc(sem("qk_transposed"), 1)
                    i = head_step(unit)
                    if i is not None and i < 16:
                        at, c = 64 * (i % 2), i // 2
                        if i == 0:
                            pe.wait_ge(sem("qk_moved"), 8)
                        if i >= 2:
                            pe.wait_ge(sem("logits_ready"), i - 1)
                        for a in range(TT):
                            last = nc.tensor.matmul(aux[i % 2][:, a * T:a * T + T], aqT[at:at + 64, c, a * P:a * P + P],
                                                    akT[at:at + 64, c, :], start=True, stop=True)
                        last.then_inc(sem("att_scores"), 1)
                    if i is not None and 1 <= i <= 16:
                        hd = i - 1
                        pe.wait_ge(sem("probs_ready"), 2 * hd + 2)
                        if hd >= 1:
                            pe.wait_ge(sem("probs_moved"), hd)
                        for k in range(TT):
                            for a in range(TT):
                                at = k * T + a * P
                                last = nc.tensor.transpose(aux[2][:, at:at + P], probs[hd % 2][:, a, k * P:k * P + P], ident)
                        last.then_inc(sem("probs_transposed"), 1)
                    if i is not None and i >= 2:
                        hd = i - 2
                        pe.wait_ge(sem("probs_moved"), hd + 1)
                        if hd >= 1:
                            pe.wait_ge(sem("att_moved"), hd)
                        for a in range(TT):
                            for k in range(TT):
                                last = nc.tensor.matmul(aux[3][:, a * 64:a * 64 + 64], probsT[hd % 2][:, k, a * P:a * P + P],
                                                        av[:, k, hd * 64:hd * 64 + 64], start=k == 0, stop=k == TT - 1)
                        last.then_inc(sem("att_product"), 1)
                    if Y_UNIT <= unit < Y_UNIT + 4:
                        a, q = (unit - Y_UNIT) // 2, (unit - Y_UNIT) % 2
                        pe.wait_ge(sem("yatt_ready"), a + 1)
                        src = att_o.rearrange("p a h e -> p a (h e)")
                        for c in range(4):
                            last = nc.tensor.transpose(aux[unit - Y_UNIT][:, c * P:c * P + P], src[:, a, (4 * q + c) * P:(4 * q + c) * P + P], ident)
                        last.then_inc(sem("tokens_transposed"), 1)
                    turn, j, u = place(unit)
                    multiply_unit(pe, turn, j, u, turn - first in (0, 1, 2, 3, 7))

        ktok = area(20480, 8, P)
        inner = bsum
        state = area(21504, 8, P)
        prefix = vec_t[:, 192:192 + 8 * CPT].rearrange("p (h c) -> p h c", h=8)
        osq = area(0, 4, 512)
        orms = area(2048, 4, 512)
        ones = cst[:, C_ONES:C_ONES + P]

        with nc.Block() as block:
            @block.sync
            def _(sp):
                sp.wait_ge(sem("k_transposed"), 4)
                load_first(sp, w_out_2, "out2", (0,))
                sp.wait_ge(sem("between"), 2)
                load_first(sp, w_out_2, "out2", (1, 2, 3))

            @block.gpsimd
            def _(pool):
                nc.gpsimd.memset(passed[1], 0.0).then_inc(sem("keys_cleared"), 1)
                pool.wait_ge(sem("inner_product"), 4)
                nc.gpsimd.memset(kmid, 1.0).then_inc(sem("scan_mask"), 1)
                pool.wait_ge(sem("scan_mask"), 1)
                nc.gpsimd.memset(by_chunk(kmid)[:, :, CHUNK - 1:CHUNK], 0.0).then_inc(sem("scan_mask"), 1)
                pool.wait_ge(sem("cross_product"), 3)
                pool.wait_ge(sem("keys_passed"), CPT)
                nc.gpsimd.memset(passed[0], 0.0).then_inc(sem("keys_cleared"), 1)
                pool.wait_ge(sem("sum_ready"), 2)
                pool.wait_ge(sem("mid_exp"), 3)
                nc.gpsimd.tensor_tensor(kmid, kmid, fT[1], ALU.mult).then_inc(sem("kmid_ready"), 1)
                pool.wait_ge(sem("k_transposed"), 2)
                nc.gpsimd.memset(passed[1], 0.0).then_inc(sem("keys_cleared"), 1)
                pool.wait_ge(sem("last_exp"), 2)
                nc.gpsimd.tensor_tensor(klast[1], klast[1], fT[1], ALU.mult).then_inc(sem("klast_ready"), 1)
                pool.wait_ge(sem("decays_taken"), 1)
                nc.gpsimd.tensor_tensor(qstart[1], qstart[1], hqT, ALU.mult).then_inc(sem("qstart_ready"), 1)
                subtract_block(pool, turns["out2"][0], 0, (0,))
            @block.scalar
            def _(act):
                def move_keys(d):
                    for half in range(2):
                        act.wait_ge(sem("k_transposed"), 2 * d + half + 1)
                        nc.scalar.activation(ktok[:, 4 * half:4 * half + 4, :], bank[half].rearrange("p (c t) -> p c t", c=4),
                                             ACT.Copy).then_inc(sem("k_moved"), 1)

                def move_state(d):
                    if d:
                        act.wait_ge(sem("between"), 1)
                    for half in range(2):
                        act.wait_ge(sem("outer_product"), 2 * d + half + 1)
                        nc.scalar.activation(state[:, 4 * half:4 * half + 4, :], bank[2 + half].rearrange("p (h v) -> p h v", h=4),
                                             ACT.Copy).then_inc(sem("state_ready"), 1)

                round_transposed(act, BEFORE_ATT, groups=2)
                take_log(act, 1)
                start_exp(act, 1)
                kmid_exp(act, 1)
                qmid_exp(act, 1)
                last_exp(act, 1)
                move_keys(0)
                move_state(0)
                move_keys(1)
                move_state(1)
                act.wait_ge(sem("between"), 2)
                for j in range(4):
                    nc.scalar.activation(osq[:, j, :], aux[j], ACT.Square).then_inc(sem("o_squared"), 1)
                round_block(act, turns["out2"][0], 0, (0,))
                for j in range(4):
                    act.wait_ge(sem("o_mean"), j + 1)
                    nc.scalar.activation(orms[:, j, :], orms[:, j, :], ACT.Ln).then_inc(sem("o_log"), 1)
                for j in range(4):
                    act.wait_ge(sem("o_log"), j + 1)
                    nc.scalar.activation(orms[:, j, :], orms[:, j, :], ACT.Exp, scale=-0.5).then_inc(sem("o_root"), 1)
                for j in range(4):
                    act.wait_ge(sem("hg_ready"), j + 1)
                    nc.scalar.activation(act_hi[:, 8 + 2 * j:10 + 2 * j, :].rearrange("p h t -> p (h t)"), orms[:, j, :],
                                         ACT.Copy).then_inc(sem("hg_rounded"), 1)

            @block.vector
            def _(dve):
                def step(instruction):
                    link(dve, instruction)

                subtract_transposed(dve, BEFORE_ATT, groups=2)
                def mask_inner(d):
                    for j in range(4):
                        dve.wait_ge(sem("inner_product"), 4 * d + j + 1)
                        mask = cst[:, (C_BWD if d else C_FWD):(C_BWD if d else C_FWD) + P].unsqueeze(1).broadcast_to([P, 4, P])
                        nc.vector.scalar_tensor_tensor(inner[d][:, 2 * j:2 * j + 2, :].rearrange("p h (a t) -> p (h a) t", a=TT),
                                                       bank[j][:, :].rearrange("p (c t) -> p c t", c=4), 1e30, mask, ALU.min, ALU.mult).then_inc(sem("masked"), 1)

                def next_keys(d, n):
                    if n > 2:
                        dve.wait_ge(sem("cross_product"), 3 * d + n - 2)
                    else:
                        dve.wait_ge(sem("keys_cleared"), n + 1 if d else 1)
                    pass_keys(dve, d, n)

                def add_cross(d):
                    later = tokens_of(d, 1, CPT)
                    dve.wait_ge(sem("cross_product"), 3 * d + 3)
                    dve.wait_ge(sem("masked"), 4 * d + 4)
                    for j in range(4):
                        to = inner[d][:, 2 * j:2 * j + 2, :].rearrange("p h (a t) -> p (h a) t", a=TT)[:, :, later]
                        nc.vector.tensor_tensor(to, to, bank[j].rearrange("p (c t) -> p c t", c=4)[:, :, later], ALU.add).then_inc(sem("inner_ready"), 1)

                def pass_queries(d):
                    tile = 0 if d else 1
                    decay = by_tile(chunk_decay[d])[:, :, tile, :]
                    at = [chunk_at(d, n) for n in range(CPT)]
                    step(nc.vector.tensor_copy(prefix[:, :, at[1]], decay[:, :, at[0]]))
                    for n in range(2, CPT):
                        step(nc.vector.tensor_tensor(prefix[:, :, at[n]], prefix[:, :, at[n - 1]], decay[:, :, at[n - 1]], ALU.mult))
                    q = by_tile(qstart[d])[:, :, tile, tokens_of(d, 1, CPT)].rearrange("p h (c t) -> p h c t", t=CHUNK)
                    lo = min(at[1:])
                    by = prefix[:, :, lo:lo + CPT - 1].unsqueeze(3).broadcast_to([P, 8, CPT - 1, CHUNK])
                    nc.vector.tensor_tensor(q, q, by, ALU.mult).then_inc(sem("queries_passed"), 1)

                next_keys(0, 2)
                mask_inner(0)
                next_keys(0, 3)
                complement(dve, 1)
                next_keys(0, 4)
                dve.wait_ge(sem("scan_mask"), 2)
                sum_logs(dve, 1)
                less_mid(1)
                add_cross(0)
                pass_queries(0)
                to_last(1)
                decays(dve, 1)
                dve.nop().then_inc(sem("decays_taken"), 1)
                dve.wait_ge(sem("mid_exp"), 4)
                nc.vector.tensor_tensor(qmid, qmid, hqT, ALU.mult).then_inc(sem("qmid_ready"), 1)
                dve.wait_ge(sem("klast_ready"), 1)
                next_keys(1, 1)
                next_keys(1, 2)
                mask_inner(1)
                next_keys(1, 3)
                next_keys(1, 4)
                add_cross(1)
                dve.wait_ge(sem("qstart_ready"), 1)
                pass_queries(1)

                for j in range(4):
                    dve.wait_ge(sem("o_squared"), j + 1)
                    gate = hgT[:, 2 * j:2 * j + 2, :].rearrange("p h t -> p (h t)")
                    step(nc.vector.scalar_tensor_tensor(gate, aux[j], colsB[:, B_HG:B_HG + 1], gate, ALU.mult, ALU.mult))
                for j in range(4):
                    dve.wait_ge(sem("o_sums"), j + 1)
                    nc.vector.tensor_scalar(orms[:, j, :], bank[j][:, :], 1.0 / P, EPS, ALU.mult, ALU.add).then_inc(sem("o_mean"), 1)
                for j in range(4):
                    dve.wait_ge(sem("o_root"), j + 1)
                    nc.vector.tensor_tensor(orms[:, j, :], hgT[:, 2 * j:2 * j + 2, :].rearrange("p h t -> p (h t)"), orms[:, j, :],
                                            ALU.mult).then_inc(sem("hg_ready"), 1)
                for j in range(4):
                    dve.wait_ge(sem("hg_rounded"), j + 1)
                    nc.vector.tensor_tensor(act_lo[:, 8 + 2 * j:10 + 2 * j, :].rearrange("p h t -> p (h t)"), orms[:, j, :],
                                            act_hi[:, 8 + 2 * j:10 + 2 * j, :].rearrange("p h t -> p (h t)"), ALU.subtract)

            @block.tensor
            def _(pe):
                for d in range(2):
                    first, second = (1, 0) if d else (0, 1)
                    if d:
                        pe.wait_ge(sem("qmid_ready"), 1)
                        pe.wait_ge(sem("kmid_ready"), 1)
                        pe.wait_ge(sem("k_moved"), 2)
                        pe.wait_ge(sem("state_ready"), 2)
                    for j in range(4):
                        for c in range(4):
                            hd, a = 2 * j + c // 2, c % 2
                            last = nc.tensor.matmul(bank[j][:, c * P:c * P + P], kmid[:, hd, a * P:a * P + P], qmid[:, hd, a * P:a * P + P],
                                                    start=True, stop=True)
                        last.then_inc(sem("inner_product"), 1)
                    if d:
                        pe.wait_ge(sem("qstart_ready"), 1)
                    for n in range(1, CPT):
                        pe.wait_ge(sem("keys_passed"), CPT * d + n)
                        for j in range(4):
                            if n == 1:
                                pe.wait_ge(sem("masked"), 4 * d + j + 1)
                            for c in range(4):
                                hd, a = 2 * j + c // 2, c % 2
                                at = CHUNK * chunk_at(d, n)
                                last = nc.tensor.matmul(bank[j][:, c * P + at:c * P + at + CHUNK], passed[(n - 1) % 2][:, hd, a * P:a * P + P],
                                                        qstart[d][:, hd, a * P + at:a * P + at + CHUNK], start=True, stop=True)
                        last.then_inc(sem("cross_product"), 1)
                    pe.wait_ge(sem("keys_passed"), CPT * d + CPT)
                    for half in range(2):
                        pe.wait_ge(sem("inner_ready"), 4 * d + half + 1)
                        for c in range(4):
                            last = nc.tensor.transpose(bank[half][:, c * P:c * P + P], passed[(CPT - 1) % 2][:, 4 * half + c, first * P:first * P + P], ident)
                        last.then_inc(sem("k_transposed"), 1)
                    pe.wait_ge(sem("tokens_moved"), BEFORE_H4)
                    for hd in range(8):
                        if hd % 2 == 0:
                            pe.wait_ge(sem("inner_ready"), 4 * d + hd // 2 + 1)
                        for a in range(TT):
                            nc.tensor.matmul(aux[hd // 2][:, (hd % 2) * T + a * P:(hd % 2) * T + a * P + P], hv[:, a, hd * P:hd * P + P],
                                             inner[d][:, hd, a * P:a * P + P], start=d == 0 and hd % 2 == 0 and a == 0, stop=False, skip_group_check=True)
                    for half in range(2):
                        pe.wait_ge(sem("k_moved"), 2 * d + half + 1)
                        for c in range(4):
                            hd = 4 * half + c
                            last = nc.tensor.matmul(bank[2 + half][:, c * P:c * P + P], ktok[:, hd, :], hv[:, first, hd * P:hd * P + P], start=True, stop=True)
                        last.then_inc(sem("outer_product"), 1)
                    pe.wait_ge(sem("queries_passed"), d + 1)
                    for hd in range(8):
                        if hd % 4 == 0:
                            pe.wait_ge(sem("state_ready"), 2 * d + hd // 4 + 1)
                        at = (hd % 2) * T + second * P
                        last = nc.tensor.matmul(aux[hd // 2][:, at:at + P], state[:, hd, :], qstart[d][:, hd, second * P:second * P + P],
                                                start=False, stop=d == 1, skip_group_check=True)
                    last.then_inc(sem("between"), 1)
                for j in range(4):
                    pe.wait_ge(sem("o_squared"), j + 1)
                    nc.tensor.matmul(bank[j][:, :], ones, osq[:, j, :], start=True, stop=True).then_inc(sem("o_sums"), 1)

        y = area(0, TT, D)
        post_row = area(4096, D)
        ple_row = area(6144, D)
        emb = area(8192, TT, D)
        w_pp = area(12288, 2, D)
        p_raw = area(16384, TT, 256)
        pT = area(16896, 2, T)
        scaled = area(18432, TT, D)
        with nc.Block() as block:
            @block.sync
            def _(sp):
                load_block(sp, w_out_2, turns["out2"][0], 1, 0)
                sp.dma_start(p_raw, p_2[0, 0].rearrange("(a p) d -> p a d", p=P)).then_inc(sem("p_loaded"), 16)
                sp.dma_start(post_row, g_post_2.broadcast_to([P, D])).then_inc(sem("post_row_loaded"), 16)
                sp.dma_start(w_pp, w_pp_2[0].rearrange("(k p) n -> p k n", p=P)).then_inc(sem("w_pp_loaded"), 16)
                for j in range(2):
                    load_block(sp, w_out_2, turns["out2"][0] + 1, j, 2 * NB)
                sp.dma_start(ple_row, g_ple_2.broadcast_to([P, D])).then_inc(sem("ple_row_loaded"), 16)
                load_first(sp, w_pg_2, "pg")
                load_rest(sp, w_pg_2, "pg")
                for a in range(TT):
                    sp.wait_ge(sem("out_ready"), a + 1)
                    sp.dma_start(out[0, a * P:a * P + P, :], h[:, a, :]).then_inc(sem("out_stored"), 16)
                sp.wait_ge(sem("out_stored"), 16 * TT)

            @block.gpsimd
            def _(pool):
                subtract_block(pool, turns["out2"][0], 0, (1,))
                subtract_rest(pool, "out2")
                subtract_all(pool, "pg")

            @block.scalar
            def _(act):
                def move_embedding(groups):
                    for j in groups:
                        act.wait_ge(sem("emb_product"), j + 1)
                        nc.scalar.activation(emb[:, j // 4, (j % 4) * 512:(j % 4) * 512 + 512], aux[j % 4], ACT.Copy).then_inc(sem("emb_moved"), 1)

                def read_y(b, product):
                    if b == 0:
                        act.wait_ge(sem("p_transposed"), 1)
                        nc.scalar.activation(pT, aux[0].rearrange("p (k t) -> p k t", k=2), ACT.Copy).then_inc(sem("p_moved"), 1)
                    if b == 2:
                        move_embedding(range(4))
                    return nc.scalar.activation(y[:, :, b * NB:b * NB + NB], product, ACT.Copy)

                def read_gate(b, product):
                    if b == 0:
                        act.wait_ge(sem("h4_ready"), TT)
                    return nc.scalar.activation(y[:, :, b * NB:b * NB + NB], product, ACT.Sigmoid)

                round_block(act, turns["out2"][0], 0, (1,))
                round_and_read(act, "out2", read_y)
                for j in range(2):
                    act.wait_ge(pair_free[j], sum(turns["out2"]))
                squares(act, y, 10)
                roots(act, 10)
                round_block(act, turns["pg"][0], 0, (0, 1))
                move_embedding(range(4, 8))
                round_transposed(act, BEFORE_H4)
                round_and_read(act, "pg", read_gate)
                squares(act, y, 12, "gated", 4)
                roots(act, 12)

            @block.vector
            def _(dve):
                def step(instruction):
                    link(dve, instruction)

                def columns(b):
                    return slice(b * NB, b * NB + NB)

                def times_row(b, row):
                    return nc.vector.tensor_tensor(scaled[:, :, columns(b)], y[:, :, columns(b)],
                                                   row[:, columns(b)].unsqueeze(1).broadcast_to([P, TT, NB]), ALU.mult)

                dve.wait_ge(sem("post_row_loaded"), 16)
                for b in range(4):
                    dve.wait_ge(pair_free[b % 2], turns["out2"][0] + b // 2 + 1)
                    step(times_row(b, post_row))
                reciprocal_rms(dve, y, 10)
                for a in range(TT):
                    nc.vector.scalar_tensor_tensor(h[:, a, :], scaled[:, a, :], rms_col(10, a), h[:, a, :], ALU.mult, ALU.add).then_inc(sem("h4_ready"), 1)
                subtract_transposed(dve, BEFORE_H4)
                dve.wait_ge(sem("ple_row_loaded"), 16)
                dve.wait_ge(sem("emb_moved"), 8)
                for b in range(4):
                    dve.wait_ge(pair_free[b % 2], turns["pg"][0] + b // 2 + 1)
                    nc.vector.tensor_tensor(y[:, :, columns(b)], y[:, :, columns(b)], emb[:, :, columns(b)], ALU.mult).then_inc(sem("gated"), 1)
                    dve.wait_ge(sem("gated"), b + 1)
                    step(times_row(b, ple_row))
                reciprocal_rms(dve, y, 12)
                dve.wait_ge(sem("h4_ready"), TT)
                for a in range(TT):
                    nc.vector.scalar_tensor_tensor(h[:, a, :], scaled[:, a, :], rms_col(12, a), h[:, a, :], ALU.mult, ALU.add).then_inc(sem("out_ready"), 1)

            @block.tensor
            def _(pe):
                first = turns["out2"][0]

                def embed(groups):
                    for j in groups:
                        a, q = j // 4, j % 4
                        if j >= 4:
                            pe.wait_ge(sem("emb_moved"), j - 3)
                        for k in range(2):
                            last = nc.tensor.matmul(aux[q], pT[:, k, a * P:a * P + P], w_pp[:, k, q * 512:q * 512 + 512], start=k == 0, stop=k == 1)
                        last.then_inc(sem("emb_product"), 1)

                multiply_block(pe, first, 0, True)
                pe.wait_ge(sem("p_loaded"), 16)
                for k in range(2):
                    for a in range(TT):
                        last = nc.tensor.transpose(aux[0][:, k * T + a * P:k * T + a * P + P], p_raw[:, a, k * P:k * P + P], ident)
                last.then_inc(sem("p_transposed"), 1)
                multiply_block(pe, first, 1, True)
                pe.wait_ge(sem("w_pp_loaded"), 16)
                pe.wait_ge(sem("p_moved"), 1)
                embed(range(4))
                multiply_turn(pe, first + 1, True)
                pe.wait_ge(sem("squares_done"), 6)
                embed(range(4, 8))
                pe.wait_ge(sem("emb_moved"), 8)
                transpose_tokens(pe, h, "h4_ready", BEFORE_H4)
                pe.wait_ge(sem("tokens_moved"), AFTER_H4)
                multiply(pe, *turns["pg"], True)


_INS = ["x", "mix_norm_g", "w_in", "conv_w", "conv_b", "lru_w_a", "lru_b_a", "lru_w_x", "lru_b_x",
        "lru_lambda", "gmlp_ln_g", "gmlp_ln_b", "gmlp_w_s", "gmlp_b_s", "w_out", "ffn_norm_g",
        "peer_w_q", "peer_sub_keys", "peer_u", "peer_v", "final_norm_g", "p_2", "positions_2",
        "w_in_2", "w_out_2", "g_pre_2", "g_post_2", "g_hg_2", "lb_fwd_2", "lb_bwd_2", "w_pg_2",
        "w_pp_2", "g_ple_2"]


def kernel(**inputs):
    import concourse.bacc as bacc
    from concourse.bass_utils import run_bass_kernel_spmd

    nc = bacc.Bacc("TRN2", target_bir_lowering=False, num_devices=1)
    arrays, args = {}, []
    for name in _INS:
        a = np.ascontiguousarray(inputs[name])
        arrays[f"in_{name}_dram"] = a
        args.append(nc.dram_tensor(f"in_{name}_dram", a.shape, mybir.dt.from_np(a.dtype), kind="ExternalInput").ap())
    arrays["constants_dram"] = shape_constants()
    args.append(nc.dram_tensor("constants_dram", (P, C_END), F32, kind="ExternalInput").ap())
    out = nc.dram_tensor("out_dram", (1, T, D), F32, kind="ExternalOutput").ap()
    build(nc, *args, out)
    r = run_bass_kernel_spmd(nc, [arrays], core_ids=[0])
    return r.results[0]["out_dram"]
```
